# Optimizing a Trainium2 kernel written in Bass

```python
import jax, jax.numpy as jnp
from jax import lax
import numpy as np
import math

D_MODEL = 1024
BATCH = 1
SEQ = 256
DEPTH = 1

D_RNN = D_MODEL
RNN_BLOCKS = 16
RNN_BLOCK_W = D_RNN // RNN_BLOCKS
CONV_W = 4
LRU_C = 8.0
HEAD_DIM = 64
N_Q_HEADS = D_MODEL // HEAD_DIM
N_KV_HEADS = 4
GQA_GROUP = N_Q_HEADS // N_KV_HEADS
WINDOW = 128
ATTN_BLOCK = WINDOW
ROPE_THETA = 10000.0
Q_W = N_Q_HEADS * HEAD_DIM
KV_W = N_KV_HEADS * HEAD_DIM
D_FF = 4 * D_MODEL
PLE_DIM = 256
NORM_EPS = 1e-6
IN_WIDTHS = [D_RNN, D_RNN, Q_W, KV_W, KV_W, D_MODEL, D_MODEL]
IN_TOTAL = int(sum(IN_WIDTHS))
SPLIT_IDX = [int(v) for v in np.cumsum(IN_WIDTHS)[:-1]]


def _rmsnorm(t, g):
    tf = t.astype(jnp.float32)
    y = tf * lax.rsqrt(jnp.mean(tf * tf, axis=-1, keepdims=True) + NORM_EPS)
    return (y * g.astype(jnp.float32)).astype(t.dtype)

def _rope_tables(S):
    inv = ROPE_THETA ** (-jnp.arange(0, HEAD_DIM, 2, dtype=jnp.float32) / HEAD_DIM)
    ang = jnp.arange(S, dtype=jnp.float32)[:, None] * inv[None, :]
    return jnp.cos(ang), jnp.sin(ang)

def _rope(t, cos, sin):
    tf = t.astype(jnp.float32)
    t1, t2 = jnp.split(tf, 2, axis=-1)
    c = cos[None, :, None, :]
    s = sin[None, :, None, :]
    return jnp.concatenate([t1 * c - t2 * s, t2 * c + t1 * s], axis=-1).astype(t.dtype)

def _causal_conv(t, w, b):
    S = t.shape[1]
    tp = jnp.pad(t, ((0, 0), (CONV_W - 1, 0), (0, 0)))
    out = b + tp[:, 0:S] * w[0]
    for j in range(1, CONV_W):
        out = out + tp[:, j:j + S] * w[j]
    return out

def _rg_lru(xc, w_rg, b_rg, w_ig, b_ig, lam):
    B, S, _ = xc.shape
    xb = xc.reshape(B, S, RNN_BLOCKS, RNN_BLOCK_W)
    r = jax.nn.sigmoid(jnp.einsum('bshi,hij->bshj', xb, w_rg).reshape(B, S, D_RNN) + b_rg)
    i = jax.nn.sigmoid(jnp.einsum('bshi,hij->bshj', xb, w_ig).reshape(B, S, D_RNN) + b_ig)
    log_a = -LRU_C * r.astype(jnp.float32) * jax.nn.softplus(-lam.astype(jnp.float32))
    a = jnp.exp(log_a)
    mult = jnp.sqrt(-jnp.expm1(2.0 * log_a))
    bterm = mult * (i * xc).astype(jnp.float32)

    def combine(left, right):
        a1, b1 = left
        a2, b2 = right
        return a1 * a2, a2 * b1 + b2

    _, h = lax.associative_scan(combine, (a, bterm), axis=1)
    return h.astype(xc.dtype)

def _sliding_window_attention(q, k, v, q_gain, k_gain, sinks, cos, sin):
    B, S, _ = q.shape
    NB = S // ATTN_BLOCK
    q = _rope(_rmsnorm(q.reshape(B, S, N_Q_HEADS, HEAD_DIM), q_gain), cos, sin)
    k = _rope(_rmsnorm(k.reshape(B, S, N_KV_HEADS, HEAD_DIM), k_gain), cos, sin)
    v = v.reshape(B, S, N_KV_HEADS, HEAD_DIM)
    qb = q.reshape(B, NB, ATTN_BLOCK, N_KV_HEADS, GQA_GROUP, HEAD_DIM)

    def band(t):
        tb = t.reshape(B, NB, ATTN_BLOCK, N_KV_HEADS, HEAD_DIM)
        prev = jnp.pad(tb[:, :-1], ((0, 0), (1, 0), (0, 0), (0, 0), (0, 0)))
        return jnp.concatenate([prev, tb], axis=2)

    kb = band(k)
    vb = band(v)
    s = jnp.einsum('bnqkgd,bnckd->bnkgqc', qb, kb).astype(jnp.float32) * (HEAD_DIM ** -0.5)
    qi = jnp.arange(ATTN_BLOCK)[:, None]
    ci = jnp.arange(2 * ATTN_BLOCK)[None, :]
    diff = ATTN_BLOCK + qi - ci
    blk = jnp.arange(NB)[:, None, None]
    valid = (diff >= 0) & (diff < WINDOW) & ((blk - 1) * ATTN_BLOCK + ci >= 0)
    s = jnp.where(valid[None, :, None, None, :, :], s, -jnp.inf)
    sink = sinks.astype(jnp.float32).reshape(N_KV_HEADS, GQA_GROUP)[None, None, :, :, None, None]
    m = jnp.maximum(jnp.max(s, axis=-1, keepdims=True), sink)
    e = jnp.exp(s - m)
    probs = e / (jnp.sum(e, axis=-1, keepdims=True) + jnp.exp(sink - m))
    o = jnp.einsum('bnkgqc,bnckd->bnqkgd', probs.astype(v.dtype), vb)
    return o.reshape(B, S, Q_W)

def first_inputs(seed: int = 0) -> dict:
    key = jax.random.key(seed)
    ks = jax.random.split(key, 24)
    f32 = jnp.float32
    L = DEPTH

    def nrm(k, shape, scale):
        return jax.random.normal(k, shape, f32) * scale

    u = jax.random.uniform(ks[10], (L, D_RNN), f32, minval=0.9, maxval=0.999)
    s_a = u ** (1.0 / LRU_C)
    lru_lambda = jnp.log(s_a) - jnp.log1p(-s_a)
    return {
        'x': nrm(ks[0], (BATCH, SEQ, D_MODEL), 1.0),
        'p': nrm(ks[1], (DEPTH, BATCH, SEQ, PLE_DIM), 1.0),
        'g_mix': 1.0 + nrm(ks[2], (L, D_MODEL), 0.02),
        'w_in': nrm(ks[3], (L, D_MODEL, IN_TOTAL), D_MODEL ** -0.5),
        'conv_w': nrm(ks[4], (L, CONV_W, D_RNN), CONV_W ** -0.5),
        'conv_b': nrm(ks[5], (L, D_RNN), 0.01),
        'w_rg': nrm(ks[6], (L, RNN_BLOCKS, RNN_BLOCK_W, RNN_BLOCK_W), RNN_BLOCK_W ** -0.5),
        'b_rg': nrm(ks[7], (L, D_RNN), 0.01),
        'w_ig': nrm(ks[8], (L, RNN_BLOCKS, RNN_BLOCK_W, RNN_BLOCK_W), RNN_BLOCK_W ** -0.5),
        'b_ig': nrm(ks[9], (L, D_RNN), 0.01),
        'lru_lambda': lru_lambda,
        'w_rnn_proj': nrm(ks[11], (L, D_RNN, D_MODEL), D_RNN ** -0.5),
        'q_gain': 1.0 + nrm(ks[12], (L, HEAD_DIM), 0.02),
        'k_gain': 1.0 + nrm(ks[13], (L, HEAD_DIM), 0.02),
        'sinks': nrm(ks[14], (L, N_Q_HEADS), 0.5),
        'w_attn_proj': nrm(ks[15], (L, Q_W, D_MODEL), Q_W ** -0.5),
        'w_out': nrm(ks[16], (L, D_MODEL, D_MODEL), D_MODEL ** -0.5),
        'g_mlp': 1.0 + nrm(ks[17], (L, D_MODEL), 0.02),
        'w_up': nrm(ks[18], (L, D_MODEL, D_FF), D_MODEL ** -0.5),
        'w_down': nrm(ks[19], (L, D_FF, D_MODEL), D_FF ** -0.5),
        'g_ple': 1.0 + nrm(ks[20], (L, D_MODEL), 0.02),
        'w_ple_gate': nrm(ks[21], (L, D_MODEL, D_MODEL), D_MODEL ** -0.5),
        'w_ple_proj': nrm(ks[22], (L, PLE_DIM, D_MODEL), PLE_DIM ** -0.5),
    }

def first_block(x, p, g_mix, w_in, conv_w, conv_b, w_rg, b_rg, w_ig, b_ig, lru_lambda,
              w_rnn_proj, q_gain, k_gain, sinks, w_attn_proj, w_out, g_mlp, w_up, w_down,
              g_ple, w_ple_gate, w_ple_proj):
    S = x.shape[1]
    cos, sin = _rope_tables(S)
    for l in range(DEPTH):
        h = _rmsnorm(x, g_mix[l])
        z = h @ w_in[l]
        x_rnn, g_rnn, q, k, v, gate_a, gate_b = jnp.split(z, SPLIT_IDX, axis=-1)
        xc = _causal_conv(x_rnn, conv_w[l], conv_b[l])
        hr = _rg_lru(xc, w_rg[l], b_rg[l], w_ig[l], b_ig[l], lru_lambda[l])
        y_a = (hr * jax.nn.gelu(g_rnn)) @ w_rnn_proj[l]
        y_b = _sliding_window_attention(q, k, v, q_gain[l], k_gain[l], sinks[l], cos, sin) @ w_attn_proj[l]
        merged = jax.nn.sigmoid(gate_a) * y_a + jax.nn.sigmoid(gate_b) * y_b
        x = x + merged @ w_out[l]
        hm = _rmsnorm(x, g_mlp[l])
        x = x + jnp.square(jax.nn.relu(hm @ w_up[l])) @ w_down[l]
        e = p[l] @ w_ple_proj[l]
        x = x + e * jax.nn.sigmoid(_rmsnorm(x, g_ple[l]) @ w_ple_gate[l])
    return x


CHUNK = 64
Q_BLOCK = 128
MLA_HEADS = 8
Q_LORA = 384
KV_LORA = 256
NOPE_DIM = 64
ROPE_DIM = 32
V_DIM = 64
POOL_WIDTH = 512
POOL_WINDOWS = (2, 4, 8, 16)
N_POOL_GROUPS = len(POOL_WINDOWS)
POOL_GROUP_DIM = POOL_WIDTH // N_POOL_GROUPS
MEM_LEN = 256
MEM_HEADS = 4
MEM_HEAD_DIM = D_MODEL // MEM_HEADS
N_GROUPS = 4
EXPERTS_PER_GROUP = 8
N_EXPERTS = N_GROUPS * EXPERTS_PER_GROUP
EXPERT_FF = 256
TOP_K = 2
EPS = 1e-6
IN_SPLITS = tuple(int(v) for v in np.cumsum([Q_LORA, KV_LORA, ROPE_DIM, POOL_WIDTH, D_MODEL]))
IN_COLS = Q_LORA + KV_LORA + ROPE_DIM + POOL_WIDTH + 2 * D_MODEL


def rms_norm(x, g):
    xf = x.astype(jnp.float32)
    y = xf * lax.rsqrt(jnp.mean(xf * xf, axis=-1, keepdims=True) + EPS)
    return (y * g.astype(jnp.float32)).astype(x.dtype)

def rope_tables(positions):
    inv_freq = 1.0 / (ROPE_THETA ** (jnp.arange(0, ROPE_DIM, 2, dtype=jnp.float32) / ROPE_DIM))
    ang = positions.astype(jnp.float32)[..., None] * inv_freq
    return jnp.cos(ang), jnp.sin(ang)

def apply_rope(x, cos, sin):
    x1, x2 = jnp.split(x.astype(jnp.float32), 2, axis=-1)
    return jnp.concatenate([x1 * cos - x2 * sin, x2 * cos + x1 * sin], axis=-1).astype(x.dtype)

def mla_attention(q_nope, q_rope, k_nope, k_rope, v):
    S = q_nope.shape[1]
    scale = 1.0 / math.sqrt(NOPE_DIM + ROPE_DIM)
    outs = []
    for blk in range(S // Q_BLOCK):
        s0, s1 = blk * Q_BLOCK, (blk + 1) * Q_BLOCK
        sc = (jnp.einsum('bqhd,bkhd->bhqk', q_nope[:, s0:s1], k_nope[:, :s1])
              + jnp.einsum('bqhd,bkd->bhqk', q_rope[:, s0:s1], k_rope[:, :s1]))
        sc = sc.astype(jnp.float32) * scale
        q_chunk = (s0 + jnp.arange(Q_BLOCK)) // CHUNK
        k_chunk = jnp.arange(s1) // CHUNK
        mask = k_chunk[None, :] <= q_chunk[:, None]
        p = jax.nn.softmax(jnp.where(mask, sc, -jnp.inf), axis=-1).astype(v.dtype)
        outs.append(jnp.einsum('bhqk,bkhd->bqhd', p, v[:, :s1]))
    return jnp.concatenate(outs, axis=1)

def multiscale_pool(u, group_w, scale):
    B, S, C = u.shape
    uf = u.astype(jnp.float32)
    cs = jnp.concatenate([jnp.zeros((B, 1, C), jnp.float32), jnp.cumsum(uf, axis=1)], axis=1)
    t = jnp.arange(S)
    outs = []
    for g, w in enumerate(POOL_WINDOWS):
        c0, c1 = g * POOL_GROUP_DIM, (g + 1) * POOL_GROUP_DIM
        csg = cs[:, :, c0:c1]
        lower = jnp.concatenate([jnp.zeros((B, w - 1, POOL_GROUP_DIM), jnp.float32), csg[:, :S - w + 1]], axis=1)
        count = jnp.minimum(t + 1, w).astype(jnp.float32)[None, :, None]
        outs.append((csg[:, 1:] - lower) / count - uf[:, :, c0:c1])
    d = jnp.stack(outs, axis=2).astype(u.dtype)
    y = jnp.einsum('bsgc,gce->bsge', d, group_w).reshape(B, S, C)
    return y * scale

def memory_cross_attention(hn, memn, w_q, w_kv, w_o):
    B, S, _ = hn.shape
    q = (hn @ w_q).reshape(B, S, MEM_HEADS, MEM_HEAD_DIM)
    k, v = jnp.split(memn @ w_kv, 2, axis=-1)
    k = k.reshape(B, MEM_LEN, MEM_HEADS, MEM_HEAD_DIM)
    v = v.reshape(B, MEM_LEN, MEM_HEADS, MEM_HEAD_DIM)
    sc = jnp.einsum('bqhd,bmhd->bhqm', q, k).astype(jnp.float32) / math.sqrt(MEM_HEAD_DIM)
    p = jax.nn.softmax(sc, axis=-1).astype(v.dtype)
    o = jnp.einsum('bhqm,bmhd->bqhd', p, v).reshape(B, S, D_MODEL)
    return o @ w_o

def hierarchical_moe(xn, w_rg, b_rg, w_re, b_re, w_gate, w_up, w_down):
    B, S, _ = xn.shape
    group_prob = jax.nn.softmax((xn @ w_rg).astype(jnp.float32) + b_rg.astype(jnp.float32), axis=-1)
    g_w, g_idx = lax.top_k(group_prob, 1)
    e_logits = ((xn @ w_re).astype(jnp.float32) + b_re.astype(jnp.float32)).reshape(B, S, N_GROUPS, EXPERTS_PER_GROUP)
    sel = jnp.einsum('bsge,bsg->bse', e_logits, jax.nn.one_hot(g_idx[..., 0], N_GROUPS, dtype=jnp.float32))
    e_w, e_idx = lax.top_k(jax.nn.softmax(sel, axis=-1), TOP_K)
    e_w = e_w / jnp.sum(e_w, axis=-1, keepdims=True)
    weights = g_w * e_w
    global_idx = g_idx * EXPERTS_PER_GROUP + e_idx
    cw = jnp.einsum('bsk,bskn->bsn', weights, jax.nn.one_hot(global_idx, N_EXPERTS, dtype=jnp.float32)).astype(xn.dtype)
    out = jnp.zeros_like(xn)
    for e in range(N_EXPERTS):
        hid = jax.nn.silu(xn @ w_gate[e]) * (xn @ w_up[e])
        out = out + (hid * cw[..., e:e + 1]) @ w_down[e]
    return out

def second_inputs(seed: int = 0) -> dict:
    key = jax.random.key(seed)
    ks = iter(jax.random.split(key, 40))
    f32 = jnp.float32

    def w(shape, fan_in):
        return jax.random.normal(next(ks), shape, f32) * (fan_in ** -0.5)

    def gain(shape):
        return 1.0 + 0.02 * jax.random.normal(next(ks), shape, f32)

    def bias(shape):
        return 0.01 * jax.random.normal(next(ks), shape, f32)

    L = DEPTH
    x = jax.random.normal(next(ks), (BATCH, SEQ, D_MODEL), f32)
    mem = jax.random.normal(next(ks), (BATCH, MEM_LEN, D_MODEL), f32)
    offsets = jax.random.randint(next(ks), (BATCH, 1), 0, 4096, dtype=jnp.int32)
    positions = (offsets + jnp.arange(SEQ, dtype=jnp.int32)[None, :]).astype(jnp.int32)
    return {
        "x": x,
        "mem": mem,
        "positions": positions,
        "mix_norm_g": gain((L, D_MODEL)),
        "w_in": w((L, D_MODEL, IN_COLS), D_MODEL),
        "q_norm_g": gain((L, Q_LORA)),
        "w_q_up": w((L, Q_LORA, MLA_HEADS * (NOPE_DIM + ROPE_DIM)), Q_LORA),
        "kv_norm_g": gain((L, KV_LORA)),
        "w_kv_up": w((L, KV_LORA, MLA_HEADS * (NOPE_DIM + V_DIM)), KV_LORA),
        "w_attn_branch": w((L, MLA_HEADS * V_DIM, D_MODEL), MLA_HEADS * V_DIM),
        "pool_w": w((L, N_POOL_GROUPS, POOL_GROUP_DIM, POOL_GROUP_DIM), POOL_GROUP_DIM),
        "pool_scale": 1.0 + 0.1 * jax.random.normal(next(ks), (L, POOL_WIDTH), f32),
        "w_pool_branch": w((L, POOL_WIDTH, D_MODEL), POOL_WIDTH),
        "w_mix_out": w((L, D_MODEL, D_MODEL), D_MODEL),
        "xattn_norm_g": gain((L, D_MODEL)),
        "mem_norm_g": gain((L, D_MODEL)),
        "w_xq": w((L, D_MODEL, D_MODEL), D_MODEL),
        "w_xkv": w((L, D_MODEL, 2 * D_MODEL), D_MODEL),
        "w_xo": w((L, D_MODEL, D_MODEL), D_MODEL),
        "ffn_norm_g": gain((L, D_MODEL)),
        "w_router_group": w((L, D_MODEL, N_GROUPS), D_MODEL),
        "b_router_group": bias((L, N_GROUPS)),
        "w_router_expert": w((L, D_MODEL, N_EXPERTS), D_MODEL),
        "b_router_expert": bias((L, N_EXPERTS)),
        "w_exp_gate": w((L, N_EXPERTS, D_MODEL, EXPERT_FF), D_MODEL),
        "w_exp_up": w((L, N_EXPERTS, D_MODEL, EXPERT_FF), D_MODEL),
        "w_exp_down": w((L, N_EXPERTS, EXPERT_FF, D_MODEL), EXPERT_FF),
        "final_norm_g": gain((D_MODEL,)),
    }

def second_block(x, mem, positions, mix_norm_g, w_in, q_norm_g, w_q_up, kv_norm_g, w_kv_up,
              w_attn_branch, pool_w, pool_scale, w_pool_branch, w_mix_out,
              xattn_norm_g, mem_norm_g, w_xq, w_xkv, w_xo,
              ffn_norm_g, w_router_group, b_router_group, w_router_expert, b_router_expert,
              w_exp_gate, w_exp_up, w_exp_down, final_norm_g):
    B, S, _ = x.shape
    cos, sin = rope_tables(positions)
    h = x
    for l in range(DEPTH):
        hn = rms_norm(h, mix_norm_g[l])
        z = hn @ w_in[l]
        q_lat, kv_lat, k_rope, u_pool, gate_a, gate_b = jnp.split(z, IN_SPLITS, axis=-1)
        q = (rms_norm(q_lat, q_norm_g[l]) @ w_q_up[l]).reshape(B, S, MLA_HEADS, NOPE_DIM + ROPE_DIM)
        q_nope, q_rope = q[..., :NOPE_DIM], q[..., NOPE_DIM:]
        q_rope = apply_rope(q_rope, cos[:, :, None, :], sin[:, :, None, :])
        kv = (rms_norm(kv_lat, kv_norm_g[l]) @ w_kv_up[l]).reshape(B, S, MLA_HEADS, NOPE_DIM + V_DIM)
        k_nope, v = kv[..., :NOPE_DIM], kv[..., NOPE_DIM:]
        k_rope = apply_rope(k_rope, cos, sin)
        attn = mla_attention(q_nope, q_rope, k_nope, k_rope, v).reshape(B, S, MLA_HEADS * V_DIM)
        y_a = attn @ w_attn_branch[l]
        y_b = multiscale_pool(u_pool, pool_w[l], pool_scale[l]) @ w_pool_branch[l]
        g_a = jax.nn.sigmoid(gate_a.astype(jnp.float32)).astype(h.dtype)
        g_b = jax.nn.sigmoid(gate_b.astype(jnp.float32)).astype(h.dtype)
        h = h + (g_a * y_a + g_b * y_b) @ w_mix_out[l]
        h = h + memory_cross_attention(rms_norm(h, xattn_norm_g[l]), rms_norm(mem, mem_norm_g[l]),
                                       w_xq[l], w_xkv[l], w_xo[l])
        h = h + hierarchical_moe(rms_norm(h, ffn_norm_g[l]), w_router_group[l], b_router_group[l],
                                 w_router_expert[l], b_router_expert[l],
                                 w_exp_gate[l], w_exp_up[l], w_exp_down[l])
    return rms_norm(h, final_norm_g)


def setup_inputs(seed=0):
    out = dict(first_inputs(seed))
    for name, value in second_inputs(seed + 1).items():
        if name != "x":
            out[name + "_2"] = value
    return out


def reference(
    x, p, g_mix, w_in, conv_w, conv_b, w_rg, b_rg, w_ig, b_ig, lru_lambda, w_rnn_proj, q_gain,
    k_gain, sinks, w_attn_proj, w_out, g_mlp, w_up, w_down, g_ple, w_ple_gate, w_ple_proj,
    mem_2, positions_2, mix_norm_g_2, w_in_2, q_norm_g_2, w_q_up_2, kv_norm_g_2, w_kv_up_2,
    w_attn_branch_2, pool_w_2, pool_scale_2, w_pool_branch_2, w_mix_out_2, xattn_norm_g_2,
    mem_norm_g_2, w_xq_2, w_xkv_2, w_xo_2, ffn_norm_g_2, w_router_group_2, b_router_group_2,
    w_router_expert_2, b_router_expert_2, w_exp_gate_2, w_exp_up_2, w_exp_down_2,
    final_norm_g_2,
):
    x = first_block(
        x, p, g_mix, w_in, conv_w, conv_b, w_rg, b_rg, w_ig, b_ig, lru_lambda, w_rnn_proj,
        q_gain, k_gain, sinks, w_attn_proj, w_out, g_mlp, w_up, w_down, g_ple, w_ple_gate,
        w_ple_proj,
    )
    return second_block(
        x, mem_2, positions_2, mix_norm_g_2, w_in_2, q_norm_g_2, w_q_up_2, kv_norm_g_2,
        w_kv_up_2, w_attn_branch_2, pool_w_2, pool_scale_2, w_pool_branch_2, w_mix_out_2,
        xattn_norm_g_2, mem_norm_g_2, w_xq_2, w_xkv_2, w_xo_2, ffn_norm_g_2, w_router_group_2,
        b_router_group_2, w_router_expert_2, b_router_expert_2, w_exp_gate_2, w_exp_up_2,
        w_exp_down_2, final_norm_g_2,
    )


_drawn_inputs = setup_inputs


def setup_inputs(seed=0):
    import zlib

    import numpy as np

    out = dict(_drawn_inputs(seed))
    spreads = {}
    factors = {'g_mix': 4.034,
     'conv_b': 2.882,
     'b_rg': 8.0,
     'b_ig': 8.0,
     'q_gain': 5.504,
     'k_gain': 8.0,
     'sinks': 4.079,
     'g_ple': 8.0,
     'mix_norm_g_2': 6.359,
     'q_norm_g_2': 8.0,
     'kv_norm_g_2': 8.0,
     'xattn_norm_g_2': 8.0,
     'mem_norm_g_2': 8.0,
     'ffn_norm_g_2': 2.837,
     'b_router_group_2': 34.766,
     'b_router_expert_2': 12.628,
     'final_norm_g_2': 7.957}
    for name, (base, spread) in spreads.items():
        noise = np.random.default_rng([zlib.crc32(name.encode()), seed]).standard_normal(out[name].shape)
        drawn = base * np.exp(spread * noise) if base else spread * noise
        out[name] = __import__('jax').numpy.asarray(drawn.astype(out[name].dtype))
    for name, factor in factors.items():
        out[name] = (out[name] * factor).astype(out[name].dtype)
    return out
```

```python
from contextlib import ExitStack

import numpy as np

import concourse.bass as bass
from concourse import mybir

ALU = mybir.AluOpType
ACT = mybir.ActivationFunctionType
AXX = mybir.AxisListType.X
F = mybir.dt.float32
R = mybir.dt.float32r
I32 = mybir.dt.int32

S = 256
D = 1024
NRAW = 4
NW = 3
SLOT = 2048
EPS = 1e-6
NEG = -1e30
TWO_PI = 6.283185307179586
NE = 32

ROWS1 = [("g_mix", 8), ("conv_w", 32), ("conv_b", 8), ("b_rg", 8), ("b_ig", 8), ("lru_lambda", 8),
         ("g_mlp", 8), ("g_ple", 8), ("mix_norm_g_2", 8), ("xattn_norm_g_2", 8), ("mem_norm_g_2", 8),
         ("ffn_norm_g_2", 8)]
ROWS2 = [("q_norm_g_2", 3), ("kv_norm_g_2", 2), ("pool_scale_2", 4)]
CONSTS = [("ident", 128), ("mask1", 384), ("mask2", 384), ("rope", 128), ("inv", 16), ("order", 12),
          ("count", 64), ("half", 2)]


def offsets(rows):
    out, at = {}, 0
    for name, n in rows:
        out[name] = at
        at += n
    return out, at


def constants():
    at, n = offsets(CONSTS)
    c = np.zeros((128, n), np.float32)
    c[:, at["ident"]:at["ident"] + 128] = np.eye(128, dtype=np.float32)
    q = np.arange(128)[:, None]
    k = np.arange(128)[None, :]
    m = at["mask1"]
    c[:, m:m + 128] = np.where(k <= q, 0.0, NEG)
    c[:, m + 128:m + 256] = np.where(k > q, 0.0, NEG)
    c[:, m + 256:m + 384] = np.where(k <= q, 0.0, NEG)
    m = at["mask2"]
    c[:, m:m + 128] = np.where(k // 64 <= q // 64, 0.0, NEG)
    c[:, m + 256:m + 384] = np.where(k // 64 <= q // 64, 0.0, NEG)
    inv = (np.float32(10000.0) ** (-np.arange(0, 64, 2, dtype=np.float32) / np.float32(64))).astype(np.float32)
    ang = (np.arange(S, dtype=np.float32)[:, None] * inv[None, :]).astype(np.float32)
    m = at["rope"]
    for t in range(2):
        c[:, m + 32 * t:m + 32 * t + 32] = np.cos(ang[128 * t:128 * t + 128])
        c[:, m + 64 + 32 * t:m + 96 + 32 * t] = np.sin(ang[128 * t:128 * t + 128])
    c[:, at["inv"]:at["inv"] + 16] = (
        np.float32(1.0) / (np.float32(10000.0) ** (np.arange(0, 32, 2, dtype=np.float32) / np.float32(32))))
    c[:, at["order"]:at["order"] + 4] = 4 - np.arange(4)
    c[:, at["order"] + 4:at["order"] + 12] = 8 - np.arange(8)
    for g, w in enumerate((2, 4, 8, 16)):
        c[:, at["count"] + 16 * g:at["count"] + 16 * g + 16] = 1.0 / np.minimum(np.arange(16) + 1, w)
    c[:, at["half"]] = -0.5
    c[:, at["half"] + 1] = 0.5
    return c


def plan_units():
    u = []

    def mat(name, lead, k, cols, key=None):
        nk = k // 128
        for b, (c0, w) in enumerate(cols):
            for r in range(0, nk, 4):
                u.append(((key or name, b, r // 4), [(name, lead, r * 128, min(4, nk - r), c0, w, 0)]))

    mat("w_in", (0,), 1024, [(512 * b, 512) for b in (0, 1)], "x")
    mat("w_in", (0,), 1024, [(2048, 512), (2560, 512), (3072, 512)], "qkv")
    mat("w_in", (0,), 1024, [(1024, 512), (1536, 512)], "g")
    mat("w_in", (0,), 1024, [(3584 + 512 * b, 512) for b in range(4)], "gates")
    mat("w_rnn_proj", (0,), 1024, [(0, 512), (512, 512)])
    mat("w_attn_proj", (0,), 1024, [(0, 512), (512, 512)])
    mat("w_out", (0,), 1024, [(0, 512), (512, 512)])
    for b in range(9):
        if b < 8:
            for r in range(2):
                u.append((("w_up", b, r), [("w_up", (0,), 512 * r, 4, 512 * b, 512, 0)]))
        if b > 0:
            for r in range(2):
                u.append((("w_down", b - 1, r), [("w_down", (0,), 512 * (b - 1) + 256 * r, 2, 0, 1024, 0)]))
    mat("w_ple_proj", (0,), 256, [(0, 512), (512, 512)])
    mat("w_ple_gate", (0,), 1024, [(0, 512), (512, 512)])
    mat("w_xkv_2", (0,), 1024, [(512 * b, 512) for b in range(4)])
    mat("w_in_2", (0,), 1024, [(0, 384), (384, 288), (672, 512)], "lat")
    mat("w_in_2", (0,), 1024, [(1184 + 512 * b, 512) for b in range(4)], "gates2")
    mat("w_q_up_2", (0,), 384, [(0, 384), (384, 384)])
    mat("w_kv_up_2", (0,), 256, [(0, 512), (512, 512)])
    mat("w_pool_branch_2", (0,), 512, [(0, 512), (512, 512)])
    mat("w_attn_branch_2", (0,), 512, [(0, 512), (512, 512)])
    mat("w_mix_out_2", (0,), 1024, [(0, 512), (512, 512)])
    mat("w_xq_2", (0,), 1024, [(0, 512), (512, 512)])
    mat("w_xo_2", (0,), 1024, [(0, 512), (512, 512)])
    u.append((("router", 0, 0), [("w_router_group_2", (0,), 0, 8, 0, 4, 0), ("w_router_expert_2", (0,), 0, 8, 0, 32, 4)]))
    for e in range(NE + 1):
        if e < NE:
            for r in range(2):
                u.append((("moe_in", e, r), [("w_exp_gate_2", (0, e), 512 * r, 4, 0, 256, 0),
                                             ("w_exp_up_2", (0, e), 512 * r, 4, 0, 256, 256)]))
        if e > 0:
            u.append((("moe_out", e - 1, 0), [("w_exp_down_2", (0, e - 1), 0, 2, 0, 1024, 0)]))
    return u


def tokens(after):
    for t in after:
        if isinstance(t, list):
            yield from tokens(t)
        elif t is not None:
            yield t


class Engines:

    def __init__(self, engines, sems):
        self.engines = engines
        self.sems = sems
        self.count = {k: 0 for k in sems}
        self.seen = {k: {} for k in engines}

    def wait(self, eng, after):
        need = {}
        for name, value in tokens(after):
            need[name] = max(need.get(name, 0), value)
        for name, value in need.items():
            if self.seen[eng].get(name, 0) < value:
                self.seen[eng][name] = value
                self.engines[eng].wait_ge(self.sems[name], value)

    def do(self, eng, fn, *after, silent=False):
        self.wait(eng, after)
        ins = fn(self.engines[eng])
        if silent:
            return None
        self.count[eng] += 1
        ins.then_inc(self.sems[eng], 1)
        return (eng, self.count[eng])

    def dma(self, eng, sem, fn, *after):
        self.wait(eng, after)
        self.count[sem] += 16
        fn(self.engines[eng]).then_inc(self.sems[sem], 16)
        return (sem, self.count[sem])


def build(nc, A, out, dumps=None, until=None):
    with ExitStack() as ctx:
        dma_sems = ([f"w{i}" for i in range(NRAW)] +
                    ["x", "rows", "const", "bd", "bcast", "mem", "pos", "pool_w", "p", "fing", "out"])
        sems = {k: ctx.enter_context(nc.semaphore(f"s_{k}")) for k in ["pe", "act", "dve", "pool"] + dma_sems}
        Q = Engines({"pe": nc.tensor, "act": nc.scalar, "dve": nc.vector, "pool": nc.gpsimd, "sp": nc.sync}, sems)
        do = Q.do

        def sb(name, n, dt=F):
            return ctx.enter_context(nc.sbuf_tensor(name, [128, n], dt))

        RAW = [sb(f"raw{i}", SLOT) for i in range(NRAW)]
        WH = [sb(f"wh{i}", SLOT, R) for i in range(NW)]
        WL = [sb(f"wl{i}", SLOT, R) for i in range(NW)]
        TH = [sb(f"th{i}", 2048, R) for i in range(2)]
        TL = [sb(f"tl{i}", 2048, R) for i in range(2)]
        X = sb("X", 2048)
        RA = sb("RA", 2080)
        RB = sb("RB", 2048)
        RC = sb("RC", 2048)
        RD = sb("RD", 1024)
        GA = sb("GA", 2048)
        GB = sb("GB", 2048)
        S0 = sb("S0", 2048)
        S1 = sb("S1", 2048)
        KT = sb("KT", 1024)
        KW = sb("KW", 512)
        BD = sb("BD", 1024)
        TMP = sb("TMP", 1280)
        PC = sb("PC", 129)
        CAT, CN = offsets(CONSTS)
        CT = sb("CT", CN)
        NR = sb("NR", 96)
        SM = sb("SM", 704)
        PB = [ctx.enter_context(nc.psum_tensor(f"pb{i}", [128, 512], F)) for i in range(8)]

        def v3(t, a, n, off=0):
            return t[:, off:off + a * n].rearrange("p (a n) -> p a n", a=a)

        def cst(name, n=None, off=0):
            o = CAT[name] + off
            return CT[:, o:o + n]

        ident = cst("ident", 128)
        R1, _ = offsets(ROWS1)
        R2, _ = offsets(ROWS2)
        PCOL = {**R1, **{k: v + 120 for k, v in R2.items()}}

        def col(name, c):
            o = PCOL[name] + c
            return PC[:, o:o + 1]

        small_at = [0]

        def small(n):
            o = small_at[0]
            small_at[0] += n
            assert small_at[0] <= 704, small_at
            return SM[:, o:o + n]

        free = {b: [] for b in range(8)}

        units = plan_units()
        index = {key: i for i, (key, _) in enumerate(units)}
        st = {"loaded": 0, "split": 0, "used": 0}
        raw_ready, split_done, used_done = {}, {}, {}

        def shape_of(i):
            _, parts = units[i]
            kc = parts[0][3]
            return kc, sum(p[5] for p in parts)

        def load(i):
            _, parts = units[i]
            kc, w = shape_of(i)
            dst = v3(RAW[i % NRAW], kc, w)
            after = split_done.get(i - NRAW, [])
            for (name, lead, r0, n, c0, cw, at) in parts:
                src = A[name]
                for j in lead:
                    src = src[j]
                src = src[r0:r0 + n * 128, c0:c0 + cw].rearrange("(k p) n -> p k n", p=128)
                tok = Q.dma("sp", f"w{i % NRAW}", lambda e, d=dst[:, :, at:at + cw], s=src: e.dma_start(d, s), after)
            raw_ready[i] = tok

        def split(i):
            kc, w = shape_of(i)
            n = kc * w
            raw, hi, lo = RAW[i % NRAW][:, 0:n], WH[i % NW][:, 0:n], WL[i % NW][:, 0:n]
            a = do("act", lambda e: e.activation(hi, raw, ACT.Copy), raw_ready[i], used_done.get(i - NW))
            b = do("dve", lambda e: e.tensor_tensor(lo, raw, hi.bitcast(F), ALU.subtract), raw_ready[i], a,
                   used_done.get(i - NW))
            split_done[i] = [a, b]

        def load_to(n):
            while st["loaded"] < min(n, len(units)):
                load(st["loaded"])
                st["loaded"] += 1

        def split_to(n):
            while st["split"] < min(n, len(units)):
                i = st["split"]
                load_to(i + 1)
                split(i)
                st["split"] += 1
                load_to(i + 1 + NRAW)

        def take(key):
            i = index[key]
            assert i == st["used"], (key, i, st)
            split_to(i + NW)
            kc, w = shape_of(i)
            return v3(WH[i % NW], kc, w), v3(WL[i % NW], kc, w), split_done[i]

        def give(key, tok):
            used_done[index[key]] = tok
            st["used"] += 1

        def mm3(o, lh, ll, rh, rl, start, stop, after, last):
            do("pe", lambda e: e.matmul(o, lh, rh, start=start, stop=False, skip_group_check=True), *after,
               silent=True)
            do("pe", lambda e: e.matmul(o, lh, rl, start=False, stop=False, skip_group_check=True), silent=True)
            return do("pe", lambda e: e.matmul(o, ll, rh, start=False, stop=stop, skip_group_check=True),
                      silent=not last)

        bg = []

        def step(n=1):
            for _ in range(n):
                if bg:
                    bg.pop(0)()

        def flush():
            while bg:
                bg.pop(0)()

        turn = [0]

        def pair():
            turn[0] ^= 1
            return (4, 5) if turn[0] else (6, 7)

        def tokens_by(key, nu, th, tl, k0, ready, w, steps=1):
            banks = pair()
            for r in range(nu):
                hi, lo, rdy = take((*key, r))
                kc = shape_of(index[(*key, r)])[0]
                for t in range(2):
                    o = PB[banks[t]][:, 0:w]
                    for k in range(kc):
                        kk = k0 + 4 * r + k
                        c = slice(kk * 256 + t * 128, kk * 256 + t * 128 + 128)
                        tok = mm3(o, th[:, c], tl[:, c], hi[:, k, 0:w], lo[:, k, 0:w], r == 0 and k == 0,
                                  r == nu - 1 and k == kc - 1, (rdy, ready, free[banks[t]]), k == kc - 1)
                give((*key, r), tok)
                step(steps)
            return banks, tok

        def features_by(key, nu, th, tl, ready, steps=1):
            banks = pair()
            for r in range(nu):
                hi, lo, rdy = take((*key, r))
                kc = shape_of(index[(*key, r)])[0]
                for c in range(4):
                    b = banks[c // 2]
                    o = PB[b][:, (c % 2) * 256:(c % 2) * 256 + 256]
                    for k in range(kc):
                        kk = 4 * r + k
                        x = slice(kk * 256, kk * 256 + 256)
                        cs = slice(c * 128, c * 128 + 128)
                        tok = mm3(o, hi[:, k, cs], lo[:, k, cs], th[:, x], tl[:, x], r == 0 and k == 0 and c % 2 == 0,
                                  r == nu - 1 and k == kc - 1, (rdy, ready, free[b]), k == kc - 1)
                give((*key, r), tok)
                step(steps)
            return banks, tok

        def split_t(src, which, c0, n, after, reuse=None):
            hi = TH[which][:, c0 * 256:(c0 + n) * 256]
            lo = TL[which][:, c0 * 256:(c0 + n) * 256]
            a = do("act", lambda e: e.activation(hi, src, ACT.Copy), after, reuse)
            b = do("dve", lambda e: e.tensor_tensor(lo, src, hi.bitcast(F), ALU.subtract), after, a, reuse)
            return [a, b]

        def turn_over(src, nc_, gain, which, ready, reuse, scale=1.0, dst=None, d0=0, banks=(0, 1, 2, 3), f32=None):
            toks = []
            fb = S1 if f32 is None else f32
            for j in range((nc_ + 1) // 2):
                b = banks[j % len(banks)]
                n = min(2, nc_ - 2 * j)
                for c in range(n):
                    for t in range(2):
                        o = PB[b][:, c * 256 + t * 128:c * 256 + t * 128 + 128]
                        s = src[:, t, (2 * j + c) * 128:(2 * j + c) * 128 + 128]
                        tok = do("pe", lambda e, o=o, s=s: e.transpose(o, s, ident), ready, free[b], c_tok)
                eng = "dve" if j % 2 else "act"
                for c in range(n):
                    o = fb[:, (2 * j + c) * 256:(2 * j + c) * 256 + 256]
                    i = PB[b][:, c * 256:c * 256 + 256]
                    g = col(gain, 2 * j + c) if gain else scale
                    if eng == "act":
                        ev = do("act", lambda e, o=o, i=i, g=g: e.activation(o, i, ACT.Copy, scale=g), tok, pc_tok, reuse)
                    else:
                        ev = do("dve", lambda e, o=o, i=i, g=g: e.tensor_scalar(o, i, g, None, ALU.mult), tok, pc_tok, reuse)
                free[b] = [ev]
                if which is not None:
                    toks += split_t(fb[:, 2 * j * 256:(2 * j + n) * 256], which, 2 * j, n, ev, reuse)
                else:
                    toks.append(ev)
            return toks

        def rsqrt_mean(dst, ss, n, after):
            w = dst.shape[-1]
            v, y, t = NR[:, 0:w], NR[:, 32:32 + w], NR[:, 64:64 + w]
            d = do("dve", lambda e: e.tensor_scalar(v, ss, 1.0 / n, EPS, ALU.mult, ALU.add), *after)
            d = do("dve", lambda e: e.tensor_scalar(t.bitcast(I32), v.bitcast(I32), 1, None, ALU.logical_shift_right), d)
            d = do("dve", lambda e: e.tensor_scalar(y.bitcast(I32), t.bitcast(I32), -1.0, float(0x5f3759df), ALU.mult, ALU.add), d)
            for i in range(3):
                o = dst if i == 2 else y
                d = do("dve", lambda e: e.tensor_tensor(t, y, y, ALU.mult), d)
                d = do("dve", lambda e: e.scalar_tensor_tensor(t, t, -0.5, v, ALU.mult, ALU.mult), d)
                d = do("dve", lambda e: e.scalar_tensor_tensor(o, t, 1.5, y, ALU.add, ALU.mult), d)
            return d

        def norm(src, w, gain, which, ready, reuse, s0_free=None, out_scratch=None):
            xs = v3(S0 if out_scratch is None else out_scratch, 2, w)
            ss = small(2)
            rs = small(2)
            for t in range(2):
                a = do("act", lambda e, t=t: e.activation(xs[:, t, :], src[:, t, :], ACT.Square, accum_out=ss[:, t:t + 1]),
                       ready, s0_free)
            r = rsqrt_mean(rs, ss, w, (a,))
            for t in range(2):
                b = do("dve", lambda e, t=t: e.tensor_scalar(xs[:, t, :], src[:, t, :], rs[:, t:t + 1], None, ALU.mult), r, a)
            return turn_over(xs, w // 128, gain, which, b, reuse)

        x_tok = Q.dma("sp", "x", lambda e: e.dma_start(v3(X, 2, D), A["x"][0].rearrange("(t p) d -> p t d", p=128)))
        const_tok = Q.dma("act", "const", lambda e: e.dma_start(CT[:, :], A["const"]))
        load_to(1)
        at = 0
        for name, n in ROWS1:
            src = A[name].rearrange("o (c p) -> (o c) p", p=128) if name != "conv_w" else \
                A[name][0].rearrange("j (c p) -> (j c) p", p=128)
            rows_tok = Q.dma("act", "rows", lambda e, s=src, at=at, n=n: e.dma_start(S0[at:at + n, 0:128], s))
            at += n
        at = 0
        for name, n in ROWS2:
            src = A[name].rearrange("o (c p) -> (o c) p", p=128)
            rows_tok = Q.dma("act", "rows", lambda e, s=src, at=at, n=n: e.dma_start(S0[at:at + n, 128:256], s))
            at += n
        BDv = [v3(BD, 8, 64, 512 * j) for j in range(2)]
        for j, name in enumerate(("w_rg", "w_ig")):
            w = A[name][0].rearrange("(c h) i j -> h i c j", h=2)
            for h in range(2):
                bd_tok = Q.dma("act", "bd", lambda e, j=j, h=h, w=w: e.dma_start(BDv[j][64 * h:64 * h + 64, :, :], w[h]))
        gq = small(64)
        gk = small(64)
        snk = small(16)
        rb = small(36)
        for dst, src in ((gq, A["q_gain"][0]), (gk, A["k_gain"][0]), (snk, A["sinks"][0]),
                         (rb[:, 0:4], A["b_router_group_2"][0]), (rb[:, 4:36], A["b_router_expert_2"][0])):
            bc_tok = Q.dma("act", "bcast", lambda e, d=dst, s=src: e.dma_start(d, s.partition_broadcast(128)))
        c_tok = const_tok
        pe1 = do("pe", lambda e: e.transpose(PB[0][:, 0:120], S0[0:120, 0:128], ident[0:120, 0:120]), rows_tok, c_tok)
        pe2 = do("pe", lambda e: e.transpose(PB[0][:, 128:137], S0[0:9, 128:256], ident[0:9, 0:9]), pe1)
        a = do("act", lambda e: e.activation(PC[:, 0:120], PB[0][:, 0:120], ACT.Copy), pe2)
        pc_tok = do("act", lambda e: e.activation(PC[:, 120:129], PB[0][:, 128:137], ACT.Copy), pe2)
        free[0] = [pc_tok]

        lam = PC[:, PCOL["lru_lambda"]:PCOL["lru_lambda"] + 8]
        hb = small(16)
        sp4 = small(8)
        sp4n = small(8)
        l0, l1, l2, l3 = small(8), small(8), small(8), small(8)
        d = do("dve", lambda e: e.tensor_scalar(l0, lam, -1.0, None, ALU.mult), pc_tok)
        d = do("dve", lambda e: e.tensor_tensor(l0, l0, lam, ALU.max), d)
        a = do("act", lambda e: e.activation(l1, l0, ACT.Exp, scale=-1.0), d)
        d = do("dve", lambda e: e.tensor_scalar(l2, l1, 2.0, None, ALU.add), a)
        d = do("dve", lambda e: e.reciprocal(l2, l2), d)
        d = do("dve", lambda e: e.tensor_tensor(l1, l1, l2, ALU.mult), d)
        d = do("dve", lambda e: e.tensor_tensor(l2, l1, l1, ALU.mult), d)
        d = do("dve", lambda e: e.tensor_scalar(l3, l2, 1.0 / 15, None, ALU.mult), d)
        for n in (13, 11, 9, 7, 5, 3):
            d = do("dve", lambda e, n=n: e.scalar_tensor_tensor(l3, l3, 1.0 / n, l2, ALU.add, ALU.mult), d)
        d = do("dve", lambda e: e.scalar_tensor_tensor(l3, l3, 1.0, l1, ALU.add, ALU.mult), d)
        d = do("dve", lambda e: e.tensor_scalar(l0, lam, -1.0, 0.0, ALU.mult, ALU.max), d)
        d = do("dve", lambda e: e.scalar_tensor_tensor(l3, l3, 2.0, l0, ALU.mult, ALU.add), d)
        d = do("dve", lambda e: e.tensor_scalar(sp4, l3, 4.0, None, ALU.mult), d)
        d = do("dve", lambda e: e.tensor_scalar(sp4n, l3, -4.0, None, ALU.mult), d)
        sp_tok = do("dve", lambda e: e.tensor_scalar(hb, PC[:, PCOL["b_rg"]:PCOL["b_rg"] + 16], 0.5, None, ALU.mult), d)

        h_tok = norm(v3(X, 2, D), D, "g_mix", 0, x_tok, None, s0_free=[pe2])
        XR = v3(RA, 8, 260)
        z = do("pool", lambda e: e.memset(XR[:, :, 0:3], 0.0))
        xr_tok = []
        for b in range(2):
            banks, tok = features_by(("x", b), 2, TH[0], TL[0], h_tok)
            for h in range(2):
                o = XR[:, 4 * b + 2 * h:4 * b + 2 * h + 2, 3:259]
                xr_tok = [do("act", lambda e, o=o, i=v3(PB[banks[h]], 2, 256): e.activation(o, i, ACT.Copy), tok)]
                free[banks[h]] = xr_tok

        rnn = {}
        XC = [TMP[:, 0:256], TMP[:, 256:512]]
        T1, T2, T3 = TMP[:, 512:768], TMP[:, 768:1024], TMP[:, 1024:1280]

        def rnn_conv(c):
            x = XR[:, c, :]
            xc = XC[c % 2]
            d = do("dve", lambda e: e.tensor_scalar(xc, x[:, 0:256], col("conv_w", c), col("conv_b", c), ALU.mult, ALU.add),
                   xr_tok, z, pc_tok, rnn.get(("mm", c - 2)))
            for j in range(1, 4):
                d = do("dve", lambda e, j=j: e.scalar_tensor_tensor(xc, x[:, j:j + 256], col("conv_w", 8 * j + c), xc,
                                                                    ALU.mult, ALU.add), d)
            rnn["xc", c] = d

        def rnn_gates(c):
            b = c % 2
            xc = XC[c % 2]
            for j in range(2):
                for h in range(2):
                    ps = slice(64 * h, 64 * h + 64)
                    m = do("pe", lambda e: e.matmul(PB[b][ps, 256 * j:256 * j + 256], BDv[j][ps, c, :], xc[ps, :],
                                                    start=True, stop=True, skip_group_check=True),
                           rnn["xc", c], bd_tok, free[b])
            rnn["mm", c] = m
            am, mm, u = S1[:, 256 * c:256 * c + 256], S0[:, 256 * c:256 * c + 256], XR[:, c, 0:256]
            a = do("act", lambda e: e.activation(T1, PB[b][:, 0:256], ACT.Tanh, bias=hb[:, c:c + 1], scale=0.5), m, sp_tok,
                   rnn.get(("m", c - 1)))
            a2 = do("act", lambda e: e.activation(T2, PB[b][:, 256:512], ACT.Tanh, bias=hb[:, 8 + c:9 + c], scale=0.5), m,
                    rnn.get(("u", c - 1)))
            free[b] = [a2]
            a3 = do("act", lambda e: e.activation(am, T1, ACT.Exp, bias=sp4n[:, c:c + 1], scale=sp4n[:, c:c + 1]), a, h_tok)
            a4 = do("act", lambda e: e.activation(T1, T1, ACT.Tanh, bias=sp4[:, c:c + 1], scale=sp4[:, c:c + 1]), a, a3)
            rnn["u", c] = do("dve", lambda e: e.scalar_tensor_tensor(u, T2, 1.0, xc, ALU.add, ALU.mult), a2, rnn["xc", c], m)
            q = do("pool", lambda e: e.tensor_tensor(mm, am, am, ALU.mult), a3, h_tok)
            m1 = do("dve", lambda e: e.scalar_tensor_tensor(mm, mm, 1.0, T1, ALU.add, ALU.mult), q, a4)
            rnn["m", c] = do("dve", lambda e: e.tensor_scalar(mm, mm, 2.0 ** -100, None, ALU.max), m1)

        def rnn_root():
            rnn["root"] = do("act", lambda e: e.activation(S0[:, :], S0[:, :], ACT.Sqrt), rnn["m", 7])

        def rnn_scan(c):
            am, mm, u = S1[:, 256 * c:256 * c + 256], S0[:, 256 * c:256 * c + 256], XR[:, c, 0:256]
            g = RB[:, 256 * c:256 * c + 256]
            T1, T3 = (TMP[:, 512:768], TMP[:, 768:1024]) if c % 2 else (TMP[:, 0:256], TMP[:, 256:512])
            a5 = do("act", lambda e: e.activation(T3, g, ACT.Square), rnn["g"], rnn["root"], rnn.get(("end", c - 2)))
            p = do("dve", lambda e: e.tensor_scalar(T3, T3, 0.044715, 1.0, ALU.mult, ALU.add), a5)
            w = do("dve", lambda e: e.scalar_tensor_tensor(u, u, 0.5, mm, ALU.mult, ALU.mult), rnn["root"], rnn["u", c])
            p = do("pool", lambda e: e.tensor_tensor(T3, T3, g, ALU.mult), p)
            s = do("dve", lambda e: e.tensor_tensor_scan(T1, am, u, 0.0, ALU.mult, ALU.add), w, rnn.get(("end", c - 2)))
            a6 = do("act", lambda e: e.activation(T3, T3, ACT.Tanh, scale=0.7978845608028654), p)
            p = do("dve", lambda e: e.scalar_tensor_tensor(T3, T3, 1.0, g, ALU.add, ALU.mult), a6, p)
            p = do("dve", lambda e: e.scalar_tensor_tensor(g, T3, 0.5, T1, ALU.mult, ALU.mult), p, s)
            rnn["end", c] = p
            rnn["y", c] = split_t(g, 1, c, 1, p)

        QK = v3(RC, 2, 1024)
        KV = v3(RD, 2, 512)
        qk_tok = []
        for b in range(3):
            banks, tok = tokens_by(("qkv", b), 2, TH[0], TL[0], 0, h_tok, 512)
            for t in range(2):
                o = QK[:, t, 512 * b:512 * b + 512] if b < 2 else KV[:, t, :]
                qk_tok.append(do("act", lambda e, o=o, i=PB[banks[t]]: e.activation(o, i[:, :], ACT.Copy), tok))
                free[banks[t]] = [qk_tok[-1]]
            if b == 0:
                bg.append(lambda: rnn_conv(0))
        g_tok = []
        for b in range(2):
            banks, tok = features_by(("g", b), 2, TH[0], TL[0], h_tok)
            for h in range(2):
                o = RB[:, (4 * b + 2 * h) * 256:(4 * b + 2 * h + 2) * 256]
                g_tok = [do("act", lambda e, o=o, i=PB[banks[h]][:, :]: e.activation(o, i, ACT.Copy), tok)]
                free[banks[h]] = g_tok
        rnn["g"] = g_tok
        for c in range(8):
            bg.append(lambda c=c: (rnn_conv(c + 1) if c < 7 else None, rnn_gates(c)))
        bg.append(rnn_root)
        for c in range(8):
            bg.append(lambda c=c: rnn_scan(c))

        at1 = {}
        rq, rk, rq8 = small(32), small(8), small(32)
        TB = KW[:, 0:512].rearrange("p (f t n) -> p f t n", f=8, t=2)

        def prep_tables():
            cosv, sinv = v3(CT, 2, 32, CAT["rope"]), v3(CT, 2, 32, CAT["rope"] + 64)
            f = 0
            for g in (gq, gk):
                for tab, half in ((cosv, 0), (sinv, 1), (cosv, 1), (sinv, 0)):
                    gb = g[:, 32 * half:32 * half + 32].unsqueeze(1).to_broadcast([128, 2, 32])
                    d = do("dve", lambda e, f=f, tab=tab, gb=gb: e.tensor_tensor(TB[:, f], tab, gb, ALU.mult), bc_tok, const_tok)
                    f += 1
            at1["tb"] = d

        def prep_sums():
            S0v = v3(S0, 2, 1024)
            a = do("act", lambda e: e.activation(S0[:, :], RC[:, :], ACT.Square), qk_tok, h_tok)
            d = do("dve", lambda e: e.tensor_reduce(rq[:, :].rearrange("p (a n) -> p a n", a=32)[:, :, 0],
                                                    S0[:, :].rearrange("p (a n) -> p a n", n=64), AXX, ALU.add), a)
            K2 = S1[:, 0:512].rearrange("p (t n) -> p t n", t=2)
            a = do("act", lambda e: e.activation(K2, KV[:, :, 0:256], ACT.Square), qk_tok, h_tok)
            d2 = do("dve", lambda e: e.tensor_reduce(rk[:, :], S1[:, 0:512].rearrange("p (a n) -> p a n", n=64), AXX, ALU.add), a)
            r = rsqrt_mean(rq, rq, 64, (d,))
            r2 = rsqrt_mean(rk, rk, 64, (d2,))
            at1["rq"] = do("dve", lambda e: e.tensor_scalar(rq8, rq, 0.125, None, ALU.mult), r)
            kv4 = KV[:, :, 0:256].rearrange("p t (h n) -> p t h n", h=4)
            rkb = rk[:, :].rearrange("p (t h) -> p t h", t=2)
            for t in range(2):
                d = do("dve", lambda e, t=t: e.tensor_tensor(kv4[:, t], kv4[:, t], rkb[:, t].unsqueeze(2).to_broadcast([128, 4, 64]),
                                                             ALU.mult), r2, a)
            at1["k"] = d

        def rope(src, dst, nh, f0, t, after, tmp):
            h = [src[:, :, 0:32], src[:, :, 32:64]]
            o = [dst[:, :, 0:32], dst[:, :, 32:64]]
            tb = [TB[:, f0 + i, t].unsqueeze(1).to_broadcast([128, nh, 32]) for i in range(4)]
            a = do("dve", lambda e: e.tensor_tensor(tmp[0], h[0], tb[0], ALU.mult), *after)
            b = do("pool", lambda e: e.tensor_tensor(tmp[1], h[1], tb[1], ALU.mult), *after)
            c = do("dve", lambda e: e.tensor_tensor(o[0], tmp[0], tmp[1], ALU.subtract), a, b)
            a = do("dve", lambda e: e.tensor_tensor(tmp[0], h[1], tb[2], ALU.mult), c)
            b = do("pool", lambda e: e.tensor_tensor(tmp[1], h[0], tb[3], ALU.mult), c)
            return do("dve", lambda e: e.tensor_tensor(o[1], tmp[0], tmp[1], ALU.add), a, b)

        def prep_rope():
            S1v = v3(S1, 2, 1024)
            for t in range(2):
                tmp = [S0[:, 512 * i:512 * i + 512].rearrange("p (h n) -> p h n", h=16) for i in range(2)]
                at1["q", t] = rope(QK[:, t].rearrange("p (h n) -> p h n", h=16), S1v[:, t].rearrange("p (h n) -> p h n", h=16),
                                   16, 0, t, (at1["tb"], at1["rq"], at1["k"], at1.get(("q", 0))), tmp)

        KD = v3(S0, 2, 512, 1024)

        def prep_rope_k():
            for t in range(2):
                kd = KD[:, t].rearrange("p (h c n) -> p h c n", h=4, c=2)
                tmp = [S0[:, 128 * i:128 * i + 128].rearrange("p (h n) -> p h n", h=4) for i in range(2)]
                k = rope(KV[:, t, 0:256].rearrange("p (h n) -> p h n", h=4), kd[:, :, 0, :], 4, 4, t,
                         (at1["q", 1], at1.get(("kd", 0))), tmp)
                at1["kd", t] = do("dve", lambda e, kd=kd: e.tensor_copy(kd[:, :, 1, :], kd[:, :, 0, :]), k)

        def prep_turn_k():
            for j in range(2):
                b = 2 + j
                for c in range(2):
                    for t in range(2):
                        m = do("pe", lambda e, c=c, t=t, j=j, b=b: e.transpose(
                            PB[b][:, c * 256 + t * 128:c * 256 + t * 128 + 128], KD[:, t, (2 * j + c) * 128:(2 * j + c) * 128 + 128],
                            ident), at1["kd", 1], free[b])
                a = do("act", lambda e, j=j, b=b: e.activation(KT[:, 512 * j:512 * j + 512], PB[b][:, :], ACT.Copy), m)
                free[b] = [a]
            at1["kT"] = a

        def prep_turn_q():
            at1["qT"] = turn_over(v3(S1, 2, 1024), 8, None, None, at1["q", 1], at1["kd", 1], banks=(2, 3), f32=RC)

        def group(name, heads, lhs, rhs, mask, kparts, exp_scale, ready, negmax, vals, dst, w):
            SS = S0[:, 0:1536].rearrange("p (h n) -> p h n", h=4)
            mx = w["mx"]
            nm = w["nm"]
            dn = w["dn"]

            def scores():
                for i, h in enumerate(heads):
                    b = i % 2
                    do("pe", lambda e, h=h, b=b: e.matmul(PB[b][:, 0:128], lhs(h, 0), rhs(h, 0, 128), start=True, stop=True,
                                                          skip_group_check=True), ready, free[b], silent=True)
                    m = do("pe", lambda e, h=h, b=b: e.matmul(PB[b][:, 128:384], lhs(h, 1), rhs(h, 0, 256), start=False, stop=True,
                                                              skip_group_check=True))
                    d = do("dve", lambda e, i=i, b=b: e.tensor_tensor(SS[:, i], PB[b][:, 0:384], mask, ALU.add), m,
                           w.get("pt"), w.get("s0"))
                    free[b] = [d]
                d1 = do("dve", lambda e: e.tensor_reduce(mx[:, 0:4], SS[:, :, 0:128], AXX, ALU.max), d)
                d2 = do("dve", lambda e: e.tensor_reduce(mx[:, 4:8], SS[:, :, 128:384], AXX, ALU.max), d)
                nd = negmax(heads, mx, nm, d2)
                for i, h in enumerate(heads):
                    for t in range(2):
                        sl = SS[:, i, 0:128] if t == 0 else SS[:, i, 128:384]
                        a = do("act", lambda e, sl=sl, i=i, t=t, h=h: e.activation(
                            sl, sl, ACT.Exp, bias=nm[:, 4 * t + i:4 * t + i + 1], scale=exp_scale(h, t),
                            accum_out=dn[:, 4 * t + i:4 * t + i + 1]), nd, w.get("rd"))
                w["exp"] = a

            def denom():
                a = w["exp"]
                if "sink" in w:
                    a = w["sink"](heads, nm, dn, a)
                d = do("dve", lambda e: e.reciprocal(dn, dn), a)
                for i in range(4):
                    for t in range(2):
                        sl = SS[:, i, 0:128] if t == 0 else SS[:, i, 128:384]
                        d2 = do("dve", lambda e, sl=sl, i=i, t=t: e.tensor_scalar(sl, sl, dn[:, 4 * t + i:4 * t + i + 1], None,
                                                                                 ALU.mult), d)
                w["p"] = d2
                w["rd"] = d2

            def values(half):
                def run():
                    for i in (2 * half, 2 * half + 1):
                        h = heads[i]
                        PT = w["area"][:, 384 * (i % 2):384 * (i % 2) + 384]
                        for j in range(3):
                            m = do("pe", lambda e, i=i, j=j: e.transpose(PB[2][:, 128 * j:128 * j + 128],
                                                                         SS[:, i, 128 * j:128 * j + 128], ident),
                                   w["p"], free[2])
                        a = do("act", lambda e, PT=PT: e.activation(PT, PB[2][:, 0:384], ACT.Copy), m, w.get(("v", i % 2)), w.get("s1"))
                        free[2] = [a]
                        w["pt"] = m
                        w["pt", i % 2] = a
                    for i in (2 * half, 2 * half + 1):
                        h = heads[i]
                        PT = w["area"][:, 384 * (i % 2):384 * (i % 2) + 384]
                        rows = slice(64 * (h % 2), 64 * (h % 2) + 64)
                        do("pe", lambda e, h=h, PT=PT, rows=rows: e.matmul(PB[3][rows, 0:128], vals(h, 0), PT[:, 0:128], start=True,
                                                                           stop=True, skip_group_check=True),
                           w["pt", i % 2], free[3], silent=True)
                        do("pe", lambda e, h=h, PT=PT, rows=rows: e.matmul(PB[3][rows, 128:256], vals(h, 0), PT[:, 128:256],
                                                                           start=False, stop=False, skip_group_check=True),
                           silent=True)
                        m = do("pe", lambda e, h=h, PT=PT, rows=rows: e.matmul(PB[3][rows, 128:256], vals(h, 1), PT[:, 256:384],
                                                                               start=False, stop=True, skip_group_check=True))
                        w["v", i % 2] = m
                    c = heads[2 * half] // 2
                    o = dst[:, 256 * c:256 * c + 256]
                    a = do("act", lambda e, o=o: e.activation(o, PB[3][:, 0:256], ACT.Copy), m, w.get("dst"))
                    free[3] = [a]
                    w["o", c] = a
                return run

            return [scores, denom, values(0), values(1)]

        def neg1(heads, mx, nm, tok):
            for t in range(2):
                o = nm[:, 4 * t:4 * t + 4]
                r = rq8[:, 16 * t + heads[0]:16 * t + heads[0] + 4]
                d = do("dve", lambda e, t=t, o=o, r=r: e.tensor_tensor(o, mx[:, 4 * t:4 * t + 4], r, ALU.mult), tok, at1["rq"],
                       w1.get("rd"))
                d = do("dve", lambda e, o=o: e.tensor_tensor(o, o, snk[:, heads[0]:heads[0] + 4], ALU.max), d)
                d = do("dve", lambda e, o=o: e.tensor_scalar(o, o, -1.0, None, ALU.mult), d)
            return d

        def sink1(heads, nm, dn, tok):
            for t in range(2):
                o = w1["sk"][:, 4 * t:4 * t + 4]
                d = do("dve", lambda e, t=t, o=o: e.tensor_tensor(o, nm[:, 4 * t:4 * t + 4], snk[:, heads[0]:heads[0] + 4], ALU.add),
                       tok)
            a = do("act", lambda e: e.activation(w1["sk"], w1["sk"], ACT.Exp), d)
            return do("dve", lambda e: e.tensor_tensor(dn, dn, w1["sk"], ALU.add), a)

        w1 = {"area": S1, "mx": small(8), "nm": small(8), "dn": small(8), "sk": small(8), "sink": sink1}

        def attention1(n):
            if n == 0:
                w1["s0"] = at1["kT"]
                w1["s1"] = at1["qT"]
                w1["dst"] = rnn["xc", 7]
            heads = [4 * n + i for i in range(4)]

            def lhs(h, t):
                r = slice(64 * (h % 2), 64 * (h % 2) + 64)
                c = (h // 2) * 256 + t * 128
                return RC[r, c:c + 128]

            def rhs(h, a, b):
                r = slice(64 * (h % 2), 64 * (h % 2) + 64)
                c = (h // 4) * 256
                return KT[r, c + a:c + b]

            return group("a1", heads, lhs, rhs, cst("mask1", 384), 64,
                         lambda h, t: rq8[:, 16 * t + h:16 * t + h + 1], [at1["kT"], at1["qT"]], neg1,
                         lambda h, t: KV[:, t, 256 + 64 * (h // 4):256 + 64 * (h // 4) + 64], RA, w1)

        bg += [prep_tables, prep_sums, prep_rope, prep_rope_k, prep_turn_k, prep_turn_q]
        for n in range(4):
            for s in range(4):
                bg.append(lambda n=n, s=s: attention1(n)[s]())

        def gates(key, th, tl, ready, steps, reuse=None):
            toks = [None, None]
            for b in range(4):
                banks, tok = tokens_by((key, b), 2, th, tl, 0, ready, 512, steps)
                g = (GA, GB)[b // 2]
                for t in range(2):
                    o = v3(g, 2, 1024)[:, t, 512 * (b % 2):512 * (b % 2) + 512]
                    a = do("act", lambda e, o=o, i=PB[banks[t]][:, :]: e.activation(o, i, ACT.Tanh, scale=0.5), tok, reuse)
                    free[banks[t]] = [a]
                    toks[b // 2] = a
            return toks

        def gated(key, nu, th, tl, ready, g, gtok, steps=1):
            for b in range(2):
                banks, tok = tokens_by((key, b), nu, th, tl, 0, ready, 512, steps)
                for t in range(2):
                    o = v3(g, 2, 1024)[:, t, 512 * b:512 * b + 512]
                    d = do("dve", lambda e, o=o, i=PB[banks[t]][:, :]: e.scalar_tensor_tensor(o, o, 1.0, i, ALU.add, ALU.mult),
                           tok, gtok)
                    free[banks[t]] = [d]
            return d, tok

        def residual(key, th, tl, ready, xtok):
            for b in range(2):
                banks, tok = tokens_by((key, b), 2, th, tl, 0, ready, 512)
                for t in range(2):
                    o = v3(X, 2, 1024)[:, t, 512 * b:512 * b + 512]
                    d = do("dve", lambda e, o=o, i=PB[banks[t]][:, :]: e.tensor_tensor(o, o, i, ALU.add), tok, xtok)
                    free[banks[t]] = [d]
            return d, tok

        ga_tok, gb_tok = gates("gates", TH[0], TL[0], h_tok, 2)
        while ("y", 7) not in rnn:
            step()
        ya_ready = [rnn["y", c] for c in range(8)]
        d, ya_pe = gated("w_rnn_proj", 2, TH[1], TL[1], [t for y in ya_ready for t in y], GA, ga_tok, 2)
        flush()
        o_tok = [split_t(RA[:, 512 * c:512 * c + 512], 0, 2 * c, 2, [w1["o", k] for k in range(8)], used_done[st["used"] - 1])
                 for c in range(4)]
        d2, yb_pe = gated("w_attn_proj", 2, TH[0], TL[0], [t for y in o_tok for t in y], GB, gb_tok)
        d3 = do("dve", lambda e: e.tensor_tensor(GA[:, :], GA[:, :], GB[:, :], ALU.add), d, d2)
        m_tok = turn_over(v3(GA, 2, 1024), 8, None, 1, d3, ya_pe, scale=0.5)
        x1, pe = residual("w_out", TH[1], TL[1], m_tok, x_tok)

        hm = norm(v3(X, 2, D), D, "g_mlp", 0, x1, yb_pe)
        hid = {}

        def mlp_down(b):
            for r in range(2):
                hi, lo, rdy = take(("w_down", b, r))
                for t in range(2):
                    for h in range(2):
                        bank = 2 * t + h
                        for k in range(2):
                            kk = 4 * (b % 2) + 2 * r + k
                            c = slice(kk * 256 + t * 128, kk * 256 + t * 128 + 128)
                            tok = mm3(PB[bank][:, :], TH[1][:, c], TL[1][:, c], hi[:, k, 512 * h:512 * h + 512],
                                      lo[:, k, 512 * h:512 * h + 512], b == 0 and r == 0 and k == 0,
                                      b == 7 and r == 1 and k == 1, (rdy, hid[b], free[bank]), k == 1)
                give(("w_down", b, r), tok)
            hid["used", b] = tok

        for b in range(9):
            if b < 8:
                banks, tok = features_by(("w_up", b), 2, TH[0], TL[0], hm)
                hid[b] = []
                for h in range(2):
                    c0 = 4 * (b % 2) + 2 * h
                    s = S1[:, c0 * 256:c0 * 256 + 512]
                    a = do("act", lambda e, s=s, i=PB[banks[h]][:, :]: e.activation(s, i, ACT.Relu), tok, hid.get(b - 2), hm)
                    free[banks[h]] = [a]
                    p = do("dve", lambda e, s=s: e.tensor_tensor(s, s, s, ALU.mult), a)
                    hid[b] += split_t(s, 1, c0, 2, p, [hid.get(("used", b - 2)), pe])
            if b > 0:
                mlp_down(b - 1)
        up_pe = hid["used", 7]
        for t in range(2):
            for h in range(2):
                o = v3(X, 2, 1024)[:, t, 512 * h:512 * h + 512]
                x2 = do("dve", lambda e, o=o, i=PB[2 * t + h][:, :]: e.tensor_tensor(o, o, i, ALU.add), up_pe)
                free[2 * t + h] = [x2]

        P = v3(GB, 2, 256)
        p_tok = Q.dma("act", "p", lambda e: e.dma_start(P, A["p"][0, 0].rearrange("(t p) d -> p t d", p=128)), d3)
        mem_tok = Q.dma("act", "mem", lambda e: e.dma_start(v3(RC, 2, D), A["mem_2"][0].rearrange("(t p) d -> p t d", p=128)),
                        w1["o", 7])
        pt_tok = turn_over(P, 2, None, 1, p_tok, up_pe)
        EB = v3(RB, 2, 1024)
        for b in range(2):
            banks, tok = tokens_by(("w_ple_proj", b), 1, TH[1], TL[1], 0, pt_tok, 512)
            for t in range(2):
                e_tok = do("act", lambda e, b=b, t=t, i=PB[banks[t]][:, :]: e.activation(EB[:, t, 512 * b:512 * b + 512], i, ACT.Copy),
                           tok, ya_pe)
                free[banks[t]] = [e_tok]
        ple_pe = tok
        xg = norm(v3(X, 2, D), D, "g_ple", 0, x2, up_pe)
        GT = v3(GA, 2, 1024)
        for b in range(2):
            banks, tok = tokens_by(("w_ple_gate", b), 2, TH[0], TL[0], 0, xg, 512)
            for t in range(2):
                g = GT[:, t, 512 * b:512 * b + 512]
                ee = EB[:, t, 512 * b:512 * b + 512]
                xx = v3(X, 2, 1024)[:, t, 512 * b:512 * b + 512]
                a = do("act", lambda e, g=g, i=PB[banks[t]][:, :]: e.activation(g, i, ACT.Tanh, scale=0.5), tok, m_tok)
                free[banks[t]] = [a]
                d = do("dve", lambda e, g=g, ee=ee: e.scalar_tensor_tensor(g, g, 1.0, ee, ALU.add, ALU.mult), a, e_tok)
                x3 = do("dve", lambda e, g=g, xx=xx: e.scalar_tensor_tensor(xx, g, 0.5, xx, ALU.mult, ALU.add), d)
        gate_pe = tok

        MN = norm(v3(RC, 2, D), D, "mem_norm_g_2", 1, mem_tok, ple_pe)
        for b in range(2):
            banks, tok = features_by(("w_xkv_2", b), 2, TH[1], TL[1], MN)
            for h in range(2):
                c0 = 4 * b + 2 * h
                mk_tok = do("act", lambda e, c0=c0, i=PB[banks[h]][:, :]: e.activation(RA[:, c0 * 256:c0 * 256 + 512], i, ACT.Copy),
                            tok, o_tok[3])
                free[banks[h]] = [mk_tok]
        MV = v3(RB, 2, 1024)
        for b in range(2):
            banks, tok = tokens_by(("w_xkv_2", b + 2), 2, TH[1], TL[1], 0, MN, 512)
            for t in range(2):
                mv_tok = do("act", lambda e, b=b, t=t, i=PB[banks[t]][:, :]: e.activation(MV[:, t, 512 * b:512 * b + 512], i, ACT.Copy),
                            tok, d)
                free[banks[t]] = [mv_tok]
        mem_pe = tok

        h2 = norm(v3(X, 2, D), D, "mix_norm_g_2", 0, x3, gate_pe)
        QL = v3(RC, 2, 384)
        KL = v3(RC, 2, 288, 768)
        banks, tok = tokens_by(("lat", 0), 2, TH[0], TL[0], 0, h2, 384)
        for t in range(2):
            ql_tok = do("act", lambda e, t=t, i=PB[banks[t]][:, 0:384]: e.activation(QL[:, t], i, ACT.Copy), tok, MN)
            free[banks[t]] = [ql_tok]
        banks, tok = tokens_by(("lat", 1), 2, TH[0], TL[0], 0, h2, 288)
        for t in range(2):
            kl_tok = do("act", lambda e, t=t, i=PB[banks[t]][:, 0:288]: e.activation(KL[:, t], i, ACT.Copy), tok, MN)
            free[banks[t]] = [kl_tok]
        U = v3(TMP, 4, 272)
        zt = do("pool", lambda e: e.memset(U[:, :, 0:16], 0.0), rnn["end", 7])
        banks, tok = features_by(("lat", 2), 2, TH[0], TL[0], h2)
        for h in range(2):
            u_tok = do("act", lambda e, h=h, i=v3(PB[banks[h]], 2, 256): e.activation(U[:, 2 * h:2 * h + 2, 16:272], i, ACT.Copy), tok,
                       rnn["end", 7])
            free[banks[h]] = [u_tok]
        pw_tok = Q.dma("act", "pool_w", lambda e: e.dma_start(v3(BD, 4, 128, 0), A["pool_w_2"][0].rearrange("g c e -> c g e")),
                       rnn["mm", 7])
        PW = v3(BD, 4, 128, 0)
        po = {}
        W2 = [S0[:, 272 * i:272 * i + 272] for i in range(4)]

        def pool_group(g):
            def run():
                w = 2 << g
                src = U[:, g, :]
                d = None
                for j in range(g + 1):
                    dst = W2[j % 2]
                    s = 1 << j
                    d0 = do("dve", lambda e, dst=dst, src=src, s=s: e.tensor_copy(dst[:, 0:s], src[:, 0:s]), d, u_tok, zt, h2,
                            po.get(("d", g - 1)))
                    d = do("dve", lambda e, dst=dst, src=src, s=s: e.tensor_tensor(dst[:, s:272], src[:, s:272], src[:, 0:272 - s],
                                                                                 ALU.add), d0, d)
                    src = dst
                m = W2[2]
                a = do("dve", lambda e: e.tensor_tensor(m[:, 0:16], src[:, 16:32], cst("count", 16, 16 * g), ALU.mult), d)
                b = do("dve", lambda e: e.tensor_scalar(m[:, 16:256], src[:, 32:272], 1.0 / w, None, ALU.mult), d)
                d = do("dve", lambda e: e.tensor_tensor(po_d[:, g, :], m[:, 0:256], U[:, g, 16:272], ALU.subtract), a, b)
                po["d", g] = d
            return run

        po_d = v3(S0, 4, 256, 1024)

        def pool_mm():
            for g in range(4):
                b = g // 2
                m = do("pe", lambda e, g=g, b=b: e.matmul(PB[b][:, 256 * (g % 2):256 * (g % 2) + 256], PW[:, g, :], po_d[:, g, :],
                                                          start=True, stop=True, skip_group_check=True), po["d", g], pw_tok, free[b])
                if g % 2:
                    for j in (g - 1, g):
                        d = do("dve", lambda e, j=j, b=b: e.tensor_scalar(S1[:, 256 * j:256 * j + 256],
                                                                        PB[b][:, 256 * (j % 2):256 * (j % 2) + 256],
                                                                        col("pool_scale_2", j), None, ALU.mult), m, h2)
                    free[b] = [d]
            po["u"] = split_t(S1[:, 0:1024], 1, 0, 4, d, mem_pe)

        pos_i = SM[:, small_at[0]:small_at[0] + 2].bitcast(I32)
        small(2)
        posf, ang, kk_, cs = small(2), small(32), small(32), small(64)
        for t in range(2):
            pos_tok = Q.dma("act", "pos", lambda e, t=t: e.dma_start(
                pos_i[:, t:t + 1], A["positions_2"][0, 128 * t:128 * t + 128].rearrange("(p o) -> p o", o=1)))
        C1, C2 = 6.28125, 0.0019350051879882812
        C3 = TWO_PI - C1 - C2

        def angles():
            d = do("dve", lambda e: e.tensor_copy(posf, pos_i), pos_tok)
            for t in range(2):
                d2 = do("dve", lambda e, t=t: e.tensor_scalar(ang[:, 16 * t:16 * t + 16], cst("inv", 16), posf[:, t:t + 1], None, ALU.mult),
                        d, const_tok)
            for j, ph in enumerate((0.25, 0.0)):
                o = cs[:, 32 * j:32 * j + 32]
                d = do("dve", lambda e, ph=ph: e.tensor_scalar(kk_, ang, 1.0 / TWO_PI, ph, ALU.mult, ALU.add), d2, d)
                d = do("dve", lambda e: e.tensor_scalar(kk_, kk_, 12582912.0, None, ALU.add), d)
                d = do("dve", lambda e: e.tensor_scalar(kk_, kk_, -12582912.0, None, ALU.add), d)
                d = do("dve", lambda e, o=o: e.scalar_tensor_tensor(o, kk_, -C1, ang, ALU.mult, ALU.add), d)
                d = do("dve", lambda e, o=o: e.scalar_tensor_tensor(o, kk_, -C2, o, ALU.mult, ALU.add), d)
                d = do("dve", lambda e, o=o: e.scalar_tensor_tensor(o, kk_, -C3, o, ALU.mult, ALU.add), d)
                if j == 0:
                    d = do("dve", lambda e, o=o: e.tensor_scalar(o, o, TWO_PI / 4, None, ALU.add), d)
                d = do("dve", lambda e, o=o: e.tensor_scalar(o, o, 3.1415925, -3.1415925, ALU.min, ALU.max), d)
            po["cs"] = do("act", lambda e: e.activation(cs, cs, ACT.Sin), d)

        bg += [angles] + [pool_group(g) for g in range(4)] + [pool_mm]
        ga2, gb2 = gates("gates2", TH[0], TL[0], h2, 1, [x3])
        flush()
        h2_pe = used_done[st["used"] - 1]
        qn = norm(QL, 384, "q_norm_g_2", 0, [ql_tok, *po["u"]], h2_pe)
        kvn_src = v3(RC, 2, 288, 768)[:, :, 0:256]
        kr = small(64)
        kr_tok = do("dve", lambda e: e.tensor_copy(v3(kr, 2, 32), KL[:, :, 256:288]), kl_tok)
        qbanks = [tokens_by(("w_q_up_2", b), 1, TH[0], TL[0], 0, qn, 384) for b in range(2)]
        q_pe = qbanks[1][1]
        kvn = norm(kvn_src, 256, "kv_norm_g_2", 0, [kl_tok, kr_tok], q_pe)
        QM = v3(RC, 2, 768)
        for b in range(2):
            banks, tok = qbanks[b]
            for t in range(2):
                qm_tok = do("act", lambda e, b=b, t=t, i=PB[banks[t]][:, 0:384]: e.activation(QM[:, t, 384 * b:384 * b + 384], i, ACT.Copy),
                            tok, kvn, kr_tok)
                free[banks[t]] = [qm_tok]
        KC = S0[:, 0:1536].rearrange("p (t h n) -> p t h n", t=2, h=8)
        VM = RD[:, :].rearrange("p (t h n) -> p t h n", t=2, h=8)
        for b in range(2):
            banks, tok = tokens_by(("w_kv_up_2", b), 1, TH[0], TL[0], 0, kvn, 512)
            for t in range(2):
                i = PB[banks[t]][:, :].rearrange("p (h n) -> p h n", h=4)
                a1 = do("act", lambda e, b=b, t=t, i=i: e.activation(KC[:, t, 4 * b:4 * b + 4, 0:64], i[:, :, 0:64], ACT.Copy), tok, kvn)
                a2 = do("act", lambda e, b=b, t=t, i=i: e.activation(VM[:, t, 4 * b:4 * b + 4, :], i[:, :, 64:128], ACT.Copy), tok)
                free[banks[t]] = [a2]
        kvm_tok = a2
        kv_pe = tok
        c4 = cs[:, 0:32].rearrange("p (t n) -> p t n", t=2)
        s4 = cs[:, 32:64].rearrange("p (t n) -> p t n", t=2)
        m0 = S1[:, 1024:1152].rearrange("p (h n) -> p h n", h=8)
        m1 = S1[:, 1152:1280].rearrange("p (h n) -> p h n", h=8)
        m2 = S1[:, 1280:1408].rearrange("p (h n) -> p h n", h=8)
        m3 = S1[:, 1408:1536].rearrange("p (h n) -> p h n", h=8)
        d = None
        for t in range(2):
            q1 = QM[:, t].rearrange("p (h n) -> p h n", h=8)
            c8 = c4[:, t].unsqueeze(1).to_broadcast([128, 8, 16])
            s8 = s4[:, t].unsqueeze(1).to_broadcast([128, 8, 16])
            a_, b_ = q1[:, :, 64:80], q1[:, :, 80:96]
            ds = [do("dve", lambda e, o=o, x=x, y=y: e.tensor_tensor(o, x, y, ALU.mult), qm_tok, po["cs"], kvn, d)
                  for o, x, y in ((m0, a_, c8), (m1, b_, s8), (m2, b_, c8), (m3, a_, s8))]
            d = do("dve", lambda e, a_=a_: e.tensor_tensor(a_, m0, m1, ALU.subtract), ds[-1])
            d = do("dve", lambda e, b_=b_: e.tensor_tensor(b_, m2, m3, ALU.add), ds[-1])
            k1, k2 = kr[:, 32 * t:32 * t + 16], kr[:, 32 * t + 16:32 * t + 32]
            n = [S1[:, 1536 + 16 * j:1552 + 16 * j] for j in range(6)]
            ds = [do("dve", lambda e, o=o, x=x, y=y: e.tensor_tensor(o, x, y, ALU.mult), kr_tok, po["cs"], kvn, d)
                  for o, x, y in ((n[0], k1, c4[:, t]), (n[1], k2, s4[:, t]), (n[2], k2, c4[:, t]), (n[3], k1, s4[:, t]))]
            d = do("dve", lambda e, n=n: e.tensor_tensor(n[4], n[0], n[1], ALU.subtract), ds[-1])
            d = do("dve", lambda e, n=n: e.tensor_tensor(n[5], n[2], n[3], ALU.add), ds[-1])
            d = do("dve", lambda e, t=t: e.tensor_copy(KC[:, t, :, 64:96], S1[:, 1600:1632].unsqueeze(1).to_broadcast([128, 8, 32])),
                   d, kvn)
        rope2 = d
        for h in range(8):
            bank = (h // 2) % 4
            for t in range(2):
                m = do("pe", lambda e, h=h, t=t, bank=bank: e.transpose(
                    PB[bank][0:96, 256 * (h % 2) + 128 * t:256 * (h % 2) + 128 * t + 128], QM[:, t, 96 * h:96 * h + 96], ident),
                    rope2, free[bank])
            if h % 2:
                a = do("act", lambda e, h=h, bank=bank: e.activation(S1[0:96, 256 * (h - 1):256 * (h + 1)], PB[bank][0:96, :], ACT.Copy),
                       m, rope2)
                free[bank] = [a]
        qt2_tok = a
        for h in range(8):
            bank = (h // 2) % 4
            for t in range(2):
                m = do("pe", lambda e, h=h, t=t, bank=bank: e.transpose(
                    PB[bank][0:96, 256 * (h % 2) + 128 * t:256 * (h % 2) + 128 * t + 128], KC[:, t, h, :], ident),
                    rope2, kvm_tok, free[bank])
            if h % 2:
                a = do("act", lambda e, h=h, bank=bank: e.activation(RC[0:96, 256 * (h - 1):256 * (h + 1)], PB[bank][0:96, :], ACT.Copy),
                       m, qt2_tok)
                free[bank] = [a]
        kt2_tok = a

        SC2 = 1.0 / float(np.sqrt(96.0))

        def neg2(heads, mx, nm, tok):
            return do("dve", lambda e: e.tensor_scalar(nm, mx, -SC2, None, ALU.mult), tok, w2.get("rd"))

        w2 = {"area": KT, "mx": w1["mx"], "nm": w1["nm"], "dn": w1["dn"], "s0": kt2_tok}
        OT2 = TMP

        def group2(n):
            heads = [4 * n + i for i in range(4)]
            SS = S0[:, 0:1536].rearrange("p (h n) -> p h n", h=4)
            return group("a2", heads, lambda h, t: S1[0:96, 256 * h + 128 * t:256 * h + 128 * t + 128],
                         lambda h, a, b: RC[0:96, 256 * h + a:256 * h + b], cst("mask2", 384), 96,
                         lambda h, t: SC2, [qt2_tok, kt2_tok], neg2, lambda h, t: VM[:, t, h, :], TMP, w2)

        w2["dst"] = po["d", 3]
        for n in range(2):
            for s in range(4):
                bg.append(lambda n=n, s=s: group2(n)[s]())
        d, pb_pe = gated("w_pool_branch_2", 1, TH[1], TL[1], po["u"], GB, gb2, 2)
        flush()
        ot = split_t(TMP[:, 0:1024], 0, 0, 4, [w2["o", k] for k in range(4)], kv_pe)
        d2, at_pe = gated("w_attn_branch_2", 1, TH[0], TL[0], ot, GA, ga2)
        d3 = do("dve", lambda e: e.tensor_tensor(GA[:, :], GA[:, :], GB[:, :], ALU.add), d, d2)
        m_tok = turn_over(v3(GA, 2, 1024), 8, None, 1, d3, [pb_pe, w2["v", 0], w2["v", 1]], scale=0.5)
        x4, mo_pe = residual("w_mix_out_2", TH[1], TL[1], m_tok, None)

        hx = norm(v3(X, 2, D), D, "xattn_norm_g_2", 0, x4, at_pe)
        for b in range(2):
            banks, tok = features_by(("w_xq_2", b), 2, TH[0], TL[0], hx)
            for h in range(2):
                c0 = 4 * b + 2 * h
                xq_tok = do("act", lambda e, c0=c0, i=PB[banks[h]][:, :]: e.activation(RC[:, c0 * 256:c0 * 256 + 512], i, ACT.Copy), tok)
                free[banks[h]] = [xq_tok]
        xq_pe = tok
        xa = {}
        mx4, dn4 = small(8), small(8)
        for h in range(4):
            b = h % 2
            for t in range(2):
                for k in range(2):
                    c = (2 * h + k) * 256
                    m = do("pe", lambda e, b=b, t=t, k=k, c=c: e.matmul(
                        PB[b][:, 256 * t:256 * t + 256], RC[:, c + 128 * t:c + 128 * t + 128], RA[:, c:c + 256],
                        start=(t == 0 and k == 0), stop=(k == 1), skip_group_check=True), xq_tok, mk_tok, free[b])
            E = S0[:, 512 * (h % 2):512 * (h % 2) + 512]
            mm = mx4[:, 2 * h:2 * h + 2]
            dd = dn4[:, 2 * h:2 * h + 2]
            d = do("dve", lambda e, b=b, mm=mm: e.tensor_reduce(mm, v3(PB[b], 2, 256), AXX, ALU.max), m)
            d = do("dve", lambda e, mm=mm: e.tensor_scalar(mm, mm, -0.0625, None, ALU.mult), d)
            for t in range(2):
                a = do("act", lambda e, b=b, t=t, E=E, mm=mm, dd=dd: e.activation(
                    E[:, 256 * t:256 * t + 256], PB[b][:, 256 * t:256 * t + 256], ACT.Exp, bias=mm[:, t:t + 1], scale=0.0625,
                    accum_out=dd[:, t:t + 1]), d, xa.get(("p", h - 2)), hx)
            free[b] = [a]
            d = do("dve", lambda e, dd=dd: e.reciprocal(dd, dd), a)
            for t in range(2):
                d2 = do("dve", lambda e, t=t, E=E, dd=dd: e.tensor_scalar(E[:, 256 * t:256 * t + 256], E[:, 256 * t:256 * t + 256],
                                                                        dd[:, t:t + 1], None, ALU.mult), d)
            for mt in range(2):
                for t in range(2):
                    m = do("pe", lambda e, mt=mt, t=t, E=E: e.transpose(PB[2][:, 256 * mt + 128 * t:256 * mt + 128 * t + 128],
                                                                       E[:, 256 * t + 128 * mt:256 * t + 128 * mt + 128], ident),
                           d2, free[2])
            xa["p", h] = m
            PTm = S0[:, 1024 + 512 * (h % 2):1536 + 512 * (h % 2)]
            a = do("act", lambda e, PTm=PTm: e.activation(PTm, PB[2][:, :], ACT.Copy), m, xa.get(("v", h - 2)), hx)
            free[2] = [a]
            for dv in range(2):
                for mt in range(2):
                    c = 256 * h + 128 * dv
                    m = do("pe", lambda e, dv=dv, mt=mt, c=c, PTm=PTm: e.matmul(
                        PB[3][:, 256 * dv:256 * dv + 256], MV[:, mt, c:c + 128], PTm[:, 256 * mt:256 * mt + 256],
                        start=(dv == 0 and mt == 0), stop=(mt == 1), skip_group_check=True), a, mv_tok, free[3])
            xa["v", h] = m
            o = GB[:, 512 * h:512 * h + 512]
            a = do("act", lambda e, o=o: e.activation(o, PB[3][:, :], ACT.Copy), m, d3)
            free[3] = [a]
            xa["o", h] = split_t(o, 1, 2 * h, 2, a, mo_pe)
        x5, xo_pe = residual("w_xo_2", TH[1], TL[1], [t for h in range(4) for t in xa["o", h]], None)

        hf = norm(v3(X, 2, D), D, "ffn_norm_g_2", 0, x5, xq_pe)
        banks = pair()
        hi, lo, rdy = take(("router", 0, 0))
        L = small(72)
        L3 = v3(L, 2, 36)
        for t in range(2):
            for k in range(8):
                c = slice(k * 256 + t * 128, k * 256 + t * 128 + 128)
                tok = mm3(PB[banks[t]][:, 0:36], TH[0][:, c], TL[0][:, c], hi[:, k, :], lo[:, k, :], k == 0, k == 7,
                          (rdy, hf, free[banks[t]]), k == 7)
            lt = do("dve", lambda e, t=t, b=banks[t]: e.tensor_tensor(L3[:, t], PB[b][:, 0:36], rb, ALU.add), tok, bc_tok)
            free[banks[t]] = [lt]
        give(("router", 0, 0), tok)

        at_ = [0]

        def rt(n):
            o = at_[0]
            at_[0] += n
            return KW[:, o:o + n]

        def b3(ap, n):
            return ap.unsqueeze(2).to_broadcast([128, 2, n])

        def first_max(src, n, dst, mxt, order, tok):
            v = v3(rt(2 * n), 2, n)
            d = do("dve", lambda e: e.tensor_reduce(mxt, src, AXX, ALU.max), tok)
            d = do("dve", lambda e: e.tensor_tensor(v, src, b3(mxt, n), ALU.is_equal), d)
            od = cst("order", n, order).unsqueeze(1).to_broadcast([128, 2, n])
            d = do("dve", lambda e: e.tensor_tensor(v, v, od, ALU.mult), d)
            q = rt(2)
            d = do("dve", lambda e: e.tensor_reduce(q, v, AXX, ALU.max), d)
            return do("dve", lambda e: e.tensor_tensor(dst, v, b3(q, n), ALU.is_equal), d)

        G = L3[:, :, 0:4]
        og = v3(rt(8), 2, 4)
        gm = rt(2)
        d = first_max(G, 4, og, gm, 0, lt)
        eg = v3(rt(8), 2, 4)
        d = do("dve", lambda e: e.tensor_tensor(eg, G, b3(gm, 4), ALU.subtract), d)
        a = do("act", lambda e: e.activation(eg, eg, ACT.Exp), d)
        pg = rt(2)
        d = do("dve", lambda e: e.tensor_reduce(pg, eg, AXX, ALU.add), a)
        d = do("dve", lambda e: e.reciprocal(pg, pg), d)
        se = rt(64)
        sel = v3(rt(16), 2, 8)
        for t in range(2):
            t4 = se[:, 32 * t:32 * t + 32].rearrange("p (g n) -> p g n", g=4)
            d = do("dve", lambda e, t=t, t4=t4: e.tensor_tensor(t4, L3[:, t, 4:36].rearrange("p (g n) -> p g n", g=4),
                                                              og[:, t].unsqueeze(2).to_broadcast([128, 4, 8]), ALU.mult), d)
            d = do("dve", lambda e, t=t: e.tensor_reduce(sel[:, t], se[:, 32 * t:32 * t + 32].rearrange("p (g n) -> p n g", g=4),
                                                         AXX, ALU.add), d)
        o1, o2 = v3(rt(16), 2, 8), v3(rt(16), 2, 8)
        ma, mb = rt(2), rt(2)
        d = first_max(sel, 8, o1, ma, 4, d)
        s2 = v3(rt(16), 2, 8)
        d = do("dve", lambda e: e.scalar_tensor_tensor(s2, o1, NEG, sel, ALU.mult, ALU.add), d)
        d = first_max(s2, 8, o2, mb, 4, d)
        e2 = rt(2)
        d = do("dve", lambda e: e.tensor_tensor(e2, mb, ma, ALU.subtract), d)
        a = do("act", lambda e: e.activation(e2, e2, ACT.Exp), d)
        wa, wb = rt(2), rt(2)
        d = do("dve", lambda e: e.tensor_scalar(wa, e2, 1.0, None, ALU.add), a)
        d = do("dve", lambda e: e.reciprocal(wa, wa), d)
        d = do("dve", lambda e: e.scalar_tensor_tensor(wa, wa, 0.5, pg, ALU.mult, ALU.mult), d)
        d = do("dve", lambda e: e.tensor_tensor(wb, wa, e2, ALU.mult), d)
        d = do("dve", lambda e: e.tensor_tensor(o1, o1, b3(wa, 8), ALU.mult), d)
        d = do("dve", lambda e: e.tensor_tensor(o2, o2, b3(wb, 8), ALU.mult), d)
        d = do("dve", lambda e: e.tensor_tensor(o1, o1, o2, ALU.add), d)
        cw = se
        for t in range(2):
            d = do("dve", lambda e, t=t: e.tensor_tensor(cw[:, 32 * t:32 * t + 32].rearrange("p (g n) -> p g n", g=4),
                                                         og[:, t].unsqueeze(2).to_broadcast([128, 4, 8]),
                                                         o1[:, t].unsqueeze(1).to_broadcast([128, 4, 8]), ALU.mult), d)
        for t in range(2):
            m = do("pe", lambda e, t=t: e.transpose(PB[0][0:32, 128 * t:128 * t + 128], cw[:, 32 * t:32 * t + 32], ident), d, free[0])
        cwT = KT[0:32, 0:256]
        a = do("act", lambda e: e.activation(cwT, PB[0][0:32, 0:256], ACT.Copy), m)
        free[0] = [a]
        AREA = [S0, S1, RA, RB]
        cwb = {}
        for e_ in range(0, NE, 2):
            b = (e_ // 2) % 4
            for j in range(2):
                m = do("pe", lambda e, x=e_ + j, b=b, j=j: e.matmul(PB[b][:, 256 * j:256 * j + 256],
                                                                    ident[0:32, x:x + 1].to_broadcast([32, 128]), cwT,
                                                                    start=True, stop=True, skip_group_check=True), a, free[b])
            ar = AREA[e_ // 8]
            eng = "act" if e_ % 4 else "dve"
            o = ar[:, 256 * (e_ % 8):256 * (e_ % 8) + 512]
            if eng == "act":
                k = do("act", lambda e, o=o, b=b: e.activation(o, PB[b][:, :], ACT.Copy), m, hf, xa["v", 3])
            else:
                k = do("dve", lambda e, o=o, b=b: e.tensor_copy(o, PB[b][:, :]), m, hf, xa["v", 3])
            free[b] = [k]
            cwb[e_] = cwb[e_ + 1] = k

        fing = Q.dma("act", "fing", lambda e: e.dma_start(RC[:, 0:1024], A["final_norm_g_2"].partition_broadcast(128)), xa["v", 3])
        ex = {}

        def moe_down(e_):
            hi, lo, rdy = take(("moe_out", e_, 0))
            for t in range(2):
                for h in range(2):
                    bank = 2 * t + h
                    for k in range(2):
                        kk = 2 * (e_ % 2) + k
                        c = slice(kk * 256 + t * 128, kk * 256 + t * 128 + 128)
                        tok = mm3(PB[bank][:, :], TH[1][:, c], TL[1][:, c], hi[:, k, 512 * h:512 * h + 512],
                                  lo[:, k, 512 * h:512 * h + 512], e_ == 0 and k == 0, e_ == NE - 1 and k == 1,
                                  (rdy, ex[e_], free[bank]), k == 1)
            give(("moe_out", e_, 0), tok)
            ex["used", e_] = tok

        for e_ in range(NE + 1):
            if e_ < NE:
                banks, tok = features_by(("moe_in", e_), 2, TH[0], TL[0], hf)
                s = GA[:, 512 * (e_ % 2):512 * (e_ % 2) + 512]
                a = do("act", lambda e, s=s, i=PB[banks[0]][:, :]: e.activation(s, i, ACT.Tanh, scale=0.5), tok, m_tok,
                       ex.get(e_ - 2))
                d = do("dve", lambda e, s=s, i=PB[banks[0]][:, :]: e.scalar_tensor_tensor(s, s, 1.0, i, ALU.add, ALU.mult), a)
                free[banks[0]] = [d]
                d = do("dve", lambda e, s=s, i=PB[banks[1]][:, :]: e.tensor_tensor(s, s, i, ALU.mult), d)
                free[banks[1]] = [d]
                cb = AREA[e_ // 8][:, 256 * (e_ % 8):256 * (e_ % 8) + 256].unsqueeze(1).to_broadcast([128, 2, 256])
                p = do("pool", lambda e, s=s, cb=cb: e.tensor_tensor(v3(s, 2, 256), v3(s, 2, 256), cb, ALU.mult), d, cwb[e_])
                ex[e_] = split_t(s, 1, 2 * (e_ % 2), 2, p, [ex.get(("used", e_ - 2)), xo_pe])
            if e_ > 0:
                moe_down(e_ - 1)
        x6 = []
        for t in range(2):
            for h in range(2):
                o = v3(X, 2, 1024)[:, t, 512 * h:512 * h + 512]
                x6 = do("dve", lambda e, o=o, i=PB[2 * t + h][:, :]: e.tensor_tensor(o, o, i, ALU.add), ex["used", NE - 1])

        fs, fr = rt(2), rt(2)
        Xv = v3(X, 2, 1024)
        for t in range(2):
            a = do("act", lambda e, t=t: e.activation(v3(S0, 2, 1024)[:, t], Xv[:, t], ACT.Square, accum_out=fs[:, t:t + 1]), x6, ex[NE - 1])
        r = rsqrt_mean(fr, fs, D, (a,))
        for t in range(2):
            d = do("dve", lambda e, t=t: e.scalar_tensor_tensor(v3(S1, 2, 1024)[:, t], Xv[:, t], fr[:, t:t + 1], RC[:, 0:1024],
                                                              ALU.mult, ALU.mult), r, fing, ex[NE - 1])
            o_ = Q.dma("sp", "out", lambda e, t=t: e.dma_start(out[0, 128 * t:128 * t + 128, :], v3(S1, 2, 1024)[:, t]), d)
        Q.wait("sp", (o_,))


def kernel(**inputs):
    import concourse.bacc as _bacc
    from concourse.bass_utils import run_bass_kernel_spmd as _run

    nc = _bacc.Bacc("TRN2", target_bir_lowering=False, num_devices=1)
    arrays, aps = {}, {}
    for name, a in {**inputs, "const": constants()}.items():
        a = np.ascontiguousarray(a)
        arrays[f"in_{name}"] = a
        aps[name] = nc.dram_tensor(f"in_{name}", a.shape, mybir.dt.from_np(a.dtype), kind="ExternalInput").ap()
    out = nc.dram_tensor("out_0", (1, S, D), F, kind="ExternalOutput").ap()
    build(nc, aps, out)
    r = _run(nc, [arrays], core_ids=[0])
    return r.results[0]["out_0"]
```

```python
from contextlib import ExitStack

import numpy as np

import concourse.bass as bass
from concourse import mybir

ALU = mybir.AluOpType
ACT = mybir.ActivationFunctionType
AXX = mybir.AxisListType.X
F = mybir.dt.float32
R = mybir.dt.float32r
I32 = mybir.dt.int32

S = 256
D = 1024
NRAW = 4
NW = 3
SLOT = 2048
EPS = 1e-6
NEG = -1e30
TWO_PI = 6.283185307179586
NE = 32
WAY = 0

ROWS1 = [("g_mix", 8), ("conv_w", 32), ("conv_b", 8), ("b_rg", 8), ("b_ig", 8), ("lru_lambda", 8),
         ("g_mlp", 8), ("g_ple", 8), ("mix_norm_g_2", 8), ("xattn_norm_g_2", 8), ("mem_norm_g_2", 8),
         ("ffn_norm_g_2", 8)]
ROWS2 = [("q_norm_g_2", 3), ("kv_norm_g_2", 2), ("pool_scale_2", 4)]
CONSTS = [("ident", 128), ("mask1", 384), ("mask2", 384), ("rope", 128), ("inv", 16), ("order", 12),
          ("count", 64), ("slots", 64), ("upper", 128), ("ones", 128)]


def offsets(rows):
    out, at = {}, 0
    for name, n in rows:
        out[name] = at
        at += n
    return out, at


def constants():
    at, n = offsets(CONSTS)
    c = np.zeros((128, n), np.float32)
    c[:, at["ident"]:at["ident"] + 128] = np.eye(128, dtype=np.float32)
    q = np.arange(128)[:, None]
    k = np.arange(128)[None, :]
    m = at["mask1"]
    c[:, m:m + 128] = np.where(k <= q, 0.0, NEG)
    c[:, m + 128:m + 256] = np.where(k > q, 0.0, NEG)
    c[:, m + 256:m + 384] = np.where(k <= q, 0.0, NEG)
    m = at["mask2"]
    c[:, m:m + 128] = np.where(k // 64 <= q // 64, 0.0, NEG)
    c[:, m + 256:m + 384] = np.where(k // 64 <= q // 64, 0.0, NEG)
    inv = (np.float32(10000.0) ** (-np.arange(0, 64, 2, dtype=np.float32) / np.float32(64))).astype(np.float32)
    ang = (np.arange(S, dtype=np.float32)[:, None] * inv[None, :]).astype(np.float32)
    m = at["rope"]
    for t in range(2):
        c[:, m + 32 * t:m + 32 * t + 32] = np.cos(ang[128 * t:128 * t + 128])
        c[:, m + 64 + 32 * t:m + 96 + 32 * t] = np.sin(ang[128 * t:128 * t + 128])
    c[:, at["inv"]:at["inv"] + 16] = (
        np.float32(1.0) / (np.float32(10000.0) ** (np.arange(0, 32, 2, dtype=np.float32) / np.float32(32))))
    c[:, at["order"]:at["order"] + 4] = 4 - np.arange(4)
    c[:, at["order"] + 4:at["order"] + 12] = 8 - np.arange(8)
    for g, w in enumerate((2, 4, 8, 16)):
        c[:, at["count"] + 16 * g:at["count"] + 16 * g + 16] = 1.0 / np.minimum(np.arange(16) + 1, w)
    c[:, at["slots"]:at["slots"] + 64] = np.arange(64)
    c[:, at["upper"]:at["upper"] + 128] = q < k
    c[:, at["ones"]:at["ones"] + 128] = 1.0
    return c


def plan_units():
    u = []

    def mat(name, lead, k, cols, key=None):
        nk = k // 128
        for b, (c0, w) in enumerate(cols):
            for r in range(0, nk, 4):
                u.append(((key or name, b, r // 4), [(name, lead, r * 128, min(4, nk - r), c0, w, 0)]))

    mat("w_in", (0,), 1024, [(512 * b, 512) for b in (0, 1)], "x")
    mat("w_in", (0,), 1024, [(2048, 512), (2560, 512), (3072, 512)], "qkv")
    mat("w_in", (0,), 1024, [(1024, 512), (1536, 512)], "g")
    mat("w_in", (0,), 1024, [(3584 + 512 * b, 512) for b in range(4)], "gates")
    mat("w_rnn_proj", (0,), 1024, [(0, 512), (512, 512)])
    mat("w_xkv_2", (0,), 1024, [(512 * b, 512) for b in range(4)])
    mat("w_attn_proj", (0,), 1024, [(0, 512), (512, 512)])
    mat("w_out", (0,), 1024, [(0, 512), (512, 512)])
    for b in range(9):
        if b < 8:
            for r in range(2):
                u.append((("w_up", b, r), [("w_up", (0,), 512 * r, 4, 512 * b, 512, 0)]))
        if b > 0:
            for r in range(2):
                u.append((("w_down", b - 1, r), [("w_down", (0,), 512 * (b - 1) + 256 * r, 2, 0, 1024, 0)]))
    mat("w_ple_proj", (0,), 256, [(0, 512), (512, 512)])
    mat("w_ple_gate", (0,), 1024, [(0, 512), (512, 512)])
    mat("w_in_2", (0,), 1024, [(0, 384), (384, 288), (672, 512)], "lat")
    g2 = [(("gates2", b, r), [("w_in_2", (0,), 512 * r, 4, 1184 + 512 * b, 512, 0)]) for b in range(4) for r in range(2)]
    u += g2[0:2]
    mat("w_q_up_2", (0,), 384, [(0, 384), (384, 384)])
    u += g2[2:4]
    mat("w_kv_up_2", (0,), 256, [(0, 512), (512, 512)])
    u += g2[4:8]
    mat("w_pool_branch_2", (0,), 512, [(0, 512), (512, 512)])
    mat("w_attn_branch_2", (0,), 512, [(0, 512), (512, 512)])
    mat("w_mix_out_2", (0,), 1024, [(0, 512), (512, 512)])
    mat("w_xq_2", (0,), 1024, [(0, 512), (512, 512)])
    mat("w_xo_2", (0,), 1024, [(0, 512), (512, 512)])
    u.append((("router", 0, 0), [("w_router_group_2", (0,), 0, 8, 0, 4, 0), ("w_router_expert_2", (0,), 0, 8, 0, 32, 4)]))
    for p in range(NE // 2 + 1):
        for e in (2 * p, 2 * p + 1):
            if p < NE // 2:
                for r in range(2):
                    u.append((("moe_in", e, r), [("w_exp_gate_2", (0, e), 512 * r, 4, 0, 256, 0),
                                                 ("w_exp_up_2", (0, e), 512 * r, 4, 0, 256, 256)]))
        for e in (2 * p - 2, 2 * p - 1):
            if p > 0:
                u.append((("moe_out", e, 0), [("w_exp_down_2", (0, e), 0, 2, 0, 1024, 0)]))
    return u


def tokens(after):
    for t in after:
        if isinstance(t, dict):
            yield from tokens(t.values())
        elif isinstance(t, list):
            yield from tokens(t)
        elif t is not None:
            yield t


class Engines:

    def __init__(self, engines, sems):
        self.engines = engines
        self.sems = sems
        self.count = {k: 0 for k in sems}
        self.seen = {k: {} for k in engines}

    def wait(self, eng, after):
        need = {}
        for name, value in tokens(after):
            need[name] = max(need.get(name, 0), value)
        for name, value in need.items():
            if self.seen[eng].get(name, 0) < value:
                self.seen[eng][name] = value
                self.engines[eng].wait_ge(self.sems[name], value)

    def do(self, eng, fn, *after, silent=False):
        self.wait(eng, after)
        ins = fn(self.engines[eng])
        if silent:
            return None
        self.count[eng] += 1
        ins.then_inc(self.sems[eng], 1)
        return (eng, self.count[eng])

    def dma(self, eng, sem, fn, *after):
        self.wait(eng, after)
        self.count[sem] += 16
        fn(self.engines[eng]).then_inc(self.sems[sem], 16)
        return (sem, self.count[sem])


def build(nc, A, out, dumps=None, until=None):
    with ExitStack() as ctx:
        dma_sems = ([f"w{i}" for i in range(NRAW)] +
                    ["x", "rows", "const", "bd", "bcast", "mem", "pos", "fb", "pool_w", "p", "fing", "out"])
        sems = {k: ctx.enter_context(nc.semaphore(f"s_{k}")) for k in ["pe", "act", "dve", "pool"] + dma_sems}
        Q = Engines({"pe": nc.tensor, "act": nc.scalar, "dve": nc.vector, "pool": nc.gpsimd, "sp": nc.sync}, sems)
        do = Q.do

        def sb(name, n, dt=F):
            return ctx.enter_context(nc.sbuf_tensor(name, [128, n], dt))

        RAW = [sb(f"raw{i}", SLOT) for i in range(NRAW)]
        WH = [sb(f"wh{i}", SLOT, R) for i in range(NW)]
        WL = [sb(f"wl{i}", SLOT, R) for i in range(NW)]
        TH = [sb(f"th{i}", 2048, R) for i in range(2)]
        TL = [sb(f"tl{i}", 2048, R) for i in range(2)]
        X = sb("X", 2048)
        S0 = sb("S0", 2048)
        S1 = sb("S1", 2048)
        KW = sb("KW", 512)
        PC = sb("PC", 129)
        CAT, CN = offsets(CONSTS)
        CT = sb("CT", CN)
        NR = sb("NR", 96)
        SM = sb("SM", 704)
        early = ExitStack()

        def sbe(name, n, dt=F, stack=early):
            return stack.enter_context(nc.sbuf_tensor(name, [128, n], dt))

        RA = sbe("RA", 2080)
        RB = sbe("RB", 2048)
        RC = sbe("RC", 2048)
        RD = sbe("RD", 1024)
        GA = sbe("GA", 2048)
        GB = sbe("GB", 2048)
        KT = sbe("KT", 1024)
        BD = sbe("BD", 1024)
        TMP = sbe("TMP", 1280)
        PB = [ctx.enter_context(nc.psum_tensor(f"pb{i}", [128, 512], F)) for i in range(8)]

        def v3(t, a, n, off=0):
            return t[:, off:off + a * n].rearrange("p (a n) -> p a n", a=a)

        def cst(name, n=None, off=0):
            o = CAT[name] + off
            return CT[:, o:o + n]

        ident = cst("ident", 128)
        R1, _ = offsets(ROWS1)
        R2, _ = offsets(ROWS2)
        PCOL = {**R1, **{k: v + 120 for k, v in R2.items()}}

        def col(name, c):
            o = PCOL[name] + c
            return PC[:, o:o + 1]

        small_at = [0]

        def small(n):
            o = small_at[0]
            small_at[0] += n
            assert small_at[0] <= 704, small_at
            return SM[:, o:o + n]

        free = {b: [] for b in range(8)}

        units = plan_units()
        index = {key: i for i, (key, _) in enumerate(units)}
        st = {"loaded": 0, "split": 0, "used": 0}
        raw_ready, split_done, used_done = {}, {}, {}

        def shape_of(i):
            _, parts = units[i]
            kc = parts[0][3]
            return kc, sum(p[5] for p in parts)

        def load(i):
            _, parts = units[i]
            kc, w = shape_of(i)
            dst = v3(RAW[i % NRAW], kc, w)
            after = split_done.get(i - NRAW, [])
            for (name, lead, r0, n, c0, cw, at) in parts:
                src = A[name]
                for j in lead:
                    src = src[j]
                src = src[r0:r0 + n * 128, c0:c0 + cw].rearrange("(k p) n -> p k n", p=128)
                tok = Q.dma("sp", f"w{i % NRAW}", lambda e, d=dst[:, :, at:at + cw], s=src: e.dma_start(d, s), after)
            raw_ready[i] = tok

        def split(i):
            kc, w = shape_of(i)
            n = kc * w
            raw, hi, lo = RAW[i % NRAW][:, 0:n], WH[i % NW][:, 0:n], WL[i % NW][:, 0:n]
            a = do("act", lambda e: e.activation(hi, raw, ACT.Copy), raw_ready[i], used_done.get(i - NW))
            m = n - (n // 4) // 4 * 4
            b = do("dve", lambda e: e.tensor_tensor(lo[:, 0:m], raw[:, 0:m], hi[:, 0:m].bitcast(F), ALU.subtract),
                   raw_ready[i], a, used_done.get(i - NW))
            c = do("pool", lambda e: e.tensor_tensor(lo[:, m:n], raw[:, m:n], hi[:, m:n].bitcast(F), ALU.subtract),
                   raw_ready[i], a, used_done.get(i - NW))
            split_done[i] = [a, b, c]

        def load_to(n):
            while st["loaded"] < min(n, len(units)):
                load(st["loaded"])
                st["loaded"] += 1

        def split_to(n):
            while st["split"] < min(n, len(units)):
                i = st["split"]
                load_to(i + 1)
                split(i)
                st["split"] += 1
                load_to(i + 1 + NRAW)

        def take(key):
            i = index[key]
            assert i == st["used"], (key, i, st)
            split_to(i + NW)
            kc, w = shape_of(i)
            return v3(WH[i % NW], kc, w), v3(WL[i % NW], kc, w), split_done[i]

        def give(key, tok):
            used_done[index[key]] = tok
            st["used"] += 1

        def mm3(o, lh, ll, rh, rl, start, stop, after, last):
            do("pe", lambda e: e.matmul(o, lh, rh, start=start, stop=False, skip_group_check=True), *after,
               silent=True)
            do("pe", lambda e: e.matmul(o, lh, rl, start=False, stop=False, skip_group_check=True), silent=True)
            return do("pe", lambda e: e.matmul(o, ll, rh, start=False, stop=stop, skip_group_check=True),
                      silent=not last)

        bg = []

        def step(n=1):
            for _ in range(n):
                if bg:
                    bg.pop(0)()

        def flush():
            while bg:
                bg.pop(0)()

        turn = [0]

        def pair():
            turn[0] ^= 1
            return (4, 5) if turn[0] else (6, 7)

        def part(ready, kk):
            return ready.get(kk) if isinstance(ready, dict) else ready

        def tokens_by(key, nu, th, tl, k0, ready, w, steps=1):
            banks = pair()
            for r in range(nu):
                hi, lo, rdy = take((*key, r))
                kc = shape_of(index[(*key, r)])[0]
                for t in range(2):
                    o = PB[banks[t]][:, 0:w]
                    for k in range(kc):
                        kk = k0 + 4 * r + k
                        c = slice(kk * 256 + t * 128, kk * 256 + t * 128 + 128)
                        tok = mm3(o, th[:, c], tl[:, c], hi[:, k, 0:w], lo[:, k, 0:w], r == 0 and k == 0,
                                  r == nu - 1 and k == kc - 1, (rdy, part(ready, kk), free[banks[t]]), k == kc - 1)
                give((*key, r), tok)
                step(steps)
            return banks, tok

        def features_by(key, nu, th, tl, ready, steps=1):
            banks = pair()
            for r in range(nu):
                hi, lo, rdy = take((*key, r))
                kc = shape_of(index[(*key, r)])[0]
                for c in range(4):
                    b = banks[c // 2]
                    o = PB[b][:, (c % 2) * 256:(c % 2) * 256 + 256]
                    for k in range(kc):
                        kk = 4 * r + k
                        x = slice(kk * 256, kk * 256 + 256)
                        cs = slice(c * 128, c * 128 + 128)
                        tok = mm3(o, hi[:, k, cs], lo[:, k, cs], th[:, x], tl[:, x], r == 0 and k == 0 and c % 2 == 0,
                                  r == nu - 1 and k == kc - 1, (rdy, part(ready, kk), free[b]), k == kc - 1)
                give((*key, r), tok)
                step(steps)
            return banks, tok

        def split_t(src, which, c0, n, after, reuse=None):
            hi = TH[which][:, c0 * 256:(c0 + n) * 256]
            lo = TL[which][:, c0 * 256:(c0 + n) * 256]
            a = do("act", lambda e: e.activation(hi, src, ACT.Copy), after, reuse)
            b = do("dve", lambda e: e.tensor_tensor(lo, src, hi.bitcast(F), ALU.subtract), after, a, reuse)
            return [a, b]

        def split_psum(src, which, c, scale, after, reuse):
            hi, lo = TH[which][:, 256 * c:256 * c + 256], TL[which][:, 256 * c:256 * c + 256]
            a = do("act", lambda e: e.activation(hi, src, ACT.Copy, scale=scale), after, pc_tok, reuse)
            b = do("dve", lambda e: e.scalar_tensor_tensor(lo, src, scale, hi.bitcast(F), ALU.mult, ALU.subtract), after, a, reuse)
            return [a, b]

        def turn_over(src, chunks, gain, which, ready, reuse, dg=None, scale=1.0, c0=0, banks=(0, 1, 2, 3)):
            toks = {}
            for c in chunks:
                b = banks[c % len(banks)]
                for t in range(2):
                    o = PB[b][:, 128 * t:128 * t + 128]
                    x = src[:, t, 128 * c:128 * c + 128]
                    if dg is None:
                        m = do("pe", lambda e: e.transpose(o, x, ident), part(ready, c), free[b], c_tok)
                    else:
                        m = do("pe", lambda e: e.matmul(o, x, dg[:, 128 * t:128 * t + 128], start=True, stop=True,
                                                        skip_group_check=True), part(ready, c), free[b])
                g = col(gain, c) if gain else scale
                free[b] = toks[c0 + c] = split_psum(PB[b][:, 0:256], which, c0 + c, g, m, reuse)
                last["turn"] = m
            return toks

        last = {}

        def rsqrt_mean(dst, ss, n, after):
            w = dst.shape[-1]
            v, y, t = NR[:, 0:w], NR[:, 32:32 + w], NR[:, 64:64 + w]
            d = do("dve", lambda e: e.tensor_scalar(v, ss, 1.0 / n, EPS, ALU.mult, ALU.add), *after)
            d = do("dve", lambda e: e.tensor_scalar(t.bitcast(I32), v.bitcast(I32), 1, None, ALU.logical_shift_right), d)
            d = do("dve", lambda e: e.tensor_scalar(y.bitcast(I32), t.bitcast(I32), -1.0, float(0x5f3759df), ALU.mult, ALU.add), d)
            for i in range(3):
                o = dst if i == 2 else y
                d = do("dve", lambda e: e.tensor_tensor(t, y, y, ALU.mult), d)
                d = do("dve", lambda e: e.scalar_tensor_tensor(t, t, -0.5, v, ALU.mult, ALU.mult), d)
                d = do("dve", lambda e: e.scalar_tensor_tensor(o, t, 1.5, y, ALU.add, ALU.mult), d)
            return d

        def squares(src, w, junk, ready, after):
            ss = small(2)
            for t in range(2):
                a = do("act", lambda e: e.activation(junk[:, 0:w], src[:, t, :], ACT.Square, accum_out=ss[:, t:t + 1]), ready, after,
                       last.get("junk"))
                last["junk"] = a
            return ss, a

        def root_mean(ss, w, dg, after, free_dg=None):
            rs = small(2)
            if ss.shape[-1] == 4:
                s2 = small(2)
                s4 = ss.rearrange("p (t b) -> p t b", t=2)
                after = do("dve", lambda e: e.tensor_tensor(s2, s4[:, :, 0], s4[:, :, 1], ALU.add), after)
                ss = s2
            r = rsqrt_mean(rs, ss, w, (after,))
            for t in range(2):
                d = do("dve", lambda e: e.tensor_scalar(dg[:, 128 * t:128 * t + 128], ident, rs[:, t:t + 1], None, ALU.mult), r,
                       free_dg, last.get("turn"), c_tok)
            return rs, d

        DG = KW[:, 0:256]

        def norm(src, w, gain, which, ready, reuse, after=None, ss=None, c0=0):
            if ss is None:
                ss, ready = squares(src, w, S0, ready, after)
            _, d = root_mean(ss, w, DG, ready)
            return turn_over(src, range(w // 128), gain, which, d, reuse, DG, c0=c0)

        x_tok = Q.dma("sp", "x", lambda e: e.dma_start(v3(X, 2, D), A["x"][0].rearrange("(t p) d -> p t d", p=128)))
        const_tok = Q.dma("act", "const", lambda e: e.dma_start(CT[:, :], A["const"]))
        load_to(1)
        at = 0
        for name, n in ROWS1:
            src = A[name].rearrange("o (c p) -> (o c) p", p=128) if name != "conv_w" else \
                A[name][0].rearrange("j (c p) -> (j c) p", p=128)
            rows_tok = Q.dma("act", "rows", lambda e, s=src, at=at, n=n: e.dma_start(S0[at:at + n, 0:128], s))
            at += n
        at = 0
        for name, n in ROWS2:
            src = A[name].rearrange("o (c p) -> (o c) p", p=128)
            rows_tok = Q.dma("act", "rows", lambda e, s=src, at=at, n=n: e.dma_start(S0[at:at + n, 128:256], s))
            at += n
        BDv = [v3(BD, 8, 64, 512 * j) for j in range(2)]
        for j, name in enumerate(("w_rg", "w_ig")):
            w = A[name][0].rearrange("(c h) i j -> h i c j", h=2)
            for h in range(2):
                bd_tok = Q.dma("act", "bd", lambda e, j=j, h=h, w=w: e.dma_start(BDv[j][64 * h:64 * h + 64, :, :], w[h]))
        gq = small(64)
        gk = small(64)
        snk = small(16)
        rb = small(36)
        for dst, src in ((gq, A["q_gain"][0]), (gk, A["k_gain"][0]), (snk, A["sinks"][0]),
                         (rb[:, 0:4], A["b_router_group_2"][0]), (rb[:, 4:36], A["b_router_expert_2"][0])):
            bc_tok = Q.dma("act", "bcast", lambda e, d=dst, s=src: e.dma_start(d, s.partition_broadcast(128)))
        c_tok = const_tok
        pe1 = do("pe", lambda e: e.transpose(PB[0][:, 0:120], S0[0:120, 0:128], ident[0:120, 0:120]), rows_tok, c_tok)
        pe2 = do("pe", lambda e: e.transpose(PB[0][:, 128:137], S0[0:9, 128:256], ident[0:9, 0:9]), pe1)
        a = do("act", lambda e: e.activation(PC[:, 0:120], PB[0][:, 0:120], ACT.Copy), pe2)
        pc_tok = do("act", lambda e: e.activation(PC[:, 120:129], PB[0][:, 128:137], ACT.Copy), pe2)
        free[0] = [pc_tok]

        lam = PC[:, PCOL["lru_lambda"]:PCOL["lru_lambda"] + 8]
        hb = small(16)
        sp4 = small(8)
        sp4n = small(8)
        l0, l1, l2, l3 = small(8), small(8), small(8), small(8)
        d = do("dve", lambda e: e.tensor_scalar(l0, lam, -1.0, None, ALU.mult), pc_tok)
        d = do("dve", lambda e: e.tensor_tensor(l0, l0, lam, ALU.max), d)
        a = do("act", lambda e: e.activation(l1, l0, ACT.Exp, scale=-1.0), d)
        d = do("dve", lambda e: e.tensor_scalar(l2, l1, 2.0, None, ALU.add), a)
        d = do("dve", lambda e: e.reciprocal(l2, l2), d)
        d = do("dve", lambda e: e.tensor_tensor(l1, l1, l2, ALU.mult), d)
        d = do("dve", lambda e: e.tensor_tensor(l2, l1, l1, ALU.mult), d)
        d = do("dve", lambda e: e.tensor_scalar(l3, l2, 1.0 / 15, None, ALU.mult), d)
        for n in (13, 11, 9, 7, 5, 3):
            d = do("dve", lambda e, n=n: e.scalar_tensor_tensor(l3, l3, 1.0 / n, l2, ALU.add, ALU.mult), d)
        d = do("dve", lambda e: e.scalar_tensor_tensor(l3, l3, 1.0, l1, ALU.add, ALU.mult), d)
        d = do("dve", lambda e: e.tensor_scalar(l0, lam, -1.0, 0.0, ALU.mult, ALU.max), d)
        d = do("dve", lambda e: e.scalar_tensor_tensor(l3, l3, 2.0, l0, ALU.mult, ALU.add), d)
        d = do("dve", lambda e: e.tensor_scalar(sp4, l3, 4.0, None, ALU.mult), d)
        d = do("dve", lambda e: e.tensor_scalar(sp4n, l3, -4.0, None, ALU.mult), d)
        sp_tok = do("dve", lambda e: e.tensor_scalar(hb, PC[:, PCOL["b_rg"]:PCOL["b_rg"] + 16], 0.5, None, ALU.mult), d)

        h_tok = norm(v3(X, 2, D), D, "g_mix", 0, x_tok, None, after=[pe2, pc_tok])
        XR = v3(RA, 8, 260)
        z = do("pool", lambda e: e.memset(XR[:, :, 0:3], 0.0))
        xr_tok = []
        for b in range(2):
            banks, tok = features_by(("x", b), 2, TH[0], TL[0], h_tok)
            for h in range(2):
                o = XR[:, 4 * b + 2 * h:4 * b + 2 * h + 2, 3:259]
                xr_tok = [do("act", lambda e, o=o, i=v3(PB[banks[h]], 2, 256): e.activation(o, i, ACT.Copy), tok)]
                free[banks[h]] = xr_tok

        rnn = {}
        XC = [TMP[:, 0:256], TMP[:, 256:512]]
        T1, T2, T3 = TMP[:, 512:768], TMP[:, 768:1024], TMP[:, 1024:1280]

        def rnn_conv(c):
            x = XR[:, c, :]
            xc = XC[c % 2]
            d = do("dve", lambda e: e.tensor_scalar(xc, x[:, 0:256], col("conv_w", c), col("conv_b", c), ALU.mult, ALU.add),
                   xr_tok, z, pc_tok, rnn.get(("mm", c - 2)))
            for j in range(1, 4):
                d = do("dve", lambda e, j=j: e.scalar_tensor_tensor(xc, x[:, j:j + 256], col("conv_w", 8 * j + c), xc,
                                                                    ALU.mult, ALU.add), d)
            rnn["xc", c] = d

        def rnn_gates(c):
            b = c % 2
            xc = XC[c % 2]
            for j in range(2):
                for h in range(2):
                    ps = slice(64 * h, 64 * h + 64)
                    m = do("pe", lambda e: e.matmul(PB[b][ps, 256 * j:256 * j + 256], BDv[j][ps, c, :], xc[ps, :],
                                                    start=True, stop=True, skip_group_check=True),
                           rnn["xc", c], bd_tok, free[b])
            rnn["mm", c] = m
            am, mm, u = S1[:, 256 * c:256 * c + 256], S0[:, 256 * c:256 * c + 256], XR[:, c, 0:256]
            a = do("act", lambda e: e.activation(T1, PB[b][:, 0:256], ACT.Tanh, bias=hb[:, c:c + 1], scale=0.5), m, sp_tok,
                   rnn.get(("m", c - 1)))
            a2 = do("act", lambda e: e.activation(T2, PB[b][:, 256:512], ACT.Tanh, bias=hb[:, 8 + c:9 + c], scale=0.5), m,
                    rnn.get(("u", c - 1)))
            free[b] = [a2]
            a3 = do("act", lambda e: e.activation(am, T1, ACT.Exp, bias=sp4n[:, c:c + 1], scale=sp4n[:, c:c + 1]), a, h_tok)
            a4 = do("act", lambda e: e.activation(T1, T1, ACT.Tanh, bias=sp4[:, c:c + 1], scale=sp4[:, c:c + 1]), a, a3)
            rnn["u", c] = do("dve", lambda e: e.scalar_tensor_tensor(u, T2, 1.0, xc, ALU.add, ALU.mult), a2, rnn["xc", c], m)
            q = do("pool", lambda e: e.tensor_tensor(mm, am, am, ALU.mult), a3, h_tok)
            m1 = do("dve", lambda e: e.scalar_tensor_tensor(mm, mm, 1.0, T1, ALU.add, ALU.mult), q, a4)
            rnn["m", c] = do("dve", lambda e: e.tensor_scalar(mm, mm, 2.0 ** -100, None, ALU.max), m1)

        def rnn_root():
            rnn["root"] = do("act", lambda e: e.activation(S0[:, :], S0[:, :], ACT.Sqrt), rnn["m", 7])

        def rnn_scan(c):
            am, mm, u = S1[:, 256 * c:256 * c + 256], S0[:, 256 * c:256 * c + 256], XR[:, c, 0:256]
            g = RB[:, 256 * c:256 * c + 256]
            T1, T3 = (TMP[:, 512:768], TMP[:, 768:1024]) if c % 2 else (TMP[:, 0:256], TMP[:, 256:512])
            a5 = do("act", lambda e: e.activation(T3, g, ACT.Square), rnn["g"], rnn["root"], rnn.get(("end", c - 2)))
            p = do("dve", lambda e: e.tensor_scalar(T3, T3, 0.044715, 1.0, ALU.mult, ALU.add), a5)
            w = do("dve", lambda e: e.scalar_tensor_tensor(u, u, 0.5, mm, ALU.mult, ALU.mult), rnn["root"], rnn["u", c])
            p = do("pool", lambda e: e.tensor_tensor(T3, T3, g, ALU.mult), p)
            s = do("dve", lambda e: e.tensor_tensor_scan(T1, am, u, 0.0, ALU.mult, ALU.add), w, rnn.get(("end", c - 2)))
            a6 = do("act", lambda e: e.activation(T3, T3, ACT.Tanh, scale=0.7978845608028654), p)
            p = do("dve", lambda e: e.scalar_tensor_tensor(T3, T3, 1.0, g, ALU.add, ALU.mult), a6, p)
            p = do("dve", lambda e: e.scalar_tensor_tensor(g, T3, 0.5, T1, ALU.mult, ALU.mult), p, s)
            rnn["end", c] = p
            rnn["y", c] = split_t(g, 1, c, 1, p)

        bg.append(lambda: rnn_conv(0))
        for c in range(8):
            bg.append(lambda c=c: (rnn_conv(c + 1) if c < 7 else None, rnn_gates(c)))
        bg.append(rnn_root)
        QK = v3(RC, 2, 1024)
        KV = v3(RD, 2, 512)
        qk_tok = []
        for b in range(3):
            banks, tok = tokens_by(("qkv", b), 2, TH[0], TL[0], 0, h_tok, 512)
            for t in range(2):
                o = QK[:, t, 512 * b:512 * b + 512] if b < 2 else KV[:, t, :]
                qk_tok.append(do("act", lambda e, o=o, i=PB[banks[t]]: e.activation(o, i[:, :], ACT.Copy), tok))
                free[banks[t]] = [qk_tok[-1]]
        g_tok = []
        for b in range(2):
            banks, tok = features_by(("g", b), 2, TH[0], TL[0], h_tok)
            for h in range(2):
                o = RB[:, (4 * b + 2 * h) * 256:(4 * b + 2 * h + 2) * 256]
                g_tok = [do("act", lambda e, o=o, i=PB[banks[h]][:, :]: e.activation(o, i, ACT.Copy), tok)]
                free[banks[h]] = g_tok
        rnn["g"] = g_tok
        for c in range(8):
            bg.append(lambda c=c: rnn_scan(c))

        at1 = {}
        rq, rk, rq8 = small(32), small(8), small(32)
        TB = KW[:, 0:512].rearrange("p (f t n) -> p f t n", f=8, t=2)

        def prep_tables():
            cosv, sinv = v3(CT, 2, 32, CAT["rope"]), v3(CT, 2, 32, CAT["rope"] + 64)
            f = 0
            for g in (gq, gk):
                for tab, half in ((cosv, 0), (sinv, 1), (cosv, 1), (sinv, 0)):
                    gb = g[:, 32 * half:32 * half + 32].unsqueeze(1).to_broadcast([128, 2, 32])
                    d = do("dve", lambda e, f=f, tab=tab, gb=gb: e.tensor_tensor(TB[:, f], tab, gb, ALU.mult), bc_tok, const_tok, h_tok)
                    f += 1
            at1["tb"] = d

        def prep_sums():
            S0v = v3(S0, 2, 1024)
            a = do("act", lambda e: e.activation(S0[:, :], RC[:, :], ACT.Square), qk_tok, h_tok, rnn["end", 7])
            d = do("dve", lambda e: e.tensor_reduce(rq[:, :].rearrange("p (a n) -> p a n", a=32)[:, :, 0],
                                                    S0[:, :].rearrange("p (a n) -> p a n", n=64), AXX, ALU.add), a)
            K2 = S1[:, 0:512].rearrange("p (t n) -> p t n", t=2)
            a = do("act", lambda e: e.activation(K2, KV[:, :, 0:256], ACT.Square), qk_tok, h_tok)
            d2 = do("dve", lambda e: e.tensor_reduce(rk[:, :], S1[:, 0:512].rearrange("p (a n) -> p a n", n=64), AXX, ALU.add), a)
            r = rsqrt_mean(rq, rq, 64, (d,))
            r2 = rsqrt_mean(rk, rk, 64, (d2,))
            at1["rq"] = do("dve", lambda e: e.tensor_scalar(rq8, rq, 0.125, None, ALU.mult), r)
            kv4 = KV[:, :, 0:256].rearrange("p t (h n) -> p t h n", h=4)
            rkb = rk[:, :].rearrange("p (t h) -> p t h", t=2)
            for t in range(2):
                d = do("dve", lambda e, t=t: e.tensor_tensor(kv4[:, t], kv4[:, t], rkb[:, t].unsqueeze(2).to_broadcast([128, 4, 64]),
                                                             ALU.mult), r2, a)
            at1["k"] = d

        def rope(src, dst, nh, f0, t, after, tmp):
            h = [src[:, :, 0:32], src[:, :, 32:64]]
            o = [dst[:, :, 0:32], dst[:, :, 32:64]]
            tb = [TB[:, f0 + i, t].unsqueeze(1).to_broadcast([128, nh, 32]) for i in range(4)]
            a = do("dve", lambda e: e.tensor_tensor(tmp[0], h[0], tb[0], ALU.mult), *after)
            b = do("pool", lambda e: e.tensor_tensor(tmp[1], h[1], tb[1], ALU.mult), *after)
            c = do("dve", lambda e: e.tensor_tensor(o[0], tmp[0], tmp[1], ALU.subtract), a, b)
            a = do("dve", lambda e: e.tensor_tensor(tmp[0], h[1], tb[2], ALU.mult), c)
            b = do("pool", lambda e: e.tensor_tensor(tmp[1], h[0], tb[3], ALU.mult), c)
            return do("dve", lambda e: e.tensor_tensor(o[1], tmp[0], tmp[1], ALU.add), a, b)

        def prep_rope():
            S1v = v3(S1, 2, 1024)
            for t in range(2):
                tmp = [S0[:, 512 * i:512 * i + 512].rearrange("p (h n) -> p h n", h=16) for i in range(2)]
                at1["q", t] = rope(QK[:, t].rearrange("p (h n) -> p h n", h=16), S1v[:, t].rearrange("p (h n) -> p h n", h=16),
                                   16, 0, t, (at1["tb"], at1["rq"], at1["k"], at1.get(("q", 0))), tmp)

        KD = v3(S0, 2, 512, 1024)

        def prep_rope_k():
            for t in range(2):
                kd = KD[:, t].rearrange("p (h c n) -> p h c n", h=4, c=2)
                tmp = [S0[:, 128 * i:128 * i + 128].rearrange("p (h n) -> p h n", h=4) for i in range(2)]
                k = rope(KV[:, t, 0:256].rearrange("p (h n) -> p h n", h=4), kd[:, :, 0, :], 4, 4, t,
                         (at1["q", 1], at1.get(("kd", 0))), tmp)
                at1["kd", t] = do("dve", lambda e, kd=kd: e.tensor_copy(kd[:, :, 1, :], kd[:, :, 0, :]), k)

        def prep_turn_k():
            for j in range(2):
                b = 2 + j
                for c in range(2):
                    for t in range(2):
                        m = do("pe", lambda e, c=c, t=t, j=j, b=b: e.transpose(
                            PB[b][:, c * 256 + t * 128:c * 256 + t * 128 + 128], KD[:, t, (2 * j + c) * 128:(2 * j + c) * 128 + 128],
                            ident), at1["kd", 1], free[b])
                a = do("act", lambda e, j=j, b=b: e.activation(KT[:, 512 * j:512 * j + 512], PB[b][:, :], ACT.Copy), m)
                free[b] = [a]
            at1["kT"] = a

        def prep_turn_q():
            S1v = v3(S1, 2, 1024)
            for j in range(4):
                b = 2 + j % 2
                for c in range(2):
                    for t in range(2):
                        m = do("pe", lambda e: e.transpose(PB[b][:, c * 256 + t * 128:c * 256 + t * 128 + 128],
                                                           S1v[:, t, (2 * j + c) * 128:(2 * j + c) * 128 + 128], ident),
                               at1["q", 1], free[b])
                a = do("act", lambda e: e.activation(RC[:, 512 * j:512 * j + 512], PB[b][:, :], ACT.Copy), m)
                free[b] = [a]
            at1["qT"] = a

        def group(name, heads, lhs, rhs, mask, kparts, exp_scale, ready, negmax, vals, dst, w):
            SS = S0[:, 0:1536].rearrange("p (h n) -> p h n", h=4)
            mx = w["mx"]
            nm = w["nm"]
            dn = w["dn"]

            def scores():
                for i, h in enumerate(heads):
                    b = i % 2
                    do("pe", lambda e, h=h, b=b: e.matmul(PB[b][:, 0:128], lhs(h, 0), rhs(h, 0, 128), start=True, stop=True,
                                                          skip_group_check=True), ready, free[b], silent=True)
                    m = do("pe", lambda e, h=h, b=b: e.matmul(PB[b][:, 128:384], lhs(h, 1), rhs(h, 0, 256), start=False, stop=True,
                                                              skip_group_check=True))
                    d = do("dve", lambda e, i=i, b=b: e.tensor_tensor(SS[:, i], PB[b][:, 0:384], mask, ALU.add), m,
                           w.get("pt"), w.get("s0"))
                    free[b] = [d]
                d1 = do("dve", lambda e: e.tensor_reduce(mx[:, 0:4], SS[:, :, 0:128], AXX, ALU.max), d)
                d2 = do("dve", lambda e: e.tensor_reduce(mx[:, 4:8], SS[:, :, 128:384], AXX, ALU.max), d)
                nd = negmax(heads, mx, nm, d2)
                for i, h in enumerate(heads):
                    for t in range(2):
                        sl = SS[:, i, 0:128] if t == 0 else SS[:, i, 128:384]
                        a = do("act", lambda e, sl=sl, i=i, t=t, h=h: e.activation(
                            sl, sl, ACT.Exp, bias=nm[:, 4 * t + i:4 * t + i + 1], scale=exp_scale(h, t),
                            accum_out=dn[:, 4 * t + i:4 * t + i + 1]), nd, w.get("rd"))
                w["exp"] = a

            def denom():
                a = w["exp"]
                if "sink" in w:
                    a = w["sink"](heads, nm, dn, a)
                d = do("dve", lambda e: e.reciprocal(dn, dn), a)
                for i in range(4):
                    for t in range(2):
                        sl = SS[:, i, 0:128] if t == 0 else SS[:, i, 128:384]
                        d2 = do("dve", lambda e, sl=sl, i=i, t=t: e.tensor_scalar(sl, sl, dn[:, 4 * t + i:4 * t + i + 1], None,
                                                                                 ALU.mult), d)
                w["p"] = d2
                w["rd"] = d2

            def values(half):
                def run():
                    for i in (2 * half, 2 * half + 1):
                        h = heads[i]
                        PT = w["area"][:, 384 * (i % 2):384 * (i % 2) + 384]
                        for j in range(3):
                            m = do("pe", lambda e, i=i, j=j: e.transpose(PB[2][:, 128 * j:128 * j + 128],
                                                                         SS[:, i, 128 * j:128 * j + 128], ident),
                                   w["p"], free[2])
                        a = do("act", lambda e, PT=PT: e.activation(PT, PB[2][:, 0:384], ACT.Copy), m, w.get(("v", i % 2)), w.get("s1"))
                        free[2] = [a]
                        w["pt"] = m
                        w["pt", i % 2] = a
                    for i in (2 * half, 2 * half + 1):
                        h = heads[i]
                        PT = w["area"][:, 384 * (i % 2):384 * (i % 2) + 384]
                        rows = slice(64 * (h % 2), 64 * (h % 2) + 64)
                        do("pe", lambda e, h=h, PT=PT, rows=rows: e.matmul(PB[3][rows, 0:128], vals(h, 0), PT[:, 0:128], start=True,
                                                                           stop=True, skip_group_check=True),
                           w["pt", i % 2], free[3], silent=True)
                        do("pe", lambda e, h=h, PT=PT, rows=rows: e.matmul(PB[3][rows, 128:256], vals(h, 0), PT[:, 128:256],
                                                                           start=False, stop=False, skip_group_check=True),
                           silent=True)
                        m = do("pe", lambda e, h=h, PT=PT, rows=rows: e.matmul(PB[3][rows, 128:256], vals(h, 1), PT[:, 256:384],
                                                                               start=False, stop=True, skip_group_check=True))
                        w["v", i % 2] = m
                    c = dst + heads[2 * half] // 2
                    w["o"][c] = split_psum(PB[3][:, 0:256], 1, c, 1.0, m, w["dst"])
                    free[3] = [w["o"][c]]
                return run

            return [scores, denom, values(0), values(1)]

        def neg1(heads, mx, nm, tok):
            for t in range(2):
                o = nm[:, 4 * t:4 * t + 4]
                r = rq8[:, 16 * t + heads[0]:16 * t + heads[0] + 4]
                d = do("dve", lambda e, t=t, o=o, r=r: e.tensor_tensor(o, mx[:, 4 * t:4 * t + 4], r, ALU.mult), tok, at1["rq"],
                       w1.get("rd"))
                d = do("dve", lambda e, o=o: e.tensor_tensor(o, o, snk[:, heads[0]:heads[0] + 4], ALU.max), d)
                d = do("dve", lambda e, o=o: e.tensor_scalar(o, o, -1.0, None, ALU.mult), d)
            return d

        def sink1(heads, nm, dn, tok):
            for t in range(2):
                o = w1["sk"][:, 4 * t:4 * t + 4]
                d = do("dve", lambda e, t=t, o=o: e.tensor_tensor(o, nm[:, 4 * t:4 * t + 4], snk[:, heads[0]:heads[0] + 4], ALU.add),
                       tok)
            a = do("act", lambda e: e.activation(w1["sk"], w1["sk"], ACT.Exp), d)
            return do("dve", lambda e: e.tensor_tensor(dn, dn, w1["sk"], ALU.add), a)

        w1 = {"area": S1, "mx": small(8), "nm": small(8), "dn": small(8), "sk": small(8), "sink": sink1, "o": {}}

        def attention1(n):
            if n == 0:
                w1["s0"] = at1["kT"]
                w1["s1"] = at1["qT"]
                w1["dst"] = ya_pe
            heads = [4 * n + i for i in range(4)]

            def lhs(h, t):
                r = slice(64 * (h % 2), 64 * (h % 2) + 64)
                c = (h // 2) * 256 + t * 128
                return RC[r, c:c + 128]

            def rhs(h, a, b):
                r = slice(64 * (h % 2), 64 * (h % 2) + 64)
                c = (h // 4) * 256
                return KT[r, c + a:c + b]

            return group("a1", heads, lhs, rhs, cst("mask1", 384), 64,
                         lambda h, t: rq8[:, 16 * t + h:16 * t + h + 1], [at1["kT"], at1["qT"]], neg1,
                         lambda h, t: KV[:, t, 256 + 64 * (h // 4):256 + 64 * (h // 4) + 64], 0, w1)

        def gates(key, th, tl, ready, steps, reuse=None):
            toks = [None, None]
            for b in range(4):
                banks, tok = tokens_by((key, b), 2, th, tl, 0, ready, 512, steps)
                g = (GA, GB)[b // 2]
                for t in range(2):
                    o = v3(g, 2, 1024)[:, t, 512 * (b % 2):512 * (b % 2) + 512]
                    a = do("act", lambda e, o=o, i=PB[banks[t]][:, :]: e.activation(o, i, ACT.Tanh, scale=0.5), tok, reuse)
                    free[banks[t]] = [a]
                    toks[b // 2] = a
            return toks

        def gated(key, nu, th, tl, ready, g, gtok, steps=1, k0=0, into=None):
            done = {}
            for b in range(2):
                banks, tok = tokens_by((key, b), nu, th, tl, k0, ready, 512, steps)
                for t in range(2):
                    o = v3(g, 2, 1024)[:, t, 512 * b:512 * b + 512]
                    d = do("dve", lambda e: e.scalar_tensor_tensor(o, o, 1.0, PB[banks[t]][:, :], ALU.add, ALU.mult), tok, gtok)
                    free[banks[t]] = [d]
                    if into is not None:
                        i = v3(into, 2, 1024)[:, t, 512 * b:512 * b + 512]
                        d = do("dve", lambda e: e.tensor_tensor(i, i, o, ALU.add), d)
                for c in range(4):
                    done[4 * b + c] = d
            return done, tok

        def squared(ss, t, b, tok, after=None):
            x = v3(X, 2, 1024)[:, t, 512 * b:512 * b + 512]
            j = 2 * t + b
            return do("act", lambda e: e.activation(S0[:, 512 * j:512 * j + 512], x, ACT.Square, accum_out=ss[:, j:j + 1]), tok,
                      after, last["junk"])

        def residual(key, th, tl, ready, xtok, after=None):
            ss = small(4)
            for b in range(2):
                banks, tok = tokens_by((key, b), 2, th, tl, 0, ready, 512)
                for t in range(2):
                    o = v3(X, 2, 1024)[:, t, 512 * b:512 * b + 512]
                    d = do("dve", lambda e: e.tensor_tensor(o, o, PB[banks[t]][:, :], ALU.add), tok, xtok)
                    free[banks[t]] = [d]
                    a = squared(ss, t, b, d, after)
            return a, tok, ss

        MD = TMP[:, 1024:1280]
        ml = {}

        def mem_stats():
            ss, a = squares(v3(RB, 2, D), D, TMP, mem_tok, rnn["y", 7])
            ml["d"] = root_mean(ss, D, MD, a, rnn["y", 7])[1]

        MN = {}

        def mem_turn(j):
            MN.update(turn_over(v3(RB, 2, D), range(4 * j, 4 * j + 4), "mem_norm_g_2", 0, ml["d"], gates_pe, MD, banks=(0, 1)))

        ga_tok, gb_tok = gates("gates", TH[0], TL[0], h_tok, 1)
        gates_pe = used_done[st["used"] - 1]
        while ("y", 7) not in rnn:
            step()
        mem_tok = Q.dma("act", "mem", lambda e: e.dma_start(v3(RB, 2, D), A["mem_2"][0].rearrange("(t p) d -> p t d", p=128)),
                        [rnn["y", c] for c in range(8)])
        bg += [prep_tables, prep_sums, mem_stats, prep_rope, lambda: mem_turn(0), prep_rope_k, lambda: mem_turn(1), prep_turn_k,
               prep_turn_q]
        d, ya_pe = gated("w_rnn_proj", 2, TH[1], TL[1], {c: rnn["y", c] for c in range(8)}, GA, ga_tok, 2)
        flush()
        for n in range(4):
            for s in range(4):
                bg.append(lambda n=n, s=s: attention1(n)[s]())

        for b in range(2):
            banks, tok = features_by(("w_xkv_2", b), 2, TH[0], TL[0], MN, 2)
            for h in range(2):
                c0 = 4 * b + 2 * h
                mk_tok = do("act", lambda e: e.activation(RA[:, c0 * 256:c0 * 256 + 512], PB[banks[h]][:, :], ACT.Copy),
                            tok, rnn["y", 7])
                free[banks[h]] = [mk_tok]
        MV = v3(RB, 2, 1024)
        for b in range(2):
            banks, tok = tokens_by(("w_xkv_2", b + 2), 2, TH[0], TL[0], 0, MN, 512, 2)
            for t in range(2):
                mv_tok = do("act", lambda e: e.activation(MV[:, t, 512 * b:512 * b + 512], PB[banks[t]][:, :], ACT.Copy), tok, MN)
                free[banks[t]] = [mv_tok]
        mem_pe = tok
        flush()
        d3, yb_pe = gated("w_attn_proj", 2, TH[1], TL[1], w1["o"], GB, gb_tok, into=GA)
        m_tok = turn_over(v3(GA, 2, 1024), range(8), None, 0, d3, mem_pe, scale=0.5)
        x1, pe, ss = residual("w_out", TH[0], TL[0], m_tok, x_tok, w1["pt"])

        hm = norm(v3(X, 2, D), D, "g_mlp", 0, x1, pe, ss=ss)
        hid = {}

        def mlp_down(b):
            for r in range(2):
                hi, lo, rdy = take(("w_down", b, r))
                for t in range(2):
                    for h in range(2):
                        bank = 2 * t + h
                        for k in range(2):
                            kk = 4 * (b % 2) + 2 * r + k
                            c = slice(kk * 256 + t * 128, kk * 256 + t * 128 + 128)
                            tok = mm3(PB[bank][:, :], TH[1][:, c], TL[1][:, c], hi[:, k, 512 * h:512 * h + 512],
                                      lo[:, k, 512 * h:512 * h + 512], b == 0 and r == 0 and k == 0,
                                      b == 7 and r == 1 and k == 1, (rdy, hid[b], free[bank]), k == 1)
                give(("w_down", b, r), tok)
            hid["used", b] = tok

        P = v3(GB, 2, 256)
        p_tok = Q.dma("act", "p", lambda e: e.dma_start(P, A["p"][0, 0].rearrange("(t p) d -> p t d", p=128)), d3)
        for b in range(9):
            if b < 8:
                banks, tok = features_by(("w_up", b), 2, TH[0], TL[0], hm)
                hid[b] = []
                for h in range(2):
                    c0 = 4 * (b % 2) + 2 * h
                    s = S1[:, c0 * 256:c0 * 256 + 512]
                    a = do("act", lambda e, s=s, i=PB[banks[h]][:, :]: e.activation(s, i, ACT.Relu), tok, hid.get(b - 2), hm)
                    free[banks[h]] = [a]
                    p = do("dve", lambda e, s=s: e.tensor_tensor(s, s, s, ALU.mult), a)
                    hid[b] += split_t(s, 1, c0, 2, p, [hid.get(("used", b - 2)), pe])
            if b == 8:
                pt_tok = turn_over(P, range(2), None, 0, p_tok, tok, banks=pair())
            if b > 0:
                mlp_down(b - 1)
        up_pe = hid["used", 7]
        ss = small(4)
        for t in range(2):
            for h in range(2):
                o = v3(X, 2, 1024)[:, t, 512 * h:512 * h + 512]
                d = do("dve", lambda e: e.tensor_tensor(o, o, PB[2 * t + h][:, :], ALU.add), up_pe)
                free[2 * t + h] = [d]
                x2 = squared(ss, t, h, d)
        _, xd = root_mean(ss, D, DG, x2)

        EB = v3(RC, 2, 1024)
        for b in range(2):
            banks, tok = tokens_by(("w_ple_proj", b), 1, TH[0], TL[0], 0, pt_tok, 512)
            for t in range(2):
                e_tok = do("act", lambda e: e.activation(EB[:, t, 512 * b:512 * b + 512], PB[banks[t]][:, :], ACT.Copy),
                           tok, ya_pe)
                free[banks[t]] = [e_tok]
        ple_pe = tok
        xg = turn_over(v3(X, 2, D), range(8), "g_ple", 0, xd, ple_pe, DG)
        ss = small(4)
        GT = v3(GA, 2, 1024)
        for b in range(2):
            banks, tok = tokens_by(("w_ple_gate", b), 2, TH[0], TL[0], 0, xg, 512)
            for t in range(2):
                g = GT[:, t, 512 * b:512 * b + 512]
                ee = EB[:, t, 512 * b:512 * b + 512]
                xx = v3(X, 2, 1024)[:, t, 512 * b:512 * b + 512]
                a = do("act", lambda e, g=g, i=PB[banks[t]][:, :]: e.activation(g, i, ACT.Tanh, scale=0.5), tok, m_tok)
                free[banks[t]] = [a]
                d = do("dve", lambda e, g=g, ee=ee: e.scalar_tensor_tensor(g, g, 1.0, ee, ALU.add, ALU.mult), a, e_tok)
                d = do("dve", lambda e, g=g, xx=xx: e.scalar_tensor_tensor(xx, g, 0.5, xx, ALU.mult, ALU.add), d)
                x3 = squared(ss, t, b, d)
        gate_pe = tok

        h2 = norm(v3(X, 2, D), D, "mix_norm_g_2", 0, x3, gate_pe, ss=ss)
        QL = v3(RC, 2, 384)
        KL = v3(KT, 2, 288)
        banks, tok = tokens_by(("lat", 0), 2, TH[0], TL[0], 0, h2, 384)
        for t in range(2):
            ql_tok = do("act", lambda e, t=t, i=PB[banks[t]][:, 0:384]: e.activation(QL[:, t], i, ACT.Copy), tok, d)
            free[banks[t]] = [ql_tok]
        banks, tok = tokens_by(("lat", 1), 2, TH[0], TL[0], 0, h2, 288)
        for t in range(2):
            kl_tok = do("act", lambda e, t=t, i=PB[banks[t]][:, 0:288]: e.activation(KL[:, t], i, ACT.Copy), tok)
            free[banks[t]] = [kl_tok]
        U = v3(TMP, 4, 272)
        zt = do("pool", lambda e: e.memset(U[:, :, 0:16], 0.0), MN)
        banks, tok = features_by(("lat", 2), 2, TH[0], TL[0], h2)
        for h in range(2):
            u_tok = do("act", lambda e, h=h, i=v3(PB[banks[h]], 2, 256): e.activation(U[:, 2 * h:2 * h + 2, 16:272], i, ACT.Copy), tok,
                       rnn["end", 7])
            free[banks[h]] = [u_tok]
        pw_tok = Q.dma("act", "pool_w", lambda e: e.dma_start(v3(BD, 4, 128, 0), A["pool_w_2"][0].rearrange("g c e -> c g e")),
                       rnn["mm", 7])
        PW = v3(BD, 4, 128, 0)
        po = {"u": {}}
        W2 = [S0[:, 272 * i:272 * i + 272] for i in range(4)]

        def pool_group(g):
            def run():
                w = 2 << g
                src = U[:, g, :]
                d = None
                for j in range(g + 1):
                    dst = W2[j % 2]
                    s = 1 << j
                    d0 = do("dve", lambda e, dst=dst, src=src, s=s: e.tensor_copy(dst[:, 0:s], src[:, 0:s]), d, u_tok, zt, h2,
                            po.get(("d", g - 1)))
                    d = do("dve", lambda e, dst=dst, src=src, s=s: e.tensor_tensor(dst[:, s:272], src[:, s:272], src[:, 0:272 - s],
                                                                                 ALU.add), d0, d)
                    src = dst
                m = W2[2]
                a = do("dve", lambda e: e.tensor_tensor(m[:, 0:16], src[:, 16:32], cst("count", 16, 16 * g), ALU.mult), d)
                b = do("dve", lambda e: e.tensor_scalar(m[:, 16:256], src[:, 32:272], 1.0 / w, None, ALU.mult), d)
                d = do("dve", lambda e: e.tensor_tensor(po_d[:, g, :], m[:, 0:256], U[:, g, 16:272], ALU.subtract), a, b)
                po["d", g] = d
            return run

        po_d = v3(S0, 4, 256, 1024)

        def pool_mm():
            for g in range(4):
                m = do("pe", lambda e: e.matmul(PB[g][:, 0:256], PW[:, g, :], po_d[:, g, :], start=True, stop=True,
                                                skip_group_check=True), po["d", g], pw_tok, free[g])
                free[g] = po["u"][g] = split_psum(PB[g][:, 0:256], 1, g, col("pool_scale_2", g), m, up_pe)

        pos_i = SM[:, small_at[0]:small_at[0] + 2].bitcast(I32)
        small(2)
        posf, ang, kk_, cs = small(2), small(32), small(32), small(64)
        for t in range(2):
            pos_tok = Q.dma("act", "pos", lambda e, t=t: e.dma_start(
                pos_i[:, t:t + 1], A["positions_2"][0, 128 * t:128 * t + 128].rearrange("(p o) -> p o", o=1)))
        C1, C2 = 6.28125, 0.0019350051879882812
        C3 = TWO_PI - C1 - C2

        def angles():
            d = do("dve", lambda e: e.tensor_copy(posf, pos_i), pos_tok)
            for t in range(2):
                d2 = do("dve", lambda e, t=t: e.tensor_scalar(ang[:, 16 * t:16 * t + 16], cst("inv", 16), posf[:, t:t + 1], None, ALU.mult),
                        d, const_tok)
            for j, ph in enumerate((0.25, 0.0)):
                o = cs[:, 32 * j:32 * j + 32]
                d = do("dve", lambda e, ph=ph: e.tensor_scalar(kk_, ang, 1.0 / TWO_PI, ph, ALU.mult, ALU.add), d2, d)
                d = do("dve", lambda e: e.tensor_scalar(kk_, kk_, 12582912.0, None, ALU.add), d)
                d = do("dve", lambda e: e.tensor_scalar(kk_, kk_, -12582912.0, None, ALU.add), d)
                d = do("dve", lambda e, o=o: e.scalar_tensor_tensor(o, kk_, -C1, ang, ALU.mult, ALU.add), d)
                d = do("dve", lambda e, o=o: e.scalar_tensor_tensor(o, kk_, -C2, o, ALU.mult, ALU.add), d)
                d = do("dve", lambda e, o=o: e.scalar_tensor_tensor(o, kk_, -C3, o, ALU.mult, ALU.add), d)
                if j == 0:
                    d = do("dve", lambda e, o=o: e.tensor_scalar(o, o, TWO_PI / 4, None, ALU.add), d)
                d = do("dve", lambda e, o=o: e.tensor_scalar(o, o, 3.1415925, -3.1415925, ALU.min, ALU.max), d)
            po["cs"] = do("act", lambda e: e.activation(cs, cs, ACT.Sin), d)

        gt2 = [None, None]

        def gates2(b, steps):
            banks, tok = tokens_by(("gates2", b), 2, TH[0], TL[0], 0, h2, 512, steps)
            for t in range(2):
                o = v3((GA, GB)[b // 2], 2, 1024)[:, t, 512 * (b % 2):512 * (b % 2) + 512]
                gt2[b // 2] = do("act", lambda e: e.activation(o, PB[banks[t]][:, :], ACT.Tanh, scale=0.5), tok, x3)
                free[banks[t]] = [gt2[b // 2]]

        la = {}
        DQ, DK = KW[:, 0:256], KW[:, 256:512]
        kvn_src = KL[:, :, 0:256]
        kr = small(64)

        def latent_stats():
            la["kr"] = do("dve", lambda e: e.tensor_copy(v3(kr, 2, 32), KL[:, :, 256:288]), kl_tok)
            sq, a = squares(QL, 384, S1, ql_tok, hid[7])
            sk, a2 = squares(kvn_src, 256, S1, kl_tok, hid[7])
            la["q"] = root_mean(sq, 384, DQ, a)[1]
            la["k"] = root_mean(sk, 256, DK, a2)[1]

        def q_turn():
            la["qn"] = turn_over(QL, range(3), "q_norm_g_2", 1, la["q"], up_pe, DQ, c0=4, banks=(2, 3))

        def k_turn():
            la["kn"] = turn_over(kvn_src, range(2), "kv_norm_g_2", 1, la["k"], q_pe, DK, c0=4, banks=(2, 3))

        bg += [latent_stats, q_turn, lambda: (angles(), pool_group(0)()), pool_group(1), pool_group(2), pool_group(3), pool_mm]
        gates2(0, 1)
        QM = v3(RC, 2, 768)
        for b in range(2):
            banks, tok = tokens_by(("w_q_up_2", b), 1, TH[1], TL[1], 4, {k + 0: v for k, v in la["qn"].items()}, 384)
            for t in range(2):
                qm_tok = do("act", lambda e: e.activation(QM[:, t, 384 * b:384 * b + 384], PB[banks[t]][:, 0:384], ACT.Copy), tok)
                free[banks[t]] = [qm_tok]
        q_pe = tok
        bg.insert(0, k_turn)
        gates2(1, 2)
        flush()
        KC = S0[:, 0:1536].rearrange("p (t h n) -> p t h n", t=2, h=8)
        VM = RD[:, :].rearrange("p (t h n) -> p t h n", t=2, h=8)
        for b in range(2):
            banks, tok = tokens_by(("w_kv_up_2", b), 1, TH[1], TL[1], 4, la["kn"], 512)
            for t in range(2):
                i = PB[banks[t]][:, :].rearrange("p (h n) -> p h n", h=4)
                a1 = do("act", lambda e: e.activation(KC[:, t, 4 * b:4 * b + 4, 0:64], i[:, :, 0:64], ACT.Copy), tok, po["d", 3],
                        po["u"])
                a2 = do("act", lambda e: e.activation(VM[:, t, 4 * b:4 * b + 4, :], i[:, :, 64:128], ACT.Copy), tok)
                free[banks[t]] = [a2]
        kvm_tok = a2
        kv_pe = tok
        c4 = cs[:, 0:32].rearrange("p (t n) -> p t n", t=2)
        s4 = cs[:, 32:64].rearrange("p (t n) -> p t n", t=2)
        m0, m1, m2, m3 = [S1[:, 1024 + 128 * j:1152 + 128 * j].rearrange("p (h n) -> p h n", h=8) for j in range(4)]
        r2 = {}

        def rope2(t):
            q1 = QM[:, t].rearrange("p (h n) -> p h n", h=8)
            c8 = c4[:, t].unsqueeze(1).to_broadcast([128, 8, 16])
            s8 = s4[:, t].unsqueeze(1).to_broadcast([128, 8, 16])
            a_, b_ = q1[:, :, 64:80], q1[:, :, 80:96]
            d = r2.get(("k", 0))
            ds = [do("dve", lambda e, o=o, x=x, y=y: e.tensor_tensor(o, x, y, ALU.mult), qm_tok, po["cs"], la["q"], d)
                  for o, x, y in ((m0, a_, c8), (m1, b_, s8), (m2, b_, c8), (m3, a_, s8))]
            d = do("dve", lambda e: e.tensor_tensor(a_, m0, m1, ALU.subtract), ds[-1])
            r2["q", t] = d = do("dve", lambda e: e.tensor_tensor(b_, m2, m3, ALU.add), ds[-1])
            k1, k2 = kr[:, 32 * t:32 * t + 16], kr[:, 32 * t + 16:32 * t + 32]
            n = [S1[:, 1536 + 16 * j:1552 + 16 * j] for j in range(6)]
            ds = [do("dve", lambda e, o=o, x=x, y=y: e.tensor_tensor(o, x, y, ALU.mult), la["kr"], d)
                  for o, x, y in ((n[0], k1, c4[:, t]), (n[1], k2, s4[:, t]), (n[2], k2, c4[:, t]), (n[3], k1, s4[:, t]))]
            d = do("dve", lambda e: e.tensor_tensor(n[4], n[0], n[1], ALU.subtract), ds[-1])
            d = do("dve", lambda e: e.tensor_tensor(n[5], n[2], n[3], ALU.add), ds[-1])
            r2["k", t] = do("dve", lambda e: e.tensor_copy(KC[:, t, :, 64:96], S1[:, 1600:1632].unsqueeze(1).to_broadcast([128, 8, 32])),
                            d, po["d", 3], po["u"])

        def turn2(src, dst, ready):
            def run():
                for h in range(8):
                    bank = h // 2 % 4
                    for t in range(2):
                        o = PB[bank][0:96, 256 * (h % 2) + 128 * t:256 * (h % 2) + 128 * t + 128]
                        m = do("pe", lambda e: e.transpose(o, src(t, h), ident), ready(), free[bank])
                    if h % 2:
                        a = do("act", lambda e: e.activation(dst[0:96, 256 * (h - 1):256 * (h + 1)], PB[bank][0:96, :], ACT.Copy),
                               m, ready())
                        free[bank] = [a]
                r2[dst.name] = a
            return run

        turn_q = turn2(lambda t, h: QM[:, t, 96 * h:96 * h + 96], S1, lambda: [r2["k", 1], r2["q", 1]])
        turn_k = turn2(lambda t, h: KC[:, t, h, :], RC, lambda: [r2["k", 1], kvm_tok, r2["S1"]])

        SC2 = 1.0 / float(np.sqrt(96.0))

        def neg2(heads, mx, nm, tok):
            return do("dve", lambda e: e.tensor_scalar(nm, mx, -SC2, None, ALU.mult), tok, w2.get("rd"))

        w2 = {"area": KT, "mx": w1["mx"], "nm": w1["nm"], "dn": w1["dn"], "o": {}, "dst": kv_pe, "s1": la["kn"]}

        def group2(n):
            heads = [4 * n + i for i in range(4)]
            w2["s0"] = r2["RC"]
            return group("a2", heads, lambda h, t: S1[0:96, 256 * h + 128 * t:256 * h + 128 * t + 128],
                         lambda h, a, b: RC[0:96, 256 * h + a:256 * h + b], cst("mask2", 384), 96,
                         lambda h, t: SC2, [r2["S1"], r2["RC"]], neg2, lambda h, t: VM[:, t, h, :], 4, w2)

        bg += [lambda: rope2(0), lambda: rope2(1), turn_q, turn_k]
        for n in range(2):
            for s in range(4):
                bg.append(lambda n=n, s=s: group2(n)[s]())
        gates2(2, 2)
        gates2(3, 2)
        d, pb_pe = gated("w_pool_branch_2", 1, TH[1], TL[1], po["u"], GB, gt2[1], 2)
        flush()
        d3, at_pe = gated("w_attn_branch_2", 1, TH[1], TL[1], w2["o"], GA, gt2[0], k0=4, into=GB)
        m_tok = turn_over(v3(GB, 2, 1024), range(8), None, 1, d3, at_pe, scale=0.5)
        x4, mo_pe, ss = residual("w_mix_out_2", TH[1], TL[1], m_tok, None, w2["pt"])

        hx = norm(v3(X, 2, D), D, "xattn_norm_g_2", 0, x4, at_pe, ss=ss)
        for b in range(2):
            banks, tok = features_by(("w_xq_2", b), 2, TH[0], TL[0], hx)
            for h in range(2):
                c0 = 4 * b + 2 * h
                xq_tok = do("act", lambda e, c0=c0, i=PB[banks[h]][:, :]: e.activation(RC[:, c0 * 256:c0 * 256 + 512], i, ACT.Copy), tok)
                free[banks[h]] = [xq_tok]
        xq_pe = tok
        xa = {"o": {}}
        mx4, dn4 = small(8), small(8)
        for h in range(4):
            b = h % 2
            for t in range(2):
                for k in range(2):
                    c = (2 * h + k) * 256
                    m = do("pe", lambda e, b=b, t=t, k=k, c=c: e.matmul(
                        PB[b][:, 256 * t:256 * t + 256], RC[:, c + 128 * t:c + 128 * t + 128], RA[:, c:c + 256],
                        start=(t == 0 and k == 0), stop=(k == 1), skip_group_check=True), xq_tok, mk_tok, free[b])
            E = S0[:, 512 * (h % 2):512 * (h % 2) + 512]
            mm = mx4[:, 2 * h:2 * h + 2]
            dd = dn4[:, 2 * h:2 * h + 2]
            d = do("dve", lambda e, b=b, mm=mm: e.tensor_reduce(mm, v3(PB[b], 2, 256), AXX, ALU.max), m)
            d = do("dve", lambda e, mm=mm: e.tensor_scalar(mm, mm, -0.0625, None, ALU.mult), d)
            for t in range(2):
                a = do("act", lambda e, b=b, t=t, E=E, mm=mm, dd=dd: e.activation(
                    E[:, 256 * t:256 * t + 256], PB[b][:, 256 * t:256 * t + 256], ACT.Exp, bias=mm[:, t:t + 1], scale=0.0625,
                    accum_out=dd[:, t:t + 1]), d, xa.get(("p", h - 2)), hx)
            free[b] = [a]
            d = do("dve", lambda e, dd=dd: e.reciprocal(dd, dd), a)
            for t in range(2):
                d2 = do("dve", lambda e, t=t, E=E, dd=dd: e.tensor_scalar(E[:, 256 * t:256 * t + 256], E[:, 256 * t:256 * t + 256],
                                                                        dd[:, t:t + 1], None, ALU.mult), d)
            for mt in range(2):
                for t in range(2):
                    m = do("pe", lambda e, mt=mt, t=t, E=E: e.transpose(PB[2][:, 256 * mt + 128 * t:256 * mt + 128 * t + 128],
                                                                       E[:, 256 * t + 128 * mt:256 * t + 128 * mt + 128], ident),
                           d2, free[2])
            xa["p", h] = m
            PTm = S0[:, 1024 + 512 * (h % 2):1536 + 512 * (h % 2)]
            a = do("act", lambda e, PTm=PTm: e.activation(PTm, PB[2][:, :], ACT.Copy), m, xa.get(("v", h - 2)), hx)
            free[2] = [a]
            for dv in range(2):
                for mt in range(2):
                    c = 256 * h + 128 * dv
                    m = do("pe", lambda e, dv=dv, mt=mt, c=c, PTm=PTm: e.matmul(
                        PB[3][:, 256 * dv:256 * dv + 256], MV[:, mt, c:c + 128], PTm[:, 256 * mt:256 * mt + 256],
                        start=(dv == 0 and mt == 0), stop=(mt == 1), skip_group_check=True), a, mv_tok, free[3])
            xa["v", h] = m
            o = GB[:, 512 * h:512 * h + 512]
            a = do("act", lambda e, o=o: e.activation(o, PB[3][:, :], ACT.Copy), m, d3)
            free[3] = [a]
            xa["o"][2 * h] = xa["o"][2 * h + 1] = split_t(o, 1, 2 * h, 2, a, mo_pe)
        x5, xo_pe, ss = residual("w_xo_2", TH[1], TL[1], xa["o"], None, xa["p", 3])

        frs, xd = root_mean(ss, D, DG, x5)
        hf = turn_over(v3(X, 2, D), range(8), "ffn_norm_g_2", 0, xd, xq_pe, DG)
        banks = pair()
        hi, lo, rdy = take(("router", 0, 0))
        L = small(72)
        L3 = v3(L, 2, 36)
        for t in range(2):
            for k in range(8):
                c = slice(k * 256 + t * 128, k * 256 + t * 128 + 128)
                tok = mm3(PB[banks[t]][:, 0:36], TH[0][:, c], TL[0][:, c], hi[:, k, :], lo[:, k, :], k == 0, k == 7,
                          (rdy, hf[k], free[banks[t]]), k == 7)
            lt = do("dve", lambda e, t=t, b=banks[t]: e.tensor_tensor(L3[:, t], PB[b][:, 0:36], rb, ALU.add), tok, bc_tok)
            free[banks[t]] = [lt]
        give(("router", 0, 0), tok)

        at_ = [0]

        def rt(n):
            o = at_[0]
            at_[0] += n
            return KW[:, o:o + n]

        def b3(ap, n):
            return ap.unsqueeze(2).to_broadcast([128, 2, n])

        def first_max(src, n, dst, mxt, order, tok):
            v = v3(rt(2 * n), 2, n)
            d = do("dve", lambda e: e.tensor_reduce(mxt, src, AXX, ALU.max), tok)
            d = do("dve", lambda e: e.tensor_tensor(v, src, b3(mxt, n), ALU.is_equal), d)
            od = cst("order", n, order).unsqueeze(1).to_broadcast([128, 2, n])
            d = do("dve", lambda e: e.tensor_tensor(v, v, od, ALU.mult), d)
            q = rt(2)
            d = do("dve", lambda e: e.tensor_reduce(q, v, AXX, ALU.max), d)
            return do("dve", lambda e: e.tensor_tensor(dst, v, b3(q, n), ALU.is_equal), d)

        G = L3[:, :, 0:4]
        og = v3(rt(8), 2, 4)
        gm = rt(2)
        d = first_max(G, 4, og, gm, 0, lt)
        eg = v3(rt(8), 2, 4)
        d = do("dve", lambda e: e.tensor_tensor(eg, G, b3(gm, 4), ALU.subtract), d)
        a = do("act", lambda e: e.activation(eg, eg, ACT.Exp), d)
        pg = rt(2)
        d = do("dve", lambda e: e.tensor_reduce(pg, eg, AXX, ALU.add), a)
        d = do("dve", lambda e: e.reciprocal(pg, pg), d)
        se = rt(64)
        sel = v3(rt(16), 2, 8)
        for t in range(2):
            t4 = se[:, 32 * t:32 * t + 32].rearrange("p (g n) -> p g n", g=4)
            d = do("dve", lambda e, t=t, t4=t4: e.tensor_tensor(t4, L3[:, t, 4:36].rearrange("p (g n) -> p g n", g=4),
                                                              og[:, t].unsqueeze(2).to_broadcast([128, 4, 8]), ALU.mult), d)
            d = do("dve", lambda e, t=t: e.tensor_reduce(sel[:, t], se[:, 32 * t:32 * t + 32].rearrange("p (g n) -> p n g", g=4),
                                                         AXX, ALU.add), d)
        o1, o2 = v3(rt(16), 2, 8), v3(rt(16), 2, 8)
        ma, mb = rt(2), rt(2)
        d = first_max(sel, 8, o1, ma, 4, d)
        s2 = v3(rt(16), 2, 8)
        d = do("dve", lambda e: e.scalar_tensor_tensor(s2, o1, NEG, sel, ALU.mult, ALU.add), d)
        d = first_max(s2, 8, o2, mb, 4, d)
        e2 = rt(2)
        d = do("dve", lambda e: e.tensor_tensor(e2, mb, ma, ALU.subtract), d)
        a = do("act", lambda e: e.activation(e2, e2, ACT.Exp), d)
        mk = rt(64)
        oo = v3(rt(16), 2, 8)
        d = do("dve", lambda e: e.tensor_tensor(oo, o1, o2, ALU.add), d)
        for t in range(2):
            mk_t = do("dve", lambda e: e.tensor_tensor(mk[:, 32 * t:32 * t + 32].rearrange("p (g n) -> p g n", g=4),
                                                       og[:, t].unsqueeze(2).to_broadcast([128, 4, 8]),
                                                       oo[:, t].unsqueeze(1).to_broadcast([128, 4, 8]), ALU.mult), d)
        U_, ONE = cst("upper", 128), cst("ones", 128)
        mk0, mk1 = mk[:, 0:32], mk[:, 32:64]
        for o, l, r, go, end in ((0, U_, mk0, True, True), (32, U_, mk1, False, False), (32, ONE, mk0, False, True),
                                 (64, ONE, mk0, False, False), (64, ONE, mk1, False, True)):
            rk_pe = do("pe", lambda e: e.matmul(PB[1][:, o:o + 32], l, r, start=go, stop=end, skip_group_check=True),
                       mk_t, free[1])
        rank = rt(64)
        most, flag = rt(1), rt(1).bitcast(I32)
        k = do("dve", lambda e: e.tensor_reduce(most, PB[1][:, 64:96], AXX, ALU.max), rk_pe)
        flag_tok = do("dve", lambda e: e.tensor_copy(flag, most), k)
        k = do("dve", lambda e: e.scalar_tensor_tensor(rank, PB[1][:, 0:64], 1.0, mk, ALU.add, ALU.mult), k)
        free[1] = [k]
        rank_tok = do("dve", lambda e: e.tensor_scalar(rank, rank, -1.0, None, ALU.add), k)
        d = rank_tok
        wa, wb = rt(2), rt(2)
        d = do("dve", lambda e: e.tensor_scalar(wa, e2, 1.0, None, ALU.add), a)
        d = do("dve", lambda e: e.reciprocal(wa, wa), d)
        d = do("dve", lambda e: e.scalar_tensor_tensor(wa, wa, 0.5, pg, ALU.mult, ALU.mult), d)
        d = do("dve", lambda e: e.tensor_tensor(wb, wa, e2, ALU.mult), d)
        d = do("dve", lambda e: e.tensor_tensor(o1, o1, b3(wa, 8), ALU.mult), d)
        d = do("dve", lambda e: e.tensor_tensor(o2, o2, b3(wb, 8), ALU.mult), d)
        d = do("dve", lambda e: e.tensor_tensor(o1, o1, o2, ALU.add), d)
        cw = se
        for t in range(2):
            d = do("dve", lambda e, t=t: e.tensor_tensor(cw[:, 32 * t:32 * t + 32].rearrange("p (g n) -> p g n", g=4),
                                                         og[:, t].unsqueeze(2).to_broadcast([128, 4, 8]),
                                                         o1[:, t].unsqueeze(1).to_broadcast([128, 4, 8]), ALU.mult), d)
        cw_tok = d
        early.close()
        xat = {h: xa["v", h] for h in range(4)}
        Xv = v3(X, 2, 1024)

        def finish(acc_tok, FG, fing, after):
            for t in range(2):
                for h in range(2):
                    o = Xv[:, t, 512 * h:512 * h + 512]
                    x6 = do("dve", lambda e: e.tensor_tensor(o, o, PB[2 * t + h][:, :], ALU.add), acc_tok)
            fs, fr = NR[:, 92:94], NR[:, 94:96]
            for t in range(2):
                a = do("act", lambda e: e.activation(v3(S0, 2, 1024)[:, t], Xv[:, t], ACT.Square, accum_out=fs[:, t:t + 1]),
                       x6, after)
            r = rsqrt_mean(fr, fs, D, (a,))
            for t in range(2):
                d = do("dve", lambda e: e.scalar_tensor_tensor(v3(S1, 2, 1024)[:, t], Xv[:, t], fr[:, t:t + 1], FG[:, 0:1024],
                                                               ALU.mult, ALU.mult), r, fing, after)
                o_ = Q.dma("sp", "out", lambda e: e.dma_start(out[0, 128 * t:128 * t + 128, :], v3(S1, 2, 1024)[:, t]), d)
            Q.wait("sp", (o_,))

        def dense(late):
            CB = [S0, S1, sbe("CB0", 2048, F, late), sbe("CB1", 2048, F, late)]
            FG = sbe("FGd", 1024, F, late)
            GS = sbe("GSd", 1024, F, late)
            CW = sbe("CWd", 256, F, late)
            for t in range(2):
                m = do("pe", lambda e: e.transpose(PB[0][0:32, 128 * t:128 * t + 128], cw[:, 32 * t:32 * t + 32], ident),
                       cw_tok, free[0])
            cwT = CW[0:32, :]
            a = do("act", lambda e: e.activation(cwT, PB[0][0:32, 0:256], ACT.Copy), m, hf)
            free[0] = [a]
            cwb = {}
            for e_ in range(0, NE, 2):
                b = (e_ // 2) % 4
                for j in range(2):
                    m = do("pe", lambda e: e.matmul(PB[b][:, 256 * j:256 * j + 256],
                                                    ident[0:32, e_ + j:e_ + j + 1].to_broadcast([32, 128]), cwT,
                                                    start=True, stop=True, skip_group_check=True), a, free[b])
                o = CB[e_ // 8][:, 256 * (e_ % 8):256 * (e_ % 8) + 512]
                if e_ % 4:
                    k = do("act", lambda e: e.activation(o, PB[b][:, :], ACT.Copy), m, hf)
                else:
                    k = do("dve", lambda e: e.tensor_copy(o, PB[b][:, :]), m, hf)
                free[b] = [k]
                cwb[e_] = cwb[e_ + 1] = k
            fing = Q.dma("act", "fing", lambda e: e.dma_start(FG[:, :], A["final_norm_g_2"].partition_broadcast(128)), hf)
            ex = {}

            def moe_down(e_):
                hi, lo, rdy = take(("moe_out", e_, 0))
                for t in range(2):
                    for h in range(2):
                        bank = 2 * t + h
                        for k in range(2):
                            kk = 2 * (e_ % 4) + k
                            c = slice(kk * 256 + t * 128, kk * 256 + t * 128 + 128)
                            tok = mm3(PB[bank][:, :], TH[1][:, c], TL[1][:, c], hi[:, k, 512 * h:512 * h + 512],
                                      lo[:, k, 512 * h:512 * h + 512], e_ == 0 and k == 0, e_ == NE - 1 and k == 1,
                                      (rdy, ex[e_], free[bank]), k == 1)
                give(("moe_out", e_, 0), tok)
                ex["used", e_] = tok

            for p in range(NE // 2 + 1):
                for e_ in (2 * p, 2 * p + 1):
                    if p == NE // 2:
                        break
                    banks, tok = features_by(("moe_in", e_), 2, TH[0], TL[0], hf)
                    s = GS[:, 512 * (e_ % 2):512 * (e_ % 2) + 512]
                    a = do("act", lambda e: e.activation(s, PB[banks[0]][:, :], ACT.Tanh, scale=0.5), tok, hf, ex.get(e_ - 2))
                    d = do("dve", lambda e: e.scalar_tensor_tensor(s, s, 1.0, PB[banks[0]][:, :], ALU.add, ALU.mult), a)
                    free[banks[0]] = [d]
                    d = do("dve", lambda e: e.tensor_tensor(s, s, PB[banks[1]][:, :], ALU.mult), d)
                    free[banks[1]] = [d]
                    cb = CB[e_ // 8][:, 256 * (e_ % 8):256 * (e_ % 8) + 256].unsqueeze(1).to_broadcast([128, 2, 256])
                    q = do("pool", lambda e: e.tensor_tensor(v3(s, 2, 256), v3(s, 2, 256), cb, ALU.mult), d, cwb[e_])
                    ex[e_] = split_t(s, 1, 2 * (e_ % 4), 2, q, [ex.get(("used", e_ - 4)), xo_pe])
                if p > 0:
                    moe_down(2 * p - 2)
                    moe_down(2 * p - 1)
            finish(ex["used", NE - 1], FG, fing, ex[NE - 1])

        def sparse(late):
            XN = [sbe("XNH", 2048, R, late), sbe("XNL", 2048, R, late)]
            XG = [[TH[0], TL[0]], [sbe("XGH", 1536, R, late), sbe("XGL", 1536, R, late)]]
            XG = [[x[:, 0:1536] for x in y] for y in XG]
            YY = [[TH[1][:, 1024:2048], TL[1][:, 1024:2048]], [x[:, :] for x in (sbe("YH", 1024, R, late), sbe("YL", 1024, R, late))]]
            HT = [[x[:, 384 * b:384 * b + 384] for x in (TH[1], TL[1])] for b in range(2)]
            SEL = [sbe(f"SEL{i}", 256, R, late) for i in range(2)]
            SET = [sbe(f"SET{i}", 256, R, late) for i in range(4)]
            FG = sbe("FG", 1024, F, late)
            FB = sbe("FB", 1024, F, late)
            CS = sbe("CS", 2, F, late)
            fing = Q.dma("act", "fing", lambda e: e.dma_start(FG[:, :], A["final_norm_g_2"].partition_broadcast(128)), hf)
            fb = Q.dma("act", "fb", lambda e: e.dma_start(FB[:, :], A["ffn_norm_g_2"][0].partition_broadcast(128)), hf)
            sel, st_, xg, gu, hd, yy, used = {}, {}, {}, {}, {}, {}, {}
            for t in range(2):
                d = do("dve", lambda e: e.scalar_tensor_tensor(v3(S1, 2, 1024)[:, t], Xv[:, t], frs[:, t:t + 1], FB[:, :], ALU.mult,
                                                               ALU.mult), fb, hf)
            xa_ = do("act", lambda e: e.activation(XN[0][:, :], S1[:, :], ACT.Copy), d, hf)
            xn = do("dve", lambda e: e.tensor_tensor(XN[1][:, :], S1[:, :], XN[0][:, :].bitcast(F), ALU.subtract), xa_)
            zs = []
            for b in range(2):
                for x in XG[b]:
                    zs.append(do("pool", lambda e: e.memset(v3(x, 8, 192)[:, :, 64:128].bitcast(F), 0.0), used_done[st["used"] - 1], hf))
                for x in HT[b]:
                    zs.append(do("pool", lambda e: e.memset(v3(x, 2, 192)[:, :, 64:128].bitcast(F), 0.0), hf, xo_pe))

            def choose(p):
                s = v3(SEL[p % 2], 2, 128)
                for t in range(2):
                    for j in range(2):
                        c = 32 * t + 2 * p + j
                        sel[p] = do("pool", lambda e: e.tensor_scalar(s[:, t, 64 * j:64 * j + 64], cst("slots", 64), rank[:, c:c + 1],
                                                                      None, ALU.is_equal),
                                    rank_tok, hf, used.get(("sel", p - 2)))
                sf = s.bitcast(F)
                for t in range(2):
                    do("pe", lambda e: e.transpose(PB[5][:, 128 * t:128 * t + 128], sf[:, t], ident), sel[p], free[5], silent=True)
                for t in range(2):
                    m = do("pe", lambda e: e.matmul(PB[5][:, 256:258], sf[:, t], cw[:, 32 * t + 2 * p:32 * t + 2 * p + 2],
                                                    start=(t == 0), stop=(t == 1), skip_group_check=True), cw_tok)
                a = do("act", lambda e: e.activation(SET[p % 4][:, :], PB[5][:, 0:256], ACT.Copy), m, used.get(("set", p - 4)))
                do("act", lambda e: e.activation(CS[0:64, p % 2:p % 2 + 1], PB[5][0:64, 256:257], ACT.Copy), gu.get(("w", p - 2)),
                   silent=True)
                b = do("act", lambda e: e.activation(CS[64:128, p % 2:p % 2 + 1], PB[5][64:128, 257:258], ACT.Copy))
                free[5] = [b]
                st_[p] = [a, b]

            def gather(p):
                s = v3(SEL[p % 2], 2, 128)
                toks = []
                for b in range(2):
                    for k in range(4):
                        for t in range(2):
                            for i in range(2):
                                l = XN[i][:, 1024 * t + 128 * (4 * b + k):1024 * t + 128 * (4 * b + k) + 128]
                                m = do("pe", lambda e: e.matmul(PB[6 + b][:, 128 * k:128 * k + 128], l, s[:, t],
                                                                start=(k == 0 and t == 0 and i == 0), stop=(t == 1 and i == 1),
                                                                skip_group_check=True),
                                       sel[p], xa_, xn, free[6 + b], silent=not (k == 3 and t == 1 and i == 1))
                    hi, lo = [x.rearrange("p (k h c) -> p k h c", k=8, h=3)[:, 4 * b:4 * b + 4, 0:3:2, :] for x in XG[p % 2]]
                    src = PB[6 + b][:, :].rearrange("p (k h c) -> p k h c", k=4, h=2)
                    a = do("act", lambda e: e.activation(hi, src, ACT.Copy), m, zs, used.get(("xg", p - 2)))
                    d = do("dve", lambda e: e.tensor_tensor(lo, src, hi.bitcast(F), ALU.subtract), a)
                    free[6 + b] = [d]
                    toks += [a, d]
                used["sel", p] = m
                xg[p] = toks

            def rise(p):
                for j in range(2):
                    for r in range(2):
                        hi, lo, rdy = take(("moe_in", 2 * p + j, r))
                        for k in range(4):
                            c = slice(192 * (4 * r + k) + 64 * j, 192 * (4 * r + k) + 64 * j + 128)
                            tok = mm3(PB[4][:, :], XG[p % 2][0][:, c], XG[p % 2][1][:, c], hi[:, k, :], lo[:, k, :],
                                      j == 0 and r == 0 and k == 0, j == 1 and r == 1 and k == 3, (rdy, xg[p], free[4]), k == 3)
                        give(("moe_in", 2 * p + j, r), tok)
                used["xg", p] = tok
                s = S0[:, 256 * (p % 2):256 * (p % 2) + 256]
                a = do("act", lambda e: e.activation(s, PB[4][:, 0:256], ACT.Tanh, scale=0.5), tok, d, hd.get(("in", p - 2)))
                q = do("dve", lambda e: e.scalar_tensor_tensor(s, s, 1.0, PB[4][:, 0:256], ALU.add, ALU.mult), a)
                q = do("dve", lambda e: e.scalar_tensor_tensor(s, s, CS[:, p % 2:p % 2 + 1], PB[4][:, 256:512], ALU.mult, ALU.mult),
                       q, st_[p])
                gu["w", p] = q
                free[4] = [q]

            def over(p):
                s = S0[:, 256 * (p % 2):256 * (p % 2) + 256]
                for f in range(2):
                    m = do("pe", lambda e: e.transpose(PB[5][:, 128 * f:128 * f + 128], s[:, 128 * f:128 * f + 128], ident),
                           gu["w", p], free[5])
                hd["in", p] = m
                hi, lo = [x.rearrange("p (k h c) -> p k h c", k=2, h=3)[:, :, 0:3:2, :] for x in HT[p % 2]]
                src = PB[5][:, 0:256].rearrange("p (k h c) -> p k h c", k=2, h=2)
                a = do("act", lambda e: e.activation(hi, src, ACT.Copy), m, zs, used.get(("ht", p - 2)))
                q = do("dve", lambda e: e.tensor_tensor(lo, src, hi.bitcast(F), ALU.subtract), a)
                free[5] = [q]
                hd[p] = [a, q]

            def down(p):
                for j in range(2):
                    hi, lo, rdy = take(("moe_out", 2 * p + j, 0))
                    for h in range(2):
                        for k in range(2):
                            c = slice(192 * k + 64 * j, 192 * k + 64 * j + 128)
                            tok = mm3(PB[6 + h][:, :], HT[p % 2][0][:, c], HT[p % 2][1][:, c], hi[:, k, 512 * h:512 * h + 512],
                                      lo[:, k, 512 * h:512 * h + 512], j == 0 and k == 0, j == 1 and k == 1,
                                      (rdy, hd[p], free[6 + h]), k == 1)
                        yy["pe", h] = tok
                    give(("moe_out", 2 * p + j, 0), tok)
                used["ht", p] = tok
                yy[p] = []
                for h in range(2):
                    hi, lo = [x[:, 512 * h:512 * h + 512] for x in YY[p % 2]]
                    a = do("act", lambda e: e.activation(hi, PB[6 + h][:, :], ACT.Copy), yy["pe", h], used.get(("y", p - 2)))
                    q = do("dve", lambda e: e.tensor_tensor(lo, PB[6 + h][:, :], hi.bitcast(F), ALU.subtract), a)
                    free[6 + h] = [q]
                    yy[p] += [a, q]

            def spread(p):
                for t in range(2):
                    for h in range(2):
                        for i in range(2):
                            m = do("pe", lambda e: e.matmul(PB[2 * t + h][:, :], SET[p % 4][:, 128 * t:128 * t + 128],
                                                            YY[p % 2][i][:, 512 * h:512 * h + 512], start=(p == 0 and i == 0),
                                                            stop=(p == NE // 2 - 1 and i == 1), skip_group_check=True),
                                   yy[p], st_[p], free[2 * t + h], silent=not (t == 1 and h == 1 and i == 1))
                used["y", p] = used["set", p] = m
                return m

            NP = NE // 2
            choose(0)
            gather(0)
            for p in range(NP + 2):
                if p + 1 < NP:
                    choose(p + 1)
                    gather(p + 1)
                if p < NP:
                    rise(p)
                if 1 <= p <= NP:
                    down(p - 1)
                if 2 <= p:
                    m = spread(p - 2)
                if p < NP:
                    over(p)
            finish(m, FG, fing, [yy[NP - 1], d])

        for name in Q.engines:
            Q.wait(name, (flag_tok,))
        largest = nc.values_load(flag[0:1, 0:1], min_val=0, max_val=2 * S)

        def state():
            return ({k: v for k, v in Q.count.items()}, {k: dict(v) for k, v in Q.seen.items()}, dict(st), turn[0],
                    dict(raw_ready), dict(split_done), dict(used_done), dict(free))

        def restore(s):
            Q.count.update(s[0])
            for k in Q.seen:
                Q.seen[k] = dict(s[1][k])
            st.update(s[2])
            turn[0] = s[3]
            for now, then in zip((raw_ready, split_done, used_done, free), s[4:]):
                now.clear()
                now.update(then)

        before = state()
        with nc.If(largest < 65):
            with ExitStack() as late:
                (sparse if WAY == 0 else dense)(late)
        restore(before)
        with nc.Else():
            with ExitStack() as late:
                (dense if WAY == 0 else sparse)(late)


def kernel(**inputs):
    import concourse.bacc as _bacc
    from concourse.bass_utils import run_bass_kernel_spmd as _run

    nc = _bacc.Bacc("TRN2", target_bir_lowering=False, num_devices=1)
    arrays, aps = {}, {}
    for name, a in {**inputs, "const": constants()}.items():
        a = np.ascontiguousarray(a)
        arrays[f"in_{name}"] = a
        aps[name] = nc.dram_tensor(f"in_{name}", a.shape, mybir.dt.from_np(a.dtype), kind="ExternalInput").ap()
    out = nc.dram_tensor("out_0", (1, S, D), F, kind="ExternalOutput").ap()
    build(nc, aps, out)
    r = _run(nc, [arrays], core_ids=[0])
    return r.results[0]["out_0"]
```

```python
from contextlib import ExitStack

import numpy as np

import concourse.bass as bass
from concourse import mybir

ALU = mybir.AluOpType
ACT = mybir.ActivationFunctionType
AXX = mybir.AxisListType.X
F = mybir.dt.float32
R = mybir.dt.float32r
I32 = mybir.dt.int32

S = 256
D = 1024
NRAW = 4
NW = 3
SLOT = 2048
EPS = 1e-6
NEG = -1e30
TWO_PI = 6.283185307179586
NE = 32

ROWS1 = [("g_mix", 8), ("conv_w", 32), ("conv_b", 8), ("b_rg", 8), ("b_ig", 8), ("lru_lambda", 8),
         ("g_mlp", 8), ("g_ple", 8), ("mix_norm_g_2", 8), ("xattn_norm_g_2", 8), ("mem_norm_g_2", 8)]
ROWS2 = [("q_norm_g_2", 3), ("kv_norm_g_2", 2), ("pool_scale_2", 4)]
CONSTS = [("ident", 128), ("mask1", 384), ("mask2", 384), ("rope", 128), ("inv", 16), ("order", 12),
          ("count", 64), ("slots", 64), ("upper", 128), ("ones", 128)]


def offsets(rows):
    out, at = {}, 0
    for name, n in rows:
        out[name] = at
        at += n
    return out, at


def constants():
    at, n = offsets(CONSTS)
    c = np.zeros((128, n), np.float32)
    c[:, at["ident"]:at["ident"] + 128] = np.eye(128, dtype=np.float32)
    q = np.arange(128)[:, None]
    k = np.arange(128)[None, :]
    m = at["mask1"]
    c[:, m:m + 128] = np.where(k <= q, 0.0, NEG)
    c[:, m + 128:m + 256] = np.where(k > q, 0.0, NEG)
    c[:, m + 256:m + 384] = np.where(k <= q, 0.0, NEG)
    m = at["mask2"]
    c[:, m:m + 128] = np.where(k // 64 <= q // 64, 0.0, NEG)
    c[:, m + 256:m + 384] = np.where(k // 64 <= q // 64, 0.0, NEG)
    inv = (np.float32(10000.0) ** (-np.arange(0, 64, 2, dtype=np.float32) / np.float32(64))).astype(np.float32)
    ang = (np.arange(S, dtype=np.float32)[:, None] * inv[None, :]).astype(np.float32)
    m = at["rope"]
    for t in range(2):
        c[:, m + 32 * t:m + 32 * t + 32] = np.cos(ang[128 * t:128 * t + 128])
        c[:, m + 64 + 32 * t:m + 96 + 32 * t] = np.sin(ang[128 * t:128 * t + 128])
    c[:, at["inv"]:at["inv"] + 16] = (
        np.float32(1.0) / (np.float32(10000.0) ** (np.arange(0, 32, 2, dtype=np.float32) / np.float32(32))))
    c[:, at["order"]:at["order"] + 4] = 4 - np.arange(4)
    c[:, at["order"] + 4:at["order"] + 12] = 8 - np.arange(8)
    for g, w in enumerate((2, 4, 8, 16)):
        c[:, at["count"] + 16 * g:at["count"] + 16 * g + 16] = 1.0 / np.minimum(np.arange(16) + 1, w)
    c[:, at["slots"]:at["slots"] + 64] = np.arange(64)
    c[:, at["upper"]:at["upper"] + 128] = q < k
    c[:, at["ones"]:at["ones"] + 128] = 1.0
    return c


def plan_units():
    u = []

    def mat(name, lead, k, cols, key=None):
        nk = k // 128
        for b, (c0, w) in enumerate(cols):
            for r in range(0, nk, 4):
                u.append(((key or name, b, r // 4), [(name, lead, r * 128, min(4, nk - r), c0, w, 0)]))

    mat("w_in", (0,), 1024, [(512 * b, 512) for b in (0, 1)], "x")
    mat("w_in", (0,), 1024, [(2048, 512), (2560, 512), (3072, 512)], "qkv")
    mat("w_in", (0,), 1024, [(1024, 512), (1536, 512)], "g")
    mat("w_in", (0,), 1024, [(3584 + 512 * b, 512) for b in range(4)], "gates")
    mat("w_rnn_proj", (0,), 1024, [(0, 512), (512, 512)])
    mat("w_xkv_2", (0,), 1024, [(512 * b, 512) for b in range(4)])
    mat("w_attn_proj", (0,), 1024, [(0, 512), (512, 512)])
    mat("w_out", (0,), 1024, [(0, 512), (512, 512)])
    for b in range(9):
        if b < 8:
            for r in range(2):
                u.append((("w_up", b, r), [("w_up", (0,), 512 * r, 4, 512 * b, 512, 0)]))
        if b > 0:
            for r in range(2):
                u.append((("w_down", b - 1, r), [("w_down", (0,), 512 * (b - 1) + 256 * r, 2, 0, 1024, 0)]))
    mat("w_ple_proj", (0,), 256, [(0, 512), (512, 512)])
    mat("w_ple_gate", (0,), 1024, [(0, 512), (512, 512)])
    mat("w_in_2", (0,), 1024, [(0, 384), (384, 288), (672, 512)], "lat")
    g2 = [(("gates2", b, r), [("w_in_2", (0,), 512 * r, 4, 1184 + 512 * b, 512, 0)]) for b in range(4) for r in range(2)]
    u += g2[0:2]
    mat("w_q_up_2", (0,), 384, [(0, 384), (384, 384)])
    u += g2[2:4]
    mat("w_kv_up_2", (0,), 256, [(0, 512), (512, 512)])
    u += g2[4:8]
    mat("w_pool_branch_2", (0,), 512, [(0, 512), (512, 512)])
    mat("w_attn_branch_2", (0,), 512, [(0, 512), (512, 512)])
    mat("w_mix_out_2", (0,), 1024, [(0, 512), (512, 512)])
    mat("w_xq_2", (0,), 1024, [(0, 512), (512, 512)])
    mat("w_xo_2", (0,), 1024, [(0, 512), (512, 512)])
    u.append((("router", 0, 0), [("w_router_group_2", (0,), 0, 8, 0, 4, 0), ("w_router_expert_2", (0,), 0, 8, 0, 32, 4)]))
    for p in range(NE // 2 + 1):
        if p < NE // 2:
            for r in range(4):
                u.append((("moe_in", p, r), [(n, 2 * p, r, 2, 0, 512, 1024 * g)
                                             for g, n in enumerate(("w_exp_gate_2", "w_exp_up_2"))]))
        if p > 0:
            for k in range(2):
                u.append((("moe_out", p - 1, k), [("w_exp_down_2", 2 * p - 2, k, 2, 0, 1024, 0)]))
    return u


def tokens(after):
    for t in after:
        if isinstance(t, dict):
            yield from tokens(t.values())
        elif isinstance(t, list):
            yield from tokens(t)
        elif t is not None:
            yield t


class Engines:

    def __init__(self, engines, sems):
        self.engines = engines
        self.sems = sems
        self.count = {k: 0 for k in sems}
        self.seen = {k: {} for k in engines}

    def wait(self, eng, after):
        need = {}
        for name, value in tokens(after):
            need[name] = max(need.get(name, 0), value)
        for name, value in need.items():
            if self.seen[eng].get(name, 0) < value:
                self.seen[eng][name] = value
                self.engines[eng].wait_ge(self.sems[name], value)

    def do(self, eng, fn, *after, silent=False):
        self.wait(eng, after)
        ins = fn(self.engines[eng])
        if silent:
            return None
        self.count[eng] += 1
        ins.then_inc(self.sems[eng], 1)
        return (eng, self.count[eng])

    def dma(self, eng, sem, fn, *after):
        self.wait(eng, after)
        self.count[sem] += 16
        fn(self.engines[eng]).then_inc(self.sems[sem], 16)
        return (sem, self.count[sem])


def build(nc, A, out):
    with ExitStack() as ctx:
        dma_sems = ([f"w{i}" for i in range(NRAW)] +
                    ["x", "rows", "rows2", "fg", "const", "bd", "bcast", "mem", "mem1", "pos", "fb", "pool_w", "p", "fing", "out", "out2"])
        sems = {k: ctx.enter_context(nc.semaphore(f"s_{k}")) for k in ["pe", "act", "dve", "pool"] + dma_sems}
        Q = Engines({"pe": nc.tensor, "act": nc.scalar, "dve": nc.vector, "pool": nc.gpsimd, "sp": nc.sync}, sems)
        do = Q.do

        def sb(name, n, dt=F):
            return ctx.enter_context(nc.sbuf_tensor(name, [128, n], dt))

        RAW = [sb(f"raw{i}", SLOT) for i in range(NRAW)]
        WH = [sb(f"wh{i}", SLOT, R) for i in range(NW)]
        WL = [sb(f"wl{i}", SLOT, R) for i in range(NW)]
        TH = [sb(f"th{i}", 2048, R) for i in range(2)]
        TL = [sb(f"tl{i}", 2048, R) for i in range(2)]
        X = sb("X", 2048)
        S0 = sb("S0", 2048)
        S1 = sb("S1", 2048)
        KW = sb("KW", 512)
        PC = sb("PC", 137)
        CAT, CN = offsets(CONSTS)
        CT = sb("CT", CN)
        NR = sb("NR", 128)
        SM = sb("SM", 768)
        early = ExitStack()

        def sbe(name, n, dt=F, stack=early):
            return stack.enter_context(nc.sbuf_tensor(name, [128, n], dt))

        GA = sbe("GA", 2048)
        GB = sbe("GB", 2048)
        RA = sbe("RA", 2080)
        RB = sbe("RB", 2048)
        RC = sbe("RC", 2048)
        RD = sbe("RD", 1024)
        KT = sbe("KT", 1024)
        BT = sbe("BT", 2304)
        BD = BT[:, 0:1024]
        TMP = BT[:, 1024:2304]
        PB = [ctx.enter_context(nc.psum_tensor(f"pb{i}", [128, 512], F)) for i in range(8)]

        def v3(t, a, n, off=0):
            return t[:, off:off + a * n].rearrange("p (a n) -> p a n", a=a)

        def cst(name, n=None, off=0):
            o = CAT[name] + off
            return CT[:, o:o + n]

        ident = cst("ident", 128)
        R1, _ = offsets(ROWS1)
        R2, _ = offsets(ROWS2)
        PCOL = {**R1, **{k: v + 120 for k, v in R2.items()}, "ffn_norm_g_2": 129}

        def col(name, c):
            o = PCOL[name] + c
            return PC[:, o:o + 1]

        small_at = [0]

        def small(n):
            o = small_at[0]
            small_at[0] += n
            assert small_at[0] <= 768, small_at
            return SM[:, o:o + n]

        free = {b: [] for b in range(8)}

        units = plan_units()
        index = {key: i for i, (key, _) in enumerate(units)}
        st = {"loaded": 0, "split": 0, "used": 0}
        raw_ready, split_done, used_done = {}, {}, {}

        def shape_of(i):
            _, parts = units[i]
            kc = parts[0][3]
            return kc, sum(p[5] for p in parts)

        def load(i):
            _, parts = units[i]
            kc, w = shape_of(i)
            dst = v3(RAW[i % NRAW], kc, w)
            after = split_done.get(i - NRAW, [])
            for (name, lead, r0, n, c0, cw, at) in parts:
                flat = RAW[i % NRAW]
                if name == "w_exp_down_2":
                    src = A[name][0, lead:lead + 2, 128 * r0:128 * r0 + 128, :].rearrange("e p n -> p e n")
                    d = v3(flat, 2, 1024)
                elif name.startswith("w_exp"):
                    src = A[name][0, lead:lead + 2].rearrange("e (p r k) n -> p r e (k n)", r=4, k=2)[:, r0]
                    d = v3(flat, 2, 512, at)
                elif name.startswith("w_router"):
                    src = A[name][0].rearrange("(p k) n -> p k n", k=8)
                    d = dst[:, :, at:at + cw]
                else:
                    src = A[name]
                    for j in lead:
                        src = src[j]
                    src = src[r0:r0 + n * 128, c0:c0 + cw].rearrange("(k p) n -> p k n", p=128)
                    d = dst[:, :, at:at + cw]
                tok = Q.dma("sp", f"w{i % NRAW}", lambda e: e.dma_start(d, src), after)
            raw_ready[i] = tok

        def split(i):
            kc, w = shape_of(i)
            n = kc * w
            raw, hi, lo = RAW[i % NRAW][:, 0:n], WH[i % NW][:, 0:n], WL[i % NW][:, 0:n]
            a = do("act", lambda e: e.activation(hi, raw, ACT.Copy), raw_ready[i], used_done.get(i - NW))
            m = n - (n // 3) // 4 * 4
            b = do("dve", lambda e: e.tensor_tensor(lo[:, 0:m], raw[:, 0:m], hi[:, 0:m].bitcast(F), ALU.subtract),
                   raw_ready[i], a, used_done.get(i - NW))
            c = do("pool", lambda e: e.tensor_tensor(lo[:, m:n], raw[:, m:n], hi[:, m:n].bitcast(F), ALU.subtract),
                   raw_ready[i], a, used_done.get(i - NW))
            split_done[i] = [a, b, c]

        def load_to(n):
            while st["loaded"] < min(n, len(units)):
                load(st["loaded"])
                st["loaded"] += 1

        def split_to(n):
            while st["split"] < min(n, len(units)):
                i = st["split"]
                load_to(i + 1)
                split(i)
                st["split"] += 1
                load_to(i + 1 + NRAW)

        def take(key):
            i = index[key]
            assert i == st["used"], (key, i, st)
            split_to(i + NW)
            kc, w = shape_of(i)
            return v3(WH[i % NW], kc, w), v3(WL[i % NW], kc, w), split_done[i]

        def give(key, tok):
            used_done[index[key]] = tok
            st["used"] += 1

        def mm3(o, lh, ll, rh, rl, start, stop, after, last):
            do("pe", lambda e: e.matmul(o, lh, rh, start=start, stop=False, skip_group_check=True), *after,
               silent=True)
            do("pe", lambda e: e.matmul(o, lh, rl, start=False, stop=False, skip_group_check=True), silent=True)
            return do("pe", lambda e: e.matmul(o, ll, rh, start=False, stop=stop, skip_group_check=True),
                      silent=not last)

        bg = []

        def step(n=1):
            for _ in range(n):
                if bg:
                    bg.pop(0)()

        def flush():
            while bg:
                bg.pop(0)()

        turn = [0]

        def pair():
            turn[0] ^= 1
            return (4, 5) if turn[0] else (6, 7)

        def part(ready, kk):
            return ready.get(kk) if isinstance(ready, dict) else ready

        def tokens_by(key, nu, th, tl, k0, ready, w, steps=1):
            banks = pair()
            for r in range(nu):
                hi, lo, rdy = take((*key, r))
                kc = shape_of(index[(*key, r)])[0]
                for t in range(2):
                    o = PB[banks[t]][:, 0:w]
                    for k in range(kc):
                        kk = k0 + 4 * r + k
                        c = slice(kk * 256 + t * 128, kk * 256 + t * 128 + 128)
                        tok = mm3(o, th[:, c], tl[:, c], hi[:, k, 0:w], lo[:, k, 0:w], r == 0 and k == 0,
                                  r == nu - 1 and k == kc - 1, (rdy, part(ready, kk), free[banks[t]]), k == kc - 1)
                give((*key, r), tok)
                step(steps)
            return banks, tok

        def features_by(key, nu, th, tl, ready, steps=1):
            banks = pair()
            for r in range(nu):
                hi, lo, rdy = take((*key, r))
                kc = shape_of(index[(*key, r)])[0]
                for c in range(4):
                    b = banks[c // 2]
                    o = PB[b][:, (c % 2) * 256:(c % 2) * 256 + 256]
                    for k in range(kc):
                        kk = 4 * r + k
                        x = slice(kk * 256, kk * 256 + 256)
                        cs = slice(c * 128, c * 128 + 128)
                        tok = mm3(o, hi[:, k, cs], lo[:, k, cs], th[:, x], tl[:, x], r == 0 and k == 0 and c % 2 == 0,
                                  r == nu - 1 and k == kc - 1, (rdy, part(ready, kk), free[b]), k == kc - 1)
                give((*key, r), tok)
                step(steps)
            return banks, tok

        def split_t(src, which, c0, n, after, reuse=None):
            hi = TH[which][:, c0 * 256:(c0 + n) * 256]
            lo = TL[which][:, c0 * 256:(c0 + n) * 256]
            a = do("act", lambda e: e.activation(hi, src, ACT.Copy), after, reuse)
            b = do("dve", lambda e: e.tensor_tensor(lo, src, hi.bitcast(F), ALU.subtract), after, a, reuse)
            return [a, b]

        def split_psum(src, which, c, scale, after, reuse):
            hi, lo = TH[which][:, 256 * c:256 * c + 256], TL[which][:, 256 * c:256 * c + 256]
            a = do("act", lambda e: e.activation(hi, src, ACT.Copy, scale=scale), after, pc_tok, reuse)
            b = do("dve", lambda e: e.scalar_tensor_tensor(lo, src, scale, hi.bitcast(F), ALU.mult, ALU.subtract), after, a, reuse)
            return [a, b]

        def turn_over(src, chunks, gain, which, ready, reuse, dg=None, scale=1.0, c0=0, banks=(0, 1, 2, 3), step=1):
            toks = {}
            for c in chunks:
                b = banks[c % len(banks)]
                for t in range(2):
                    o = PB[b][:, 128 * t:128 * t + 128]
                    x = src[:, t, 128 * c:128 * c + 128] if step == 1 else src[:, t, c:128 * step:step]
                    if dg is None:
                        m = do("pe", lambda e: e.transpose(o, x, ident), part(ready, c), free[b], c_tok)
                    else:
                        m = do("pe", lambda e: e.matmul(o, x, dg[:, 128 * t:128 * t + 128], start=True, stop=True,
                                                        skip_group_check=True), part(ready, c), free[b])
                g = col(gain, c) if gain else scale
                free[b] = toks[c0 + c] = split_psum(PB[b][:, 0:256], which, c0 + c, g, m, reuse)
                last["turn"] = m
            return toks

        last = {}

        def rsqrt_mean(dst, ss, n, after):
            w = dst.shape[-1]
            v, y, t = NR[:, 0:w], NR[:, 40:40 + w], NR[:, 80:80 + w]
            d = do("dve", lambda e: e.tensor_scalar(v, ss, 1.0 / n, EPS, ALU.mult, ALU.add), *after)
            d = do("dve", lambda e: e.tensor_scalar(t.bitcast(I32), v.bitcast(I32), 1, None, ALU.logical_shift_right), d)
            d = do("dve", lambda e: e.tensor_scalar(y.bitcast(I32), t.bitcast(I32), -1.0, float(0x5f3759df), ALU.mult, ALU.add), d)
            for i in range(3):
                o = dst if i == 2 else y
                d = do("dve", lambda e: e.tensor_tensor(t, y, y, ALU.mult), d)
                d = do("dve", lambda e: e.scalar_tensor_tensor(t, t, -0.5, v, ALU.mult, ALU.mult), d)
                d = do("dve", lambda e: e.scalar_tensor_tensor(o, t, 1.5, y, ALU.add, ALU.mult), d)
            return d

        def squares(src, w, junk, ready, after):
            ss = small(2)
            for t in range(2):
                a = do("act", lambda e: e.activation(junk[:, 0:w], src[:, t, :], ACT.Square, accum_out=ss[:, t:t + 1]), ready, after,
                       last.get("junk"))
                last["junk"] = a
            return ss, a

        def root_mean(ss, w, dg, after, free_dg=None):
            rs = small(2)
            if ss.shape[-1] == 4:
                s2 = small(2)
                s4 = ss.rearrange("p (t b) -> p t b", t=2)
                after = do("dve", lambda e: e.tensor_tensor(s2, s4[:, :, 0], s4[:, :, 1], ALU.add), after)
                ss = s2
            r = rsqrt_mean(rs, ss, w, (after,))
            for t in range(2):
                d = do("dve", lambda e: e.tensor_scalar(dg[:, 128 * t:128 * t + 128], ident, rs[:, t:t + 1], None, ALU.mult), r,
                       free_dg, last.get("turn"), c_tok)
            return rs, d

        DG = KW[:, 0:256]

        def norm(src, w, gain, which, ready, reuse, after=None, ss=None, c0=0):
            if ss is None:
                ss, ready = squares(src, w, S0, ready, after)
            _, d = root_mean(ss, w, DG, ready)
            return turn_over(src, range(w // 128), gain, which, d, reuse, DG, c0=c0)

        x_tok = Q.dma("sp", "x", lambda e: e.dma_start(v3(X, 2, D), A["x"][0].rearrange("(t p) d -> p t d", p=128)))
        const_tok = Q.dma("act", "const", lambda e: e.dma_start(CT[:, :], A["const"]))
        at = 0
        for name, n in ROWS1:
            src = A[name].rearrange("o (c p) -> (o c) p", p=128) if name != "conv_w" else \
                A[name][0].rearrange("j (c p) -> (j c) p", p=128)
            if at < 48:
                rows_tok = Q.dma("act", "rows", lambda e: e.dma_start(S0[at:at + n, 0:128], src))
            else:
                rows2_tok = Q.dma("sp", "rows2", lambda e: e.dma_start(S0[at:at + n, 0:128], src))
            at += n
        at = 0
        for name, n in ROWS2:
            src = A[name].rearrange("o (c p) -> (o c) p", p=128)
            rows_tok = Q.dma("act", "rows", lambda e: e.dma_start(S0[at:at + n, 128:256], src))
            at += n
        load_to(NRAW)
        BDv = [v3(BD, 8, 64, 512 * j) for j in range(2)]
        for j, name in enumerate(("w_rg", "w_ig")):
            w = A[name][0].rearrange("(c h) i j -> h i c j", h=2)
            for h in range(2):
                bd_tok = Q.dma("sp", "bd", lambda e, j=j, h=h, w=w: e.dma_start(BDv[j][64 * h:64 * h + 64, :, :], w[h]))
        gq = small(64)
        gk = small(64)
        snk = small(16)
        rb = small(36)
        for dst, src in ((gq, A["q_gain"][0]), (gk, A["k_gain"][0]), (snk, A["sinks"][0]),
                         (rb[:, 0:4], A["b_router_group_2"][0]), (rb[:, 4:36], A["b_router_expert_2"][0])):
            bc_tok = Q.dma("sp", "bcast", lambda e, d=dst, s=src: e.dma_start(d, s.partition_broadcast(128)))
        fg_tok = Q.dma("sp", "fg", lambda e: e.dma_start(PC[:, 129:137], A["ffn_norm_g_2"][0].rearrange("(p k) -> p k", k=8)))
        c_tok = const_tok
        ss, a = squares(v3(X, 2, D), D, S1, x_tok, None)
        _, xd = root_mean(ss, D, DG, a)
        mem1_tok = Q.dma("act", "mem1", lambda e: e.dma_start(v3(S1, 2, D), A["mem_2"][0].rearrange("(t p) d -> p t d", p=128)), a)
        pe1 = do("pe", lambda e: e.transpose(PB[0][:, 0:112], S0[0:112, 0:128], ident[0:112, 0:112]), rows_tok, rows2_tok, c_tok)
        pe2 = do("pe", lambda e: e.transpose(PB[0][:, 128:137], S0[0:9, 128:256], ident[0:9, 0:9]), pe1)
        a = do("act", lambda e: e.activation(PC[:, 0:112], PB[0][:, 0:112], ACT.Copy), pe2)
        pc_tok = do("act", lambda e: e.activation(PC[:, 120:129], PB[0][:, 128:137], ACT.Copy), pe2)
        free[0] = [pc_tok]
        split_to(2)

        lam = PC[:, PCOL["lru_lambda"]:PCOL["lru_lambda"] + 8]
        hb = small(16)
        sp4 = small(8)
        sp4n = small(8)
        l0, l1, l2, l3 = small(8), small(8), small(8), small(8)
        d = do("dve", lambda e: e.tensor_scalar(l0, lam, -1.0, None, ALU.mult), pc_tok)
        d = do("dve", lambda e: e.tensor_tensor(l0, l0, lam, ALU.max), d)
        a = do("act", lambda e: e.activation(l1, l0, ACT.Exp, scale=-1.0), d)
        d = do("dve", lambda e: e.tensor_scalar(l2, l1, 2.0, None, ALU.add), a)
        d = do("dve", lambda e: e.reciprocal(l2, l2), d)
        d = do("dve", lambda e: e.tensor_tensor(l1, l1, l2, ALU.mult), d)
        d = do("dve", lambda e: e.tensor_tensor(l2, l1, l1, ALU.mult), d)
        d = do("dve", lambda e: e.tensor_scalar(l3, l2, 1.0 / 15, None, ALU.mult), d)
        for n in (13, 11, 9, 7, 5, 3):
            d = do("dve", lambda e, n=n: e.scalar_tensor_tensor(l3, l3, 1.0 / n, l2, ALU.add, ALU.mult), d)
        d = do("dve", lambda e: e.scalar_tensor_tensor(l3, l3, 1.0, l1, ALU.add, ALU.mult), d)
        d = do("dve", lambda e: e.tensor_scalar(l0, lam, -1.0, 0.0, ALU.mult, ALU.max), d)
        d = do("dve", lambda e: e.scalar_tensor_tensor(l3, l3, 2.0, l0, ALU.mult, ALU.add), d)
        d = do("dve", lambda e: e.tensor_scalar(sp4, l3, 4.0, None, ALU.mult), d)
        d = do("dve", lambda e: e.tensor_scalar(sp4n, l3, -4.0, None, ALU.mult), d)
        sp_tok = do("dve", lambda e: e.tensor_scalar(hb, PC[:, PCOL["b_rg"]:PCOL["b_rg"] + 16], 0.5, None, ALU.mult), d)

        h_tok = turn_over(v3(X, 2, D), range(8), "g_mix", 0, xd, None, DG)
        XR = v3(RA, 8, 260)
        z = do("pool", lambda e: e.memset(XR[:, :, 0:3], 0.0))
        xr_tok = []
        for b in range(2):
            banks, tok = features_by(("x", b), 2, TH[0], TL[0], h_tok)
            for h in range(2):
                o = XR[:, 4 * b + 2 * h:4 * b + 2 * h + 2, 3:259]
                xr_tok = [do("act", lambda e, o=o, i=v3(PB[banks[h]], 2, 256): e.activation(o, i, ACT.Copy), tok)]
                free[banks[h]] = xr_tok

        rnn = {}
        XC = [TMP[:, 0:256], TMP[:, 256:512]]
        T2 = TMP[:, 768:1024]

        def rnn_conv(c):
            x = XR[:, c, :]
            xc = XC[c % 2]
            d = do("dve", lambda e: e.tensor_scalar(xc, x[:, 0:256], col("conv_w", c), col("conv_b", c), ALU.mult, ALU.add),
                   xr_tok, z, pc_tok, rnn.get(("mm", c - 2)), rnn.get(("u", c - 2)))
            for j in range(1, 4):
                d = do("dve", lambda e, j=j: e.scalar_tensor_tensor(xc, x[:, j:j + 256], col("conv_w", 8 * j + c), xc,
                                                                    ALU.mult, ALU.add), d)
            rnn["xc", c] = d

        def rnn_gates(c):
            b = c % 2
            xc = XC[c % 2]
            T1 = TMP[:, 512:768] if c % 2 else TMP[:, 1024:1280]
            for j in range(2):
                for h in range(2):
                    ps = slice(64 * h, 64 * h + 64)
                    m = do("pe", lambda e: e.matmul(PB[b][ps, 256 * j:256 * j + 256], BDv[j][ps, c, :], xc[ps, :],
                                                    start=True, stop=True, skip_group_check=True),
                           rnn["xc", c], bd_tok, free[b])
            rnn["mm", c] = m
            am, mm, u = S1[:, 256 * c:256 * c + 256], S0[:, 256 * c:256 * c + 256], XR[:, c, 0:256]
            a = do("act", lambda e: e.activation(T1, PB[b][:, 0:256], ACT.Tanh, bias=hb[:, c:c + 1], scale=0.5), m, sp_tok,
                   rnn.get(("m", c - 2)))
            a2 = do("act", lambda e: e.activation(T2, PB[b][:, 256:512], ACT.Tanh, bias=hb[:, 8 + c:9 + c], scale=0.5), m,
                    rnn.get(("u", c - 1)))
            free[b] = [a2]
            a3 = do("act", lambda e: e.activation(am, T1, ACT.Exp, bias=sp4n[:, c:c + 1], scale=sp4n[:, c:c + 1]), a, h_tok, ml["rs"])
            rnn["t", c] = do("act", lambda e: e.activation(T1, T1, ACT.Tanh, bias=sp4[:, c:c + 1], scale=sp4[:, c:c + 1]), a, a3)
            if c < 7:
                rnn_conv(c + 1)
            if c > 0:
                rnn_mult(c - 1)
            rnn["u", c] = do("dve", lambda e: e.scalar_tensor_tensor(u, T2, 1.0, xc, ALU.add, ALU.mult), a2, rnn["xc", c], m)
            rnn["q", c] = do("pool", lambda e: e.tensor_tensor(mm, am, am, ALU.mult), a3, h_tok)

        def rnn_mult(c):
            mm = S0[:, 256 * c:256 * c + 256]
            T1 = TMP[:, 512:768] if c % 2 else TMP[:, 1024:1280]
            m1 = do("dve", lambda e: e.scalar_tensor_tensor(mm, mm, 1.0, T1, ALU.add, ALU.mult), rnn["q", c], rnn["t", c])
            rnn["m", c] = do("dve", lambda e: e.tensor_scalar(mm, mm, 2.0 ** -100, None, ALU.max), m1)

        def rnn_root():
            rnn_mult(7)
            rnn["root"] = do("act", lambda e: e.activation(S0[:, :], S0[:, :], ACT.Sqrt), rnn["m", 7])

        def rnn_scan(c):
            am, mm, u = S1[:, 256 * c:256 * c + 256], S0[:, 256 * c:256 * c + 256], XR[:, c, 0:256]
            g = RB[:, 256 * c:256 * c + 256]
            T1, T3 = (TMP[:, 512:768], TMP[:, 768:1024]) if c % 2 else (TMP[:, 0:256], TMP[:, 256:512])
            a5 = do("act", lambda e: e.activation(T3, g, ACT.Square), rnn["g"], rnn["root"], rnn.get(("end", c - 2)))
            if c > 0:
                rnn_out(c - 1)
            p = do("dve", lambda e: e.tensor_scalar(T3, T3, 0.044715, 1.0, ALU.mult, ALU.add), a5)
            rnn["p", c] = do("pool", lambda e: e.tensor_tensor(T3, T3, g, ALU.mult), p)
            w = do("dve", lambda e: e.scalar_tensor_tensor(u, u, 0.5, mm, ALU.mult, ALU.mult), rnn["root"], rnn["u", c])
            rnn["s", c] = do("dve", lambda e: e.tensor_tensor_scan(T1, am, u, 0.0, ALU.mult, ALU.add), w, rnn.get(("end", c - 2)))

        def rnn_out(c):
            g = RB[:, 256 * c:256 * c + 256]
            T1, T3 = (TMP[:, 512:768], TMP[:, 768:1024]) if c % 2 else (TMP[:, 0:256], TMP[:, 256:512])
            a6 = do("act", lambda e: e.activation(T3, T3, ACT.Tanh, scale=0.7978845608028654), rnn["p", c])
            p = do("dve", lambda e: e.scalar_tensor_tensor(T3, T3, 1.0, g, ALU.add, ALU.mult), a6)
            p = do("dve", lambda e: e.scalar_tensor_tensor(g, T3, 0.5, T1, ALU.mult, ALU.mult), p, rnn["s", c])
            rnn["end", c] = p
            rnn["y", c] = split_t(g, 1, c, 1, p)

        ml = {}
        ss, a = squares(v3(S1, 2, D), D, S0, mem1_tok, [h_tok, pe2])
        mrs = small(2)
        ml["rs"] = [a, rsqrt_mean(mrs, ss, D, (a,))]
        rnn_conv(0)
        for c in range(8):
            bg.append(lambda c=c: rnn_gates(c))
        bg.append(rnn_root)
        QK = v3(RC, 2, 1024)
        KV = v3(RD, 2, 512)
        qk_tok = []
        for b in range(3):
            banks, tok = tokens_by(("qkv", b), 2, TH[0], TL[0], 0, h_tok, 512)
            for t in range(2):
                o = QK[:, t, 512 * b:512 * b + 512] if b < 2 else KV[:, t, :]
                qk_tok.append(do("act", lambda e, o=o, i=PB[banks[t]]: e.activation(o, i[:, :], ACT.Copy), tok))
                free[banks[t]] = [qk_tok[-1]]
        g_tok = []
        for b in range(2):
            banks, tok = features_by(("g", b), 2, TH[0], TL[0], h_tok)
            for h in range(2):
                o = RB[:, (4 * b + 2 * h) * 256:(4 * b + 2 * h + 2) * 256]
                g_tok = [do("act", lambda e, o=o, i=PB[banks[h]][:, :]: e.activation(o, i, ACT.Copy), tok)]
                free[banks[h]] = g_tok
        rnn["g"] = g_tok
        at1 = {}
        rqk, rq8 = small(40), small(32)
        rq, rk = rqk[:, 0:32], rqk[:, 32:40]
        TB = KW[:, 0:512].rearrange("p (f t n) -> p f t n", f=8, t=2)

        def prep_tables():
            cosv, sinv = v3(CT, 2, 32, CAT["rope"]), v3(CT, 2, 32, CAT["rope"] + 64)
            f = 0
            for g in (gq, gk):
                for tab, half in ((cosv, 0), (sinv, 1), (cosv, 1), (sinv, 0)):
                    gb = g[:, 32 * half:32 * half + 32].unsqueeze(1).to_broadcast([128, 2, 32])
                    d = do("dve", lambda e, f=f, tab=tab, gb=gb: e.tensor_tensor(TB[:, f], tab, gb, ALU.mult), bc_tok, const_tok, h_tok)
                    f += 1
            at1["tb"] = d

        def prep_sums():
            S0v = v3(S0, 2, 1024)
            a = do("act", lambda e: e.activation(GB[:, :], RC[:, :], ACT.Square), qk_tok)
            d = do("dve", lambda e: e.tensor_reduce(rqk[:, 0:32].rearrange("p (a n) -> p a n", a=32)[:, :, 0],
                                                    GB[:, :].rearrange("p (a n) -> p a n", n=64), AXX, ALU.add), a)
            K2 = GA[:, 0:512].rearrange("p (t n) -> p t n", t=2)
            a = do("act", lambda e: e.activation(K2, KV[:, :, 0:256], ACT.Square), qk_tok)
            d2 = do("dve", lambda e: e.tensor_reduce(rqk[:, 32:40], GA[:, 0:512].rearrange("p (a n) -> p a n", n=64), AXX, ALU.add), a)
            r2 = r = rsqrt_mean(rqk, rqk, 64, (d, d2))
            at1["rq"] = do("dve", lambda e: e.tensor_scalar(rq8, rq, 0.125, None, ALU.mult), r)
            kv4 = KV[:, :, 0:256].rearrange("p t (h n) -> p t h n", h=4)
            rkb = rk[:, :].rearrange("p (t h) -> p t h", t=2)
            for t in range(2):
                d = do("dve", lambda e, t=t: e.tensor_tensor(kv4[:, t], kv4[:, t], rkb[:, t].unsqueeze(2).to_broadcast([128, 4, 64]),
                                                             ALU.mult), r2, a)
            at1["k"] = d

        def rope(src, nh, f0, t, after, tmp):
            h = [src[:, :, 0:32], src[:, :, 32:64]]
            tb = [TB[:, f0 + i, t].unsqueeze(1).to_broadcast([128, nh, 32]) for i in range(4)]
            ds = [do(g, lambda e: e.tensor_tensor(tmp[i], h[j], tb[i], ALU.mult), *after)
                  for g, i, j in (("pool", 1, 1), ("dve", 0, 0), ("dve", 2, 1), ("pool", 3, 0))]
            a = do("dve", lambda e: e.tensor_tensor(h[0], tmp[0], tmp[1], ALU.subtract), ds)
            return [a, do("dve", lambda e: e.tensor_tensor(h[1], tmp[2], tmp[3], ALU.add), ds)]

        def prep_rope(t):
            tmp = [GB[:, 512 * i:512 * i + 512].rearrange("p (h n) -> p h n", h=16) for i in range(4)]
            at1["q", t] = rope(QK[:, t].rearrange("p (h n) -> p h n", h=16), 16, 0, t,
                               (at1["tb"], at1["rq"], at1["k"], at1.get(("q", 0))), tmp)

        KD = v3(S0, 2, 512, 1024)

        def prep_rope_k():
            for t in range(2):
                tmp = [GB[:, 128 * i:128 * i + 128].rearrange("p (h n) -> p h n", h=4) for i in range(4)]
                at1["kr", t] = rope(KV[:, t, 0:256].rearrange("p (h n) -> p h n", h=4), 4, 4, t,
                                    (at1["q", 1], at1.get(("kr", 0))), tmp)

        def prep_dup():
            for t in range(2):
                kd = KD[:, t].rearrange("p (h c n) -> p h c n", h=4, c=2)
                k4 = KV[:, t, 0:256].rearrange("p (h n) -> p h n", h=4).unsqueeze(2).to_broadcast([128, 4, 2, 64])
                at1["kd", t] = do("dve", lambda e: e.tensor_copy(kd, k4), at1["kr", t], rnn["end", 7])

        def prep_turn_k():
            for j in range(2):
                b = 2 + j
                for c in range(2):
                    for t in range(2):
                        m = do("pe", lambda e, c=c, t=t, j=j, b=b: e.transpose(
                            PB[b][:, c * 256 + t * 128:c * 256 + t * 128 + 128], KD[:, t, (2 * j + c) * 128:(2 * j + c) * 128 + 128],
                            ident), at1["kd", 1], free[b])
                a = do("act", lambda e, j=j, b=b: e.activation(KT[:, 512 * j:512 * j + 512], PB[b][:, :], ACT.Copy), m)
                free[b] = [a]
            at1["kT"] = a

        def prep_turn_q():
            for j in range(4):
                b = 2 + j % 2
                for c in range(2):
                    for t in range(2):
                        m = do("pe", lambda e: e.transpose(PB[b][:, c * 256 + t * 128:c * 256 + t * 128 + 128],
                                                           QK[:, t, (2 * j + c) * 128:(2 * j + c) * 128 + 128], ident),
                               at1["q", 1], free[b])
                a = do("act", lambda e: e.activation(S1[:, 512 * j:512 * j + 512], PB[b][:, :], ACT.Copy), m, rnn["end", 7])
                free[b] = [a]
            at1["qT"] = a

        def group(heads, lhs, rhs, mask, exp_scale, ready, negmax, vals, dst, w, sh):
            SS = w["ss"].rearrange("p (h n) -> p h n", h=4)
            mx = w["mx"]
            nm = w["nm"]
            dn = w["dn"]

            def scores():
                for i, h in enumerate(heads):
                    b = i % 2
                    do("pe", lambda e, h=h, b=b: e.matmul(PB[b][:, 0:128], lhs(h, 0), rhs(h, 0, 128), start=True, stop=True,
                                                          skip_group_check=True), ready, free[b], silent=True)
                    m = do("pe", lambda e, h=h, b=b: e.matmul(PB[b][:, 128:384], lhs(h, 1), rhs(h, 0, 256), start=False, stop=True,
                                                              skip_group_check=True))
                    d = do("dve", lambda e, i=i, b=b: e.tensor_tensor(SS[:, i], PB[b][:, 0:384], mask, ALU.add), m,
                           w.get("pt"), sh["s0"])
                    free[b] = [d]
                d1 = do("dve", lambda e: e.tensor_reduce(mx[:, 0:4], SS[:, :, 0:128], AXX, ALU.max), d)
                d2 = do("dve", lambda e: e.tensor_reduce(mx[:, 4:8], SS[:, :, 128:384], AXX, ALU.max), d)
                nd = negmax(heads, w, d2)
                for i, h in enumerate(heads):
                    for t in range(2):
                        sl = SS[:, i, 0:128] if t == 0 else SS[:, i, 128:384]
                        a = do("act", lambda e, sl=sl, i=i, t=t, h=h: e.activation(
                            sl, sl, ACT.Exp, bias=nm[:, 4 * t + i:4 * t + i + 1], scale=exp_scale(h, t),
                            accum_out=dn[:, 4 * t + i:4 * t + i + 1]), nd, w.get("rd"))
                w["exp"] = a

            def denom():
                a = w["exp"]
                if "sink" in w:
                    a = w["sink"](heads, w, a)
                d = do("dve", lambda e: e.reciprocal(dn, dn), a)
                for i in range(4):
                    for t in range(2):
                        sl = SS[:, i, 0:128] if t == 0 else SS[:, i, 128:384]
                        w["p", i % 2] = do(("dve", "pool")[i % 2], lambda e, sl=sl, i=i, t=t: e.tensor_scalar(
                            sl, sl, dn[:, 4 * t + i:4 * t + i + 1], None, ALU.mult), d)
                w["p"] = w["rd"] = [w["p", 0], w["p", 1]]

            def values(half):
                def run():
                    for i in (2 * half, 2 * half + 1):
                        h = heads[i]
                        PT = sh["area"][i % 2]
                        b = (2, 0)[i % 2]
                        for j in range(3):
                            m = do("pe", lambda e: e.transpose(PB[b][:, 128 * j:128 * j + 128], SS[:, i, 128 * j:128 * j + 128], ident),
                                   w["p"], free[b])
                        a = do("act", lambda e: e.activation(PT, PB[b][:, 0:384], ACT.Copy), m, sh.get(("v", i % 2)), sh["s0"])
                        free[b] = [a]
                        w["pt"] = sh["pt"] = m
                        sh["pt", i % 2] = a
                    for i in (2 * half, 2 * half + 1):
                        h = heads[i]
                        PT = sh["area"][i % 2]
                        rows = slice(64 * (h % 2), 64 * (h % 2) + 64)
                        do("pe", lambda e, h=h, PT=PT, rows=rows: e.matmul(PB[3][rows, 0:128], vals(h, 0), PT[:, 0:128], start=True,
                                                                           stop=True, skip_group_check=True),
                           sh["pt", i % 2], free[3], silent=True)
                        do("pe", lambda e, h=h, PT=PT, rows=rows: e.matmul(PB[3][rows, 128:256], vals(h, 0), PT[:, 128:256],
                                                                           start=False, stop=False, skip_group_check=True),
                           silent=True)
                        m = do("pe", lambda e, h=h, PT=PT, rows=rows: e.matmul(PB[3][rows, 128:256], vals(h, 1), PT[:, 256:384],
                                                                               start=False, stop=True, skip_group_check=True))
                        sh["v", i % 2] = m
                    c = dst + heads[2 * half] // 2
                    sh["o"][c] = split_psum(PB[3][:, 0:256], 1, c, 1.0, m, sh["dst"])
                    free[3] = [sh["o"][c]]
                return run

            return [scores, denom, values(0), values(1)]

        def neg1(heads, w, tok):
            for t in range(2):
                o = w["nm"][:, 4 * t:4 * t + 4]
                r = rq8[:, 16 * t + heads[0]:16 * t + heads[0] + 4]
                d = do("dve", lambda e: e.tensor_tensor(o, w["mx"][:, 4 * t:4 * t + 4], r, ALU.mult), tok, at1["rq"], w.get("rd"))
                d = do("dve", lambda e: e.tensor_tensor(o, o, snk[:, heads[0]:heads[0] + 4], ALU.max), d)
                d = do("dve", lambda e: e.tensor_scalar(o, o, -1.0, None, ALU.mult), d)
            return d

        def sink1(heads, w, tok):
            for t in range(2):
                o = w["sk"][:, 4 * t:4 * t + 4]
                d = do("dve", lambda e: e.tensor_tensor(o, w["nm"][:, 4 * t:4 * t + 4], snk[:, heads[0]:heads[0] + 4], ALU.add), tok)
            a = do("act", lambda e: e.activation(w["sk"], w["sk"], ACT.Exp), d)
            return do("dve", lambda e: e.tensor_tensor(w["dn"], w["dn"], w["sk"], ALU.add), a)

        W = [{"mx": small(8), "nm": small(8), "dn": small(8), "sk": small(8), "sink": sink1} for i in range(2)]
        W[0]["ss"], W[1]["ss"] = S0[:, 0:1536], RC[:, 0:1536]
        w1 = {"area": [S0[:, 1536:1920], RC[:, 1536:1920]], "o": {}}

        def attention1(n):
            if n == 0:
                w1["s0"] = [at1["kT"], at1["qT"]]
            heads = [4 * n + i for i in range(4)]

            def lhs(h, t):
                r = slice(64 * (h % 2), 64 * (h % 2) + 64)
                c = (h // 2) * 256 + t * 128
                return S1[r, c:c + 128]

            def rhs(h, a, b):
                r = slice(64 * (h % 2), 64 * (h % 2) + 64)
                c = (h // 4) * 256
                return KT[r, c + a:c + b]

            return group(heads, lhs, rhs, cst("mask1", 384),
                         lambda h, t: rq8[:, 16 * t + h:16 * t + h + 1], [at1["kT"], at1["qT"]], neg1,
                         lambda h, t: KV[:, t, 256 + 64 * (h // 4):256 + 64 * (h // 4) + 64], 0, W[n % 2], w1)

        def steps_of(group, n):
            def run(*which):
                return lambda: [group(g)[k]() for g, k in which]
            out = [run((0, 0))]
            for g in range(n):
                out += [run((g, 1), (g + 1, 0)) if g + 1 < n else run((g, 1)), run((g, 2), (g, 3))]
            return out

        def gates(key, th, tl, ready, steps, reuse):
            toks = [None, None]
            for b in range(4):
                banks, tok = tokens_by((key, b), 2, th, tl, 0, ready, 512, steps[b])
                g = (GA, GB)[b // 2]
                if b == 2:
                    while ("kr", 1) not in at1:
                        step()
                for t in range(2):
                    o = v3(g, 2, 1024)[:, t, 512 * (b % 2):512 * (b % 2) + 512]
                    a = do("act", lambda e: e.activation(o, PB[banks[t]][:, :], ACT.Tanh, scale=0.5), tok, reuse())
                    free[banks[t]] = [a]
                    toks[b // 2] = a
            return toks

        def gated(key, nu, th, tl, ready, g, gtok, steps=1, k0=0, into=None):
            done = {}
            for b in range(2):
                banks, tok = tokens_by((key, b), nu, th, tl, k0, ready, 512, steps)
                for t in range(2):
                    o = v3(g, 2, 1024)[:, t, 512 * b:512 * b + 512]
                    d = do("dve", lambda e: e.scalar_tensor_tensor(o, o, 1.0, PB[banks[t]][:, :], ALU.add, ALU.mult), tok, gtok)
                    free[banks[t]] = [d]
                    if into is not None:
                        i = v3(into, 2, 1024)[:, t, 512 * b:512 * b + 512]
                        d = do("dve", lambda e: e.tensor_tensor(i, i, o, ALU.add), d)
                for c in range(4):
                    done[4 * b + c] = d
            return done, tok

        def squared(ss, t, b, tok, after=None):
            x = v3(X, 2, 1024)[:, t, 512 * b:512 * b + 512]
            j = 2 * t + b
            return do("act", lambda e: e.activation(S0[:, 512 * j:512 * j + 512], x, ACT.Square, accum_out=ss[:, j:j + 1]), tok,
                      after, last["junk"])

        def residual(key, th, tl, ready, xtok, after=None):
            ss = small(4)
            for b in range(2):
                banks, tok = tokens_by((key, b), 2, th, tl, 0, ready, 512)
                for t in range(2):
                    o = v3(X, 2, 1024)[:, t, 512 * b:512 * b + 512]
                    d = do("dve", lambda e: e.tensor_tensor(o, o, PB[banks[t]][:, :], ALU.add), tok, xtok)
                    free[banks[t]] = [d]
                    a = squared(ss, t, b, d, after)
            return a, tok, ss

        MD = TMP[:, 1024:1280]

        def mem_diag():
            for t in range(2):
                ml["d"] = do("dve", lambda e: e.tensor_scalar(MD[:, 128 * t:128 * t + 128], ident, mrs[:, t:t + 1], None, ALU.mult),
                             rnn["root"])

        MN = {}

        def mem_turn(j):
            MN.update(turn_over(v3(RB, 2, D), range(4 * j, 4 * j + 4), "mem_norm_g_2", 0, [ml["d"], mem_tok], gates_pe, MD, banks=(0, 1)))

        bg += [prep_tables, prep_sums]
        for c in range(8):
            bg.append(lambda c=c: rnn_scan(c))
            if c in (1, 3, 5):
                bg.append((lambda: prep_rope(0), lambda: prep_rope(1), prep_rope_k)[c // 2])
        bg.append(lambda: rnn_out(7))
        ga_tok, gb_tok = gates("gates", TH[0], TL[0], h_tok, (2, 2, 1, 1), lambda: [at1["k"], at1.get(("kr", 1))])
        gates_pe = used_done[st["used"] - 1]
        while ("y", 7) not in rnn:
            step()
        mem_tok = Q.dma("act", "mem", lambda e: e.dma_start(v3(RB, 2, D), A["mem_2"][0].rearrange("(t p) d -> p t d", p=128)),
                        [rnn["y", c] for c in range(8)])
        attend = steps_of(attention1, 4)
        bg += [lambda: (prep_dup(), mem_diag()), lambda: (prep_turn_k(), prep_turn_q()), attend[0], lambda: mem_turn(0),
               lambda: mem_turn(1)]
        d, ya_pe = gated("w_rnn_proj", 2, TH[1], TL[1], {c: rnn["y", c] for c in range(8)}, GA, ga_tok, 1)
        flush()
        w1["dst"] = ya_pe
        bg += attend[1:]

        for b in range(2):
            banks, tok = features_by(("w_xkv_2", b), 2, TH[0], TL[0], MN, 1)
            for h in range(2):
                c0 = 4 * b + 2 * h
                mk_tok = do("act", lambda e: e.activation(RA[:, c0 * 256:c0 * 256 + 512], PB[banks[h]][:, :], ACT.Copy),
                            tok, rnn["y", 7])
                free[banks[h]] = [mk_tok]
        MV = v3(RB, 2, 1024)
        for b in range(2):
            banks, tok = tokens_by(("w_xkv_2", b + 2), 2, TH[0], TL[0], 0, MN, 512, 1)
            for t in range(2):
                mv_tok = do("act", lambda e: e.activation(MV[:, t, 512 * b:512 * b + 512], PB[banks[t]][:, :], ACT.Copy), tok, MN)
                free[banks[t]] = [mv_tok]
        mem_pe = tok
        flush()
        d3, yb_pe = gated("w_attn_proj", 2, TH[1], TL[1], w1["o"], GB, gb_tok, into=GA)
        m_tok = turn_over(v3(GA, 2, 1024), range(8), None, 0, d3, mem_pe, scale=0.5)
        x1, pe, ss = residual("w_out", TH[0], TL[0], m_tok, x_tok, [w1["pt"], w1["v", 0], w1["v", 1]])

        hm = norm(v3(X, 2, D), D, "g_mlp", 0, x1, pe, ss=ss)
        hid = {}

        def mlp_down(b):
            for r in range(2):
                hi, lo, rdy = take(("w_down", b, r))
                for t in range(2):
                    for h in range(2):
                        bank = 2 * t + h
                        for k in range(2):
                            kk = 4 * (b % 2) + 2 * r + k
                            c = slice(kk * 256 + t * 128, kk * 256 + t * 128 + 128)
                            tok = mm3(PB[bank][:, :], TH[1][:, c], TL[1][:, c], hi[:, k, 512 * h:512 * h + 512],
                                      lo[:, k, 512 * h:512 * h + 512], b == 0 and r == 0 and k == 0,
                                      b == 7 and r == 1 and k == 1, (rdy, hid[b], free[bank]), k == 1)
                give(("w_down", b, r), tok)
            hid["used", b] = tok

        P = v3(GB, 2, 256)
        p_tok = Q.dma("act", "p", lambda e: e.dma_start(P, A["p"][0, 0].rearrange("(t p) d -> p t d", p=128)), d3)
        for b in range(9):
            if b < 8:
                banks, tok = features_by(("w_up", b), 2, TH[0], TL[0], hm)
                hid[b] = []
                for h in range(2):
                    c0 = 4 * (b % 2) + 2 * h
                    s = S1[:, c0 * 256:c0 * 256 + 512]
                    a = do("act", lambda e, s=s, i=PB[banks[h]][:, :]: e.activation(s, i, ACT.Relu), tok, hid.get(b - 2), hm)
                    free[banks[h]] = [a]
                    p = do("dve", lambda e, s=s: e.tensor_tensor(s, s, s, ALU.mult), a)
                    hid[b] += split_t(s, 1, c0, 2, p, [hid.get(("used", b - 2)), pe])
            if b == 8:
                pt_tok = turn_over(P, range(2), None, 0, p_tok, tok, banks=pair())
            if b > 0:
                mlp_down(b - 1)
        up_pe = hid["used", 7]
        ss = small(4)
        for t in range(2):
            for h in range(2):
                o = v3(X, 2, 1024)[:, t, 512 * h:512 * h + 512]
                d = do("dve", lambda e: e.tensor_tensor(o, o, PB[2 * t + h][:, :], ALU.add), up_pe)
                free[2 * t + h] = [d]
                x2 = squared(ss, t, h, d)
        _, xd = root_mean(ss, D, DG, x2)

        EB = v3(RC, 2, 1024)
        for b in range(2):
            banks, tok = tokens_by(("w_ple_proj", b), 1, TH[0], TL[0], 0, pt_tok, 512)
            for t in range(2):
                e_tok = do("act", lambda e: e.activation(EB[:, t, 512 * b:512 * b + 512], PB[banks[t]][:, :], ACT.Copy),
                           tok, ya_pe)
                free[banks[t]] = [e_tok]
        ple_pe = tok
        xg = turn_over(v3(X, 2, D), range(8), "g_ple", 0, xd, ple_pe, DG)
        ss = small(4)
        GT = v3(GA, 2, 1024)
        for b in range(2):
            banks, tok = tokens_by(("w_ple_gate", b), 2, TH[0], TL[0], 0, xg, 512)
            a = [do("act", lambda e: e.activation(GT[:, t, 512 * b:512 * b + 512], PB[banks[t]][:, :], ACT.Tanh, scale=0.5), tok, m_tok)
                 for t in range(2)]
            for t in range(2):
                free[banks[t]] = [a[t]]
                g, ee, xx = [x[:, t, 512 * b:512 * b + 512] for x in (GT, EB, v3(X, 2, 1024))]
                d = do("dve", lambda e: e.scalar_tensor_tensor(g, g, 1.0, ee, ALU.add, ALU.mult), a[t], e_tok)
                d = do("dve", lambda e: e.scalar_tensor_tensor(xx, g, 0.5, xx, ALU.mult, ALU.add), d)
                x3 = squared(ss, t, b, d)
        gate_pe = tok

        h2 = norm(v3(X, 2, D), D, "mix_norm_g_2", 0, x3, gate_pe, ss=ss)
        QL = v3(RC, 2, 384)
        KL = v3(KT, 2, 288)
        banks, tok = tokens_by(("lat", 0), 2, TH[0], TL[0], 0, h2, 384)
        for t in range(2):
            ql_tok = do("act", lambda e, t=t, i=PB[banks[t]][:, 0:384]: e.activation(QL[:, t], i, ACT.Copy), tok, d)
            free[banks[t]] = [ql_tok]
        banks, tok = tokens_by(("lat", 1), 2, TH[0], TL[0], 0, h2, 288)
        for t in range(2):
            kl_tok = do("act", lambda e, t=t, i=PB[banks[t]][:, 0:288]: e.activation(KL[:, t], i, ACT.Copy), tok)
            free[banks[t]] = [kl_tok]
        U = v3(TMP, 4, 272)
        zt = do("pool", lambda e: e.memset(U[:, :, 0:16], 0.0), MN)
        banks, tok = features_by(("lat", 2), 2, TH[0], TL[0], h2)
        for h in range(2):
            u_tok = do("act", lambda e, h=h, i=v3(PB[banks[h]], 2, 256): e.activation(U[:, 2 * h:2 * h + 2, 16:272], i, ACT.Copy), tok,
                       rnn["end", 7])
            free[banks[h]] = [u_tok]
        pw_tok = Q.dma("act", "pool_w", lambda e: e.dma_start(v3(BD, 4, 128, 0), A["pool_w_2"][0].rearrange("g c e -> c g e")),
                       rnn["mm", 7])
        PW = v3(BD, 4, 128, 0)
        po = {"u": {}}
        W2 = [S0[:, 272 * i:272 * i + 272] for i in range(4)]

        def pool_group(g):
            def run():
                w = 2 << g
                src = U[:, g, :]
                d = None
                for j in range(g + 1):
                    dst = W2[j % 2]
                    s = 1 << j
                    d0 = do("dve", lambda e, dst=dst, src=src, s=s: e.tensor_copy(dst[:, 0:s], src[:, 0:s]), d, u_tok, zt, h2,
                            po.get(("d", g - 1)))
                    d = do("dve", lambda e, dst=dst, src=src, s=s: e.tensor_tensor(dst[:, s:272], src[:, s:272], src[:, 0:272 - s],
                                                                                 ALU.add), d0, d)
                    src = dst
                m = W2[2]
                a = do("dve", lambda e: e.tensor_tensor(m[:, 0:16], src[:, 16:32], cst("count", 16, 16 * g), ALU.mult), d)
                b = do("dve", lambda e: e.tensor_scalar(m[:, 16:256], src[:, 32:272], 1.0 / w, None, ALU.mult), d)
                d = do("dve", lambda e: e.tensor_tensor(po_d[:, g, :], m[:, 0:256], U[:, g, 16:272], ALU.subtract), a, b)
                po["d", g] = d
            return run

        po_d = v3(S0, 4, 256, 1024)

        def pool_mm():
            for g in range(4):
                m = do("pe", lambda e: e.matmul(PB[g][:, 0:256], PW[:, g, :], po_d[:, g, :], start=True, stop=True,
                                                skip_group_check=True), po["d", g], pw_tok, free[g])
                free[g] = po["u"][g] = split_psum(PB[g][:, 0:256], 1, g, col("pool_scale_2", g), m, up_pe)

        pos_i = SM[:, small_at[0]:small_at[0] + 2].bitcast(I32)
        small(2)
        posf, ang, kk_, cs = small(2), small(32), small(32), small(64)
        for t in range(2):
            pos_tok = Q.dma("act", "pos", lambda e, t=t: e.dma_start(
                pos_i[:, t:t + 1], A["positions_2"][0, 128 * t:128 * t + 128].rearrange("(p o) -> p o", o=1)))
        C1, C2 = 6.28125, 0.0019350051879882812
        C3 = TWO_PI - C1 - C2

        def angles():
            d = do("dve", lambda e: e.tensor_copy(posf, pos_i), pos_tok)
            for t in range(2):
                d2 = do("dve", lambda e, t=t: e.tensor_scalar(ang[:, 16 * t:16 * t + 16], cst("inv", 16), posf[:, t:t + 1], None, ALU.mult),
                        d, const_tok)
            for j, ph in enumerate((0.25, 0.0)):
                o = cs[:, 32 * j:32 * j + 32]
                d = do("dve", lambda e, ph=ph: e.tensor_scalar(kk_, ang, 1.0 / TWO_PI, ph, ALU.mult, ALU.add), d2, d)
                d = do("dve", lambda e: e.tensor_scalar(kk_, kk_, 12582912.0, None, ALU.add), d)
                d = do("dve", lambda e: e.tensor_scalar(kk_, kk_, -12582912.0, None, ALU.add), d)
                d = do("dve", lambda e, o=o: e.scalar_tensor_tensor(o, kk_, -C1, ang, ALU.mult, ALU.add), d)
                d = do("dve", lambda e, o=o: e.scalar_tensor_tensor(o, kk_, -C2, o, ALU.mult, ALU.add), d)
                d = do("dve", lambda e, o=o: e.scalar_tensor_tensor(o, kk_, -C3, o, ALU.mult, ALU.add), d)
                if j == 0:
                    d = do("dve", lambda e, o=o: e.tensor_scalar(o, o, TWO_PI / 4, None, ALU.add), d)
                d = do("dve", lambda e, o=o: e.tensor_scalar(o, o, 3.1415925, -3.1415925, ALU.min, ALU.max), d)
            po["cs"] = do("act", lambda e: e.activation(cs, cs, ACT.Sin), d)

        gt2 = [None, None]

        def gates2(b, steps):
            banks, tok = tokens_by(("gates2", b), 2, TH[0], TL[0], 0, h2, 512, steps)
            for t in range(2):
                o = v3((GA, GB)[b // 2], 2, 1024)[:, t, 512 * (b % 2):512 * (b % 2) + 512]
                gt2[b // 2] = do("act", lambda e: e.activation(o, PB[banks[t]][:, :], ACT.Tanh, scale=0.5), tok, x3)
                free[banks[t]] = [gt2[b // 2]]

        la = {}
        DQ, DK = KW[:, 0:256], KW[:, 256:512]
        kvn_src = KL[:, :, 0:256]
        kr = small(64)

        def latent_stats():
            la["kr"] = do("dve", lambda e: e.tensor_copy(v3(kr, 2, 32), KL[:, :, 256:288]), kl_tok)
            sq, a = squares(QL, 384, S1, ql_tok, hid[7])
            sk, a2 = squares(kvn_src, 256, S1, kl_tok, hid[7])
            la["q"] = root_mean(sq, 384, DQ, a)[1]
            la["k"] = root_mean(sk, 256, DK, a2)[1]

        def q_turn():
            la["qn"] = turn_over(QL, range(3), "q_norm_g_2", 1, la["q"], up_pe, DQ, c0=4, banks=(2, 3))

        def k_turn():
            la["kn"] = turn_over(kvn_src, range(2), "kv_norm_g_2", 1, la["k"], q_pe, DK, c0=4, banks=(2, 3))

        bg += [latent_stats, q_turn, lambda: (angles(), pool_group(0)()), pool_group(1), pool_group(2), pool_group(3), pool_mm]
        gates2(0, 1)
        QM = v3(RC, 2, 768)
        for b in range(2):
            banks, tok = tokens_by(("w_q_up_2", b), 1, TH[1], TL[1], 4, la["qn"], 384)
            for t in range(2):
                qm_tok = do("act", lambda e: e.activation(QM[:, t, 384 * b:384 * b + 384], PB[banks[t]][:, 0:384], ACT.Copy), tok)
                free[banks[t]] = [qm_tok]
        q_pe = tok
        bg.insert(0, k_turn)
        gates2(1, 2)
        flush()
        KC = S0[:, 0:1536].rearrange("p (t h n) -> p t h n", t=2, h=8)
        VM = RD[:, :].rearrange("p (t h n) -> p t h n", t=2, h=8)
        c4 = cs[:, 0:32].rearrange("p (t n) -> p t n", t=2)
        s4 = cs[:, 32:64].rearrange("p (t n) -> p t n", t=2)
        m0, m1, m2, m3 = [S1[:, 1024 + 128 * j:1152 + 128 * j].rearrange("p (h n) -> p h n", h=8) for j in range(4)]
        r2 = {}

        def rope2(t):
            q1 = QM[:, t].rearrange("p (h n) -> p h n", h=8)
            c8 = c4[:, t].unsqueeze(1).to_broadcast([128, 8, 16])
            s8 = s4[:, t].unsqueeze(1).to_broadcast([128, 8, 16])
            a_, b_ = q1[:, :, 64:80], q1[:, :, 80:96]
            d = r2.get(("k", 0))
            ds = [do("dve", lambda e, o=o, x=x, y=y: e.tensor_tensor(o, x, y, ALU.mult), qm_tok, po["cs"], la["q"], d)
                  for o, x, y in ((m0, a_, c8), (m1, b_, s8), (m2, b_, c8), (m3, a_, s8))]
            d = do("dve", lambda e: e.tensor_tensor(a_, m0, m1, ALU.subtract), ds[-1])
            r2["q", t] = d = do("dve", lambda e: e.tensor_tensor(b_, m2, m3, ALU.add), ds[-1])
            k1, k2 = kr[:, 32 * t:32 * t + 16], kr[:, 32 * t + 16:32 * t + 32]
            n = [S1[:, 1536 + 16 * j:1552 + 16 * j] for j in range(6)]
            ds = [do("dve", lambda e, o=o, x=x, y=y: e.tensor_tensor(o, x, y, ALU.mult), la["kr"], d)
                  for o, x, y in ((n[0], k1, c4[:, t]), (n[1], k2, s4[:, t]), (n[2], k2, c4[:, t]), (n[3], k1, s4[:, t]))]
            d = do("dve", lambda e: e.tensor_tensor(n[4], n[0], n[1], ALU.subtract), ds[-1])
            d = do("dve", lambda e: e.tensor_tensor(n[5], n[2], n[3], ALU.add), ds[-1])
            r2["k", t] = do("dve", lambda e: e.tensor_copy(KC[:, t, :, 64:96], S1[:, 1600:1632].unsqueeze(1).to_broadcast([128, 8, 32])),
                            d, po["d", 3], po["u"])

        def turn2(src, dst, ready):
            def run():
                for h in range(8):
                    bank = h // 2 % 4
                    for t in range(2):
                        o = PB[bank][0:96, 256 * (h % 2) + 128 * t:256 * (h % 2) + 128 * t + 128]
                        m = do("pe", lambda e: e.transpose(o, src(t, h), ident), ready(), free[bank])
                    if h % 2:
                        a = do("act", lambda e: e.activation(dst[0:96, 256 * (h - 1):256 * (h + 1)], PB[bank][0:96, :], ACT.Copy),
                               m, ready())
                        free[bank] = [a]
                r2[dst.name] = a
            return run

        turn_q = turn2(lambda t, h: QM[:, t, 96 * h:96 * h + 96], S1, lambda: [r2["k", 1], r2["q", 1]])
        bg += [lambda: rope2(0), lambda: rope2(1)]
        for b in range(2):
            banks, tok = tokens_by(("w_kv_up_2", b), 1, TH[1], TL[1], 4, la["kn"], 512)
            for t in range(2):
                i = PB[banks[t]][:, :].rearrange("p (h n) -> p h n", h=4)
                a1 = do("act", lambda e: e.activation(KC[:, t, 4 * b:4 * b + 4, 0:64], i[:, :, 0:64], ACT.Copy), tok, po["d", 3],
                        po["u"])
                a2 = do("act", lambda e: e.activation(VM[:, t, 4 * b:4 * b + 4, :], i[:, :, 64:128], ACT.Copy), tok)
                free[banks[t]] = [a2]
        kvm_tok = a2
        kv_pe = tok
        turn_k = turn2(lambda t, h: KC[:, t, h, :], RC, lambda: [r2["k", 1], kvm_tok, r2["S1"]])

        SC2 = 1.0 / float(np.sqrt(96.0))

        def neg2(heads, w, tok):
            return do("dve", lambda e: e.tensor_scalar(w["nm"], w["mx"], -SC2, None, ALU.mult), tok, w.get("rd"))

        V = [{k: w[k] for k in ("mx", "nm", "dn")} for w in W]
        V[0]["ss"], V[1]["ss"] = S0[:, 0:1536], BT[:, 512:2048]
        w2 = {"area": [KT[:, 0:384], KT[:, 384:768]], "o": {}, "dst": kv_pe}

        def group2(n):
            heads = [4 * n + i for i in range(4)]
            w2["s0"] = [r2["RC"], la["kn"], la["kr"], po["u"], po["d", 3]]
            return group(heads, lambda h, t: S1[0:96, 256 * h + 128 * t:256 * h + 128 * t + 128],
                         lambda h, a, b: RC[0:96, 256 * h + a:256 * h + b], cst("mask2", 384),
                         lambda h, t: SC2, [r2["S1"], r2["RC"]], neg2, lambda h, t: VM[:, t, h, :], 4, V[n], w2)

        attend = steps_of(group2, 2)
        bg += [lambda: (turn_q(), turn_k()), *attend]
        gates2(2, 1)
        gates2(3, 1)
        d, pb_pe = gated("w_pool_branch_2", 1, TH[1], TL[1], po["u"], GB, gt2[1], 1)
        flush()
        d3, at_pe = gated("w_attn_branch_2", 1, TH[1], TL[1], w2["o"], GA, gt2[0], k0=4, into=GB)
        m_tok = turn_over(v3(GB, 2, 1024), range(8), None, 1, d3, at_pe, scale=0.5)
        x4, mo_pe, ss = residual("w_mix_out_2", TH[1], TL[1], m_tok, None, [w2["pt"], w2["v", 0], w2["v", 1]])

        hx = norm(v3(X, 2, D), D, "xattn_norm_g_2", 0, x4, at_pe, ss=ss)
        xa = {"o": {}}
        mx4, dn4 = small(8), small(8)

        def m_scores(h):
            b = h % 2
            for t in range(2):
                for k in range(2):
                    c = (2 * h + k) * 256
                    m = do("pe", lambda e: e.matmul(
                        PB[b][:, 256 * t:256 * t + 256], RC[:, c + 128 * t:c + 128 * t + 128], RA[:, c:c + 256],
                        start=(t == 0 and k == 0), stop=(k == 1), skip_group_check=True), xa["q", h // 2], mk_tok, free[b])
            E = S0[:, 512 * b:512 * b + 512]
            mm, dd = mx4[:, 2 * h:2 * h + 2], dn4[:, 2 * h:2 * h + 2]
            d = do("dve", lambda e: e.tensor_reduce(mm, v3(PB[b], 2, 256), AXX, ALU.max), m)
            d = do("dve", lambda e: e.tensor_scalar(mm, mm, -0.0625, None, ALU.mult), d)
            for t in range(2):
                a = do("act", lambda e: e.activation(
                    E[:, 256 * t:256 * t + 256], PB[b][:, 256 * t:256 * t + 256], ACT.Exp, bias=mm[:, t:t + 1], scale=0.0625,
                    accum_out=dd[:, t:t + 1]), d, xa.get(("t", h - 2)), hx)
            free[b] = [a]
            d = do("dve", lambda e: e.reciprocal(dd, dd), a)
            for t in range(2):
                xa["p", h] = do("dve", lambda e: e.tensor_scalar(E[:, 256 * t:256 * t + 256], E[:, 256 * t:256 * t + 256],
                                                                 dd[:, t:t + 1], None, ALU.mult), d)

        def m_turn(h):
            E = S0[:, 512 * (h % 2):512 * (h % 2) + 512]
            for mt in range(2):
                for t in range(2):
                    m = do("pe", lambda e: e.transpose(PB[2][:, 256 * mt + 128 * t:256 * mt + 128 * t + 128],
                                                       E[:, 256 * t + 128 * mt:256 * t + 128 * mt + 128], ident),
                           xa["p", h], free[2])
            xa["t", h] = m
            PTm = S0[:, 1024 + 512 * (h % 2):1536 + 512 * (h % 2)]
            xa["pt", h] = do("act", lambda e: e.activation(PTm, PB[2][:, :], ACT.Copy), m, xa.get(("v", h - 2)), hx)
            free[2] = [xa["pt", h]]

        def m_values(h):
            PTm = S0[:, 1024 + 512 * (h % 2):1536 + 512 * (h % 2)]
            for dv in range(2):
                for mt in range(2):
                    c = 256 * h + 128 * dv
                    m = do("pe", lambda e: e.matmul(
                        PB[3][:, 256 * dv:256 * dv + 256], MV[:, mt, c:c + 128], PTm[:, 256 * mt:256 * mt + 256],
                        start=(dv == 0 and mt == 0), stop=(mt == 1), skip_group_check=True), xa["pt", h], mv_tok, free[3])
            xa["v", h] = m
            hi, lo = TH[1][:, 512 * h:512 * h + 512], TL[1][:, 512 * h:512 * h + 512]
            a = do("act", lambda e: e.activation(hi, PB[3][:, :], ACT.Copy), m, mo_pe)
            d = do("dve", lambda e: e.tensor_tensor(lo, PB[3][:, :], hi.bitcast(F), ALU.subtract), a)
            free[3] = [d]
            xa["o"][2 * h] = xa["o"][2 * h + 1] = [a, d]

        for b in range(2):
            banks, tok = features_by(("w_xq_2", b), 2, TH[0], TL[0], hx)
            for h in range(2):
                c0 = 4 * b + 2 * h
                xa["q", b] = do("act", lambda e: e.activation(RC[:, c0 * 256:c0 * 256 + 512], PB[banks[h]][:, :], ACT.Copy), tok)
                free[banks[h]] = [xa["q", b]]
            if b == 0:
                bg += [lambda: m_scores(0), lambda: m_scores(1)]
        xq_pe = tok
        for h in range(4):
            m_turn(h)
            if h < 2:
                m_scores(h + 2)
            m_values(h)
        x5, xo_pe, ss = residual("w_xo_2", TH[1], TL[1], xa["o"], None, [xa["v", h] for h in range(4)])

        frs, xd = root_mean(ss, D, DG, x5)
        hf = turn_over(v3(X, 2, D), range(8), "ffn_norm_g_2", 0, xd, [xq_pe, fg_tok], DG, step=8)
        Xv = v3(X, 2, 1024)
        early.close()
        XN = [sb("XNH", 2048, R), sb("XNL", 2048, R)]
        FB = sb("FB", 1024)
        XN4 = [x[:, :].rearrange("p (t k q) -> p t k q", t=2, k=8) for x in XN]
        by_chunks = S1[:, :].rearrange("p (t q k) -> p t k q", t=2, k=8)
        fb = Q.dma("act", "fb", lambda e: e.dma_start(FB[:, :], A["ffn_norm_g_2"][0].partition_broadcast(128)), x5, xo_pe)
        xs = []
        for t in range(2):
            a = do("act", lambda e: e.activation(v3(S1, 2, 1024)[:, t], Xv[:, t], ACT.Copy, scale=frs[:, t:t + 1]), xd, hf)
            xs.append(do("pool", lambda e: e.tensor_tensor(v3(S1, 2, 1024)[:, t], v3(S1, 2, 1024)[:, t], FB[:, :], ALU.mult), a, fb))
        banks = pair()
        hi, lo, rdy = take(("router", 0, 0))
        L = small(72)
        L3 = v3(L, 2, 36)
        for t in range(2):
            for k in range(8):
                c = slice(k * 256 + t * 128, k * 256 + t * 128 + 128)
                tok = mm3(PB[banks[t]][:, 0:36], TH[0][:, c], TL[0][:, c], hi[:, k, :], lo[:, k, :], k == 0, k == 7,
                          (rdy, hf[k], free[banks[t]]), k == 7)
            lt = do("dve", lambda e, t=t, b=banks[t]: e.tensor_tensor(L3[:, t], PB[b][:, 0:36], rb, ALU.add), tok, bc_tok)
            free[banks[t]] = [lt]
        give(("router", 0, 0), tok)
        rt_pe = tok

        at_ = [0]

        def rt(n):
            o = at_[0]
            at_[0] += n
            return KW[:, o:o + n]

        def b3(ap, n):
            return ap.unsqueeze(2).to_broadcast([128, 2, n])

        def first_max(src, n, dst, mxt, order, tok):
            v = v3(rt(2 * n), 2, n)
            d = do("dve", lambda e: e.tensor_reduce(mxt, src, AXX, ALU.max), tok)
            d = do("dve", lambda e: e.tensor_tensor(v, src, b3(mxt, n), ALU.is_equal), d)
            od = cst("order", n, order).unsqueeze(1).to_broadcast([128, 2, n])
            d = do("dve", lambda e: e.tensor_tensor(v, v, od, ALU.mult), d)
            q = rt(2)
            d = do("dve", lambda e: e.tensor_reduce(q, v, AXX, ALU.max), d)
            return do("dve", lambda e: e.tensor_tensor(dst, v, b3(q, n), ALU.is_equal), d)

        G = L3[:, :, 0:4]
        og = v3(rt(8), 2, 4)
        gm = rt(2)
        d = first_max(G, 4, og, gm, 0, lt)
        eg = v3(rt(8), 2, 4)
        d = do("dve", lambda e: e.tensor_tensor(eg, G, b3(gm, 4), ALU.subtract), d)
        a = do("act", lambda e: e.activation(eg, eg, ACT.Exp), d)
        pg = rt(2)
        d = do("dve", lambda e: e.tensor_reduce(pg, eg, AXX, ALU.add), a)
        d = do("dve", lambda e: e.reciprocal(pg, pg), d)
        se = rt(64)
        sel = v3(rt(16), 2, 8)
        for t in range(2):
            t4 = se[:, 32 * t:32 * t + 32].rearrange("p (g n) -> p g n", g=4)
            d = do("dve", lambda e, t=t, t4=t4: e.tensor_tensor(t4, L3[:, t, 4:36].rearrange("p (g n) -> p g n", g=4),
                                                              og[:, t].unsqueeze(2).to_broadcast([128, 4, 8]), ALU.mult), d)
            d = do("dve", lambda e, t=t: e.tensor_reduce(sel[:, t], se[:, 32 * t:32 * t + 32].rearrange("p (g n) -> p n g", g=4),
                                                         AXX, ALU.add), d)
        o1, o2 = v3(rt(16), 2, 8), v3(rt(16), 2, 8)
        ma, mb = rt(2), rt(2)
        d = first_max(sel, 8, o1, ma, 4, d)
        s2 = v3(rt(16), 2, 8)
        d = do("dve", lambda e: e.scalar_tensor_tensor(s2, o1, NEG, sel, ALU.mult, ALU.add), d)
        d = first_max(s2, 8, o2, mb, 4, d)
        e2 = rt(2)
        d = do("dve", lambda e: e.tensor_tensor(e2, mb, ma, ALU.subtract), d)
        a = do("act", lambda e: e.activation(e2, e2, ACT.Exp), d)
        mk = rt(64)
        oo = v3(rt(16), 2, 8)
        d = do("dve", lambda e: e.tensor_tensor(oo, o1, o2, ALU.add), d)
        for t in range(2):
            mk_t = do("dve", lambda e: e.tensor_tensor(mk[:, 32 * t:32 * t + 32].rearrange("p (g n) -> p g n", g=4),
                                                       og[:, t].unsqueeze(2).to_broadcast([128, 4, 8]),
                                                       oo[:, t].unsqueeze(1).to_broadcast([128, 4, 8]), ALU.mult), d)
        U_, ONE = cst("upper", 128), cst("ones", 128)
        mk0, mk1 = mk[:, 0:32], mk[:, 32:64]
        for o, l, r, go, end in ((0, U_, mk0, True, True), (32, U_, mk1, False, False), (32, ONE, mk0, False, True),
                                 (64, ONE, mk0, False, False), (64, ONE, mk1, False, True)):
            rk_pe = do("pe", lambda e: e.matmul(PB[1][:, o:o + 32], l, r, start=go, stop=end, skip_group_check=True),
                       mk_t, free[1])
        rank = rt(64)
        most, flag = rt(1), rt(1).bitcast(I32)
        k = do("dve", lambda e: e.tensor_reduce(most, PB[1][:, 64:96], AXX, ALU.max), rk_pe)
        flag_tok = do("dve", lambda e: e.tensor_copy(flag, most), k)
        k = do("dve", lambda e: e.scalar_tensor_tensor(rank, PB[1][:, 0:64], 1.0, mk, ALU.add, ALU.mult), k)
        free[1] = [k]
        rank_tok = do("dve", lambda e: e.tensor_scalar(rank, rank, -1.0, None, ALU.add), k)
        d = rank_tok
        wa, wb = rt(2), rt(2)
        d = do("dve", lambda e: e.tensor_scalar(wa, e2, 1.0, None, ALU.add), a)
        d = do("dve", lambda e: e.reciprocal(wa, wa), d)
        d = do("dve", lambda e: e.scalar_tensor_tensor(wa, wa, 0.5, pg, ALU.mult, ALU.mult), d)
        d = do("dve", lambda e: e.tensor_tensor(wb, wa, e2, ALU.mult), d)
        d = do("dve", lambda e: e.tensor_tensor(o1, o1, b3(wa, 8), ALU.mult), d)
        d = do("dve", lambda e: e.tensor_tensor(o2, o2, b3(wb, 8), ALU.mult), d)
        d = do("dve", lambda e: e.tensor_tensor(o1, o1, o2, ALU.add), d)
        cw = se
        for t in range(2):
            d = do("dve", lambda e, t=t: e.tensor_tensor(cw[:, 32 * t:32 * t + 32].rearrange("p (g n) -> p g n", g=4),
                                                         og[:, t].unsqueeze(2).to_broadcast([128, 4, 8]),
                                                         o1[:, t].unsqueeze(1).to_broadcast([128, 4, 8]), ALU.mult), d)
        cw_tok = d
        xn = []
        for t in range(2):
            xa_ = do("act", lambda e: e.activation(XN4[0][:, t], by_chunks[:, t], ACT.Copy), xs[t], m_tok)
            xn.append(do(("pool", "dve")[t], lambda e: e.tensor_tensor(XN4[1][:, t], by_chunks[:, t], XN4[0][:, t].bitcast(F),
                                                                       ALU.subtract), xa_, m_tok))

        def finish(acc_tok, FG, fing, after):
            fs, fr, f2 = NR[:, 120:124], NR[:, 124:126], NR[:, 126:128]
            for t in range(2):
                for h in range(2):
                    o = Xv[:, t, 512 * h:512 * h + 512]
                    j = 2 * t + h
                    x6 = do("dve", lambda e: e.tensor_tensor(o, o, PB[j][:, :], ALU.add), acc_tok)
                    a = do("act", lambda e: e.activation(S0[:, 512 * j:512 * j + 512], o, ACT.Square, accum_out=fs[:, j:j + 1]),
                           x6, after)
            s4 = fs.rearrange("p (t b) -> p t b", t=2)
            d = do("dve", lambda e: e.tensor_tensor(f2, s4[:, :, 0], s4[:, :, 1], ALU.add), a)
            r = rsqrt_mean(fr, f2, D, (d,))
            os = []
            for t in range(2):
                for h in range(2):
                    c = slice(512 * h, 512 * h + 512)
                    d = do("dve", lambda e: e.scalar_tensor_tensor(v3(S1, 2, 1024)[:, t, c], Xv[:, t, c], fr[:, t:t + 1], FG[:, c],
                                                                   ALU.mult, ALU.mult), r, fing, after)
                    eng = ("sp", "act")[h]
                    os.append(Q.dma(eng, ("out", "out2")[h], lambda e: e.dma_start(out[0, 128 * t:128 * t + 128, c],
                                                                                   v3(S1, 2, 1024)[:, t, c]), d))
            Q.wait("sp", os)

        def dense(late):
            CB = [S0, S1, sbe("CB0", 2048, F, late), sbe("CB1", 2048, F, late)]
            FG = sbe("FGd", 1024, F, late)
            GS = sbe("GSd", 1024, F, late)
            CW = sbe("CWd", 256, F, late)
            for t in range(2):
                m = do("pe", lambda e: e.transpose(PB[0][0:32, 128 * t:128 * t + 128], cw[:, 32 * t:32 * t + 32], ident),
                       cw_tok, free[0])
            cwT = CW[0:32, :]
            a = do("act", lambda e: e.activation(cwT, PB[0][0:32, 0:256], ACT.Copy), m, hf)
            free[0] = [a]
            cwb = {}
            for e_ in range(0, NE, 2):
                b = (e_ // 2) % 4
                for j in range(2):
                    m = do("pe", lambda e: e.matmul(PB[b][:, 256 * j:256 * j + 256],
                                                    ident[0:32, e_ + j:e_ + j + 1].to_broadcast([32, 128]), cwT,
                                                    start=True, stop=True, skip_group_check=True), a, free[b])
                o = CB[e_ // 8][:, 256 * (e_ % 8):256 * (e_ % 8) + 512]
                if e_ % 4:
                    k = do("act", lambda e: e.activation(o, PB[b][:, :], ACT.Copy), m, hf, xa_, xn)
                else:
                    k = do("dve", lambda e: e.tensor_copy(o, PB[b][:, :]), m, hf, xa_, xn)
                free[b] = [k]
                cwb[e_] = cwb[e_ + 1] = k
            fing = Q.dma("act", "fing", lambda e: e.dma_start(FG[:, :], A["final_norm_g_2"].partition_broadcast(128)), hf)
            ex = {}

            def moe_down(p):
                for k in range(2):
                    hi, lo, rdy = take(("moe_out", p, k))
                    for bank in range(4):
                        t, h = bank // 2, bank % 2
                        for j in range(2):
                            kk = 2 * ((2 * p + j) % 4) + k
                            c = slice(kk * 256 + t * 128, kk * 256 + t * 128 + 128)
                            tok = mm3(PB[bank][:, :], TH[1][:, c], TL[1][:, c], hi[:, j, 512 * h:512 * h + 512],
                                      lo[:, j, 512 * h:512 * h + 512], p == 0 and j == 0 and k == 0,
                                      p == NE // 2 - 1 and j == 1 and k == 1,
                                      (rdy, ex[2 * p], ex[2 * p + 1], free[bank]), j == 1)
                    give(("moe_out", p, k), tok)
                ex["used", 2 * p] = ex["used", 2 * p + 1] = tok

            for p in range(NE // 2 + 1):
                if p < NE // 2:
                    for r in range(4):
                        hi, lo, rdy = take(("moe_in", p, r))
                        hi, lo = [x.rearrange("p a (b n) -> p (a b) n", n=256).rearrange("p (g e k) n -> p g e k n", g=2, e=2)
                                  for x in (hi, lo)]
                        for j in range(2):
                            for c in range(4):
                                b = 4 + 2 * j + c // 2
                                for k in range(2):
                                    x = slice((2 * r + k) * 256, (2 * r + k) * 256 + 256)
                                    cs_ = slice(128 * (c % 2), 128 * (c % 2) + 128)
                                    tok = mm3(PB[b][:, 256 * (c % 2):256 * (c % 2) + 256], hi[:, c // 2, j, k, cs_],
                                              lo[:, c // 2, j, k, cs_], TH[0][:, x], TL[0][:, x], r == 0 and k == 0 and c % 2 == 0,
                                              r == 3 and k == 1, (rdy, hf, free[b]), k == 1)
                            ex["pe", j] = tok
                        give(("moe_in", p, r), tok)
                    for j in range(2):
                        e_ = 2 * p + j
                        b = 4 + 2 * j
                        s = GS[:, 512 * j:512 * j + 512]
                        a = do("act", lambda e: e.activation(s, PB[b][:, :], ACT.Tanh, scale=0.5), ex["pe", j], hf, ex.get(e_ - 2))
                        d = do("dve", lambda e: e.scalar_tensor_tensor(s, s, 1.0, PB[b][:, :], ALU.add, ALU.mult), a)
                        free[b] = [d]
                        d = do("dve", lambda e: e.tensor_tensor(s, s, PB[b + 1][:, :], ALU.mult), d)
                        free[b + 1] = [d]
                        cb = CB[e_ // 8][:, 256 * (e_ % 8):256 * (e_ % 8) + 256].unsqueeze(1).to_broadcast([128, 2, 256])
                        q = do("pool", lambda e: e.tensor_tensor(v3(s, 2, 256), v3(s, 2, 256), cb, ALU.mult), d, cwb[e_])
                        ex[e_] = split_t(s, 1, 2 * (e_ % 4), 2, q, [ex.get(("used", e_ - 4)), xo_pe])
                if p > 0:
                    moe_down(p - 1)
            finish(ex["used", NE - 1], FG, fing, ex[NE - 1])

        def sparse(late):
            XG = [[TH[0], TL[0]], [sbe("XGH", 2048, R, late), sbe("XGL", 2048, R, late)]]
            YY = [[TH[1][:, 1024:2048], TL[1][:, 1024:2048]], [x[:, :] for x in (sbe("YH", 1024, R, late), sbe("YL", 1024, R, late))]]
            HT = [[x[:, 384 * b:384 * b + 384] for x in (TH[1], TL[1])] for b in range(2)]
            SEL = [sbe(f"SEL{i}", 512, R, late) for i in range(2)]
            SET = [sbe(f"SET{i}", 256, R, late) for i in range(4)]
            FG = sbe("FG", 1024, F, late)
            CS = sbe("CS", 2, F, late)
            fing = Q.dma("act", "fing", lambda e: e.dma_start(FG[:, :], A["final_norm_g_2"].partition_broadcast(128)), hf)
            sel, st_, xg, gu, hd, yy, used = {}, {}, {}, {}, {}, {}, {}
            zs = [do("pool", lambda e: e.memset(v3(x, 2, 192)[:, :, 64:128].bitcast(F), 0.0), hf, xo_pe) for b in range(2) for x in HT[b]]

            def select(q):
                s = v3(SEL[q % 2], 2, 256)
                for t in range(2):
                    c = 32 * t + 4 * q
                    sel[q] = do("dve", lambda e: e.tensor_tensor(
                        s[:, t].rearrange("p (e n) -> p e n", e=4), cst("slots", 64).unsqueeze(1).to_broadcast([128, 4, 64]),
                        rank[:, c:c + 4].unsqueeze(2).to_broadcast([128, 4, 64]), ALU.is_equal),
                        rank_tok, hf, used.get(("sel", q - 2)))

            def choose(p):
                q = p // 2
                sf = v3(SEL[q % 2], 2, 256).bitcast(F)[:, :, 128 * (p % 2):128 * (p % 2) + 128]
                for t in range(2):
                    do("pe", lambda e: e.transpose(PB[5][:, 128 * t:128 * t + 128], sf[:, t], ident), sel[q], free[5], silent=True)
                for t in range(2):
                    m = do("pe", lambda e: e.matmul(PB[5][:, 256:258], sf[:, t], cw[:, 32 * t + 2 * p:32 * t + 2 * p + 2],
                                                    start=(t == 0), stop=(t == 1), skip_group_check=True), cw_tok)
                used["sel", q] = m
                a = do("act", lambda e: e.activation(SET[p % 4][:, :], PB[5][:, 0:256], ACT.Copy), m, used.get(("set", p - 4)))
                do("act", lambda e: e.activation(CS[0:64, p % 2:p % 2 + 1], PB[5][0:64, 256:257], ACT.Copy), gu.get(("w", p - 2)),
                   silent=True)
                b = do("act", lambda e: e.activation(CS[64:128, p % 2:p % 2 + 1], PB[5][64:128, 257:258], ACT.Copy))
                free[5] = [b]
                st_[p] = [a, b]

            def gather(q, rounds):
                s = v3(SEL[q % 2], 2, 256)
                for r in rounds:
                    b = 6 + r % 2
                    for k in range(2):
                        for t in range(2):
                            for i in range(2):
                                l = XN[i][:, 1024 * t + 128 * (2 * r + k):1024 * t + 128 * (2 * r + k) + 128]
                                m = do("pe", lambda e: e.matmul(PB[b][:, 256 * k:256 * k + 256], l, s[:, t],
                                                                start=(k == 0 and t == 0 and i == 0), stop=(t == 1 and i == 1),
                                                                skip_group_check=True),
                                       sel[q], xa_, xn, free[b], silent=not (k == 1 and t == 1 and i == 1))
                    hi, lo = [x[:, 512 * r:512 * r + 512] for x in XG[q % 2]]
                    a = do("act", lambda e: e.activation(hi, PB[b][:, :], ACT.Copy), m, used.get(("xg", q - 2)), rt_pe)
                    d = do("dve", lambda e: e.tensor_tensor(lo, PB[b][:, :], hi.bitcast(F), ALU.subtract), a)
                    free[b] = [d]
                    xg[q, 2 * r] = xg[q, 2 * r + 1] = [a, d]

            def rise(p):
                q = p // 2
                for r in range(4):
                    hi, lo, rdy = take(("moe_in", p, r))
                    hi, lo = [x.rearrange("p a (b n) -> p (a b) n", n=256).rearrange("p (g e k) n -> p g e k n", g=2, e=2)
                              for x in (hi, lo)]
                    for k in range(2):
                        kk = 2 * r + k
                        c = 256 * kk + 128 * (p % 2)
                        for l, w in ((0, hi), (0, lo), (1, hi)):
                            for j in range(2):
                                tok = do("pe", lambda e: e.matmul(
                                    PB[4 + j][:, :], XG[q % 2][l][:, c:c + 128], w[:, :, j, k],
                                    start=(kk == 0 and l == 0 and w is hi), stop=(kk == 7 and l == 1), skip_group_check=True),
                                    rdy, xg[q, kk], free[4 + j], silent=not (k == 1 and l == 1 and j == 1))
                    give(("moe_in", p, r), tok)
                used["xg", q] = tok
                gu["w", p] = []
                for j in range(2):
                    ps = slice(64 * j, 64 * j + 64)
                    s = S0[ps, 256 * (p % 2):256 * (p % 2) + 256]
                    a = do("act", lambda e: e.activation(s, PB[4 + j][ps, 0:256], ACT.Tanh, scale=0.5), tok, d, hd.get(("in", p - 2)))
                    w = do("dve", lambda e: e.scalar_tensor_tensor(s, s, 1.0, PB[4 + j][ps, 0:256], ALU.add, ALU.mult), a)
                    w = do("dve", lambda e: e.scalar_tensor_tensor(s, s, CS[ps, p % 2:p % 2 + 1], PB[4 + j][ps, 256:512], ALU.mult,
                                                                   ALU.mult), w, st_[p])
                    gu["w", p].append(w)
                    free[4 + j] = [w]

            def over(p):
                s = S0[:, 256 * (p % 2):256 * (p % 2) + 256]
                for f in range(2):
                    m = do("pe", lambda e: e.transpose(PB[4][:, 128 * f:128 * f + 128], s[:, 128 * f:128 * f + 128], ident),
                           gu["w", p], free[4])
                hd["in", p] = m
                hi, lo = [x.rearrange("p (k h c) -> p k h c", k=2, h=3)[:, :, 0:3:2, :] for x in HT[p % 2]]
                src = PB[4][:, 0:256].rearrange("p (k h c) -> p k h c", k=2, h=2)
                a = do("act", lambda e: e.activation(hi, src, ACT.Copy), m, zs, xo_pe, used.get(("ht", p - 2)))
                q = do("dve", lambda e: e.tensor_tensor(lo, src, hi.bitcast(F), ALU.subtract), a)
                free[4] = [q]
                hd[p] = [a, q]

            def down(p):
                for k in range(2):
                    hi, lo, rdy = take(("moe_out", p, k))
                    for h in range(2):
                        for l, w in ((0, hi), (0, lo), (1, hi)):
                            for j in range(2):
                                c = 192 * k + 64 * j
                                tok = do("pe", lambda e: e.matmul(
                                    PB[6 + h][:, :], HT[p % 2][l][:, c:c + 128], w[:, j, 512 * h:512 * h + 512],
                                    start=(k == 0 and l == 0 and w is hi and j == 0), stop=(k == 1 and l == 1 and j == 1),
                                    skip_group_check=True),
                                    rdy, hd[p], free[6 + h], silent=not (l == 1 and j == 1))
                        yy["pe", h] = tok
                    give(("moe_out", p, k), tok)
                used["ht", p] = tok
                yy[p] = []
                for h in range(2):
                    hi, lo = [x[:, 512 * h:512 * h + 512] for x in YY[p % 2]]
                    a = do("act", lambda e: e.activation(hi, PB[6 + h][:, :], ACT.Copy), yy["pe", h], used.get(("y", p - 2)), xo_pe)
                    q = do("dve", lambda e: e.tensor_tensor(lo, PB[6 + h][:, :], hi.bitcast(F), ALU.subtract), a)
                    free[6 + h] = [q]
                    yy[p] += [a, q]

            def spread(p):
                for t in range(2):
                    for h in range(2):
                        for i in range(2):
                            m = do("pe", lambda e: e.matmul(PB[2 * t + h][:, :], SET[p % 4][:, 128 * t:128 * t + 128],
                                                            YY[p % 2][i][:, 512 * h:512 * h + 512], start=(p == 0 and i == 0),
                                                            stop=(p == NE // 2 - 1 and i == 1), skip_group_check=True),
                                   yy[p], st_[p], free[2 * t + h], silent=not (t == 1 and h == 1 and i == 1))
                used["y", p] = used["set", p] = m
                return m

            NP = NE // 2
            select(0)
            choose(0)
            gather(0, range(4))
            for p in range(NP + 2):
                if p < NP:
                    if p % 2 == 0 and p + 2 < NP:
                        select(p // 2 + 1)
                    rise(p)
                if 1 <= p <= NP:
                    down(p - 1)
                if 2 <= p:
                    m = spread(p - 2)
                if p < NP:
                    over(p)
                    if p + 1 < NP:
                        choose(p + 1)
                if p // 2 + 1 < NP // 2:
                    gather(p // 2 + 1, range(2 * (p % 2), 2 * (p % 2) + 2))
            finish(m, FG, fing, [yy[NP - 1], d])

        for name in Q.engines:
            Q.wait(name, (flag_tok,))
        largest = nc.values_load(flag[0:1, 0:1], min_val=0, max_val=2 * S)

        def state():
            return ({k: v for k, v in Q.count.items()}, {k: dict(v) for k, v in Q.seen.items()}, dict(st), turn[0],
                    dict(raw_ready), dict(split_done), dict(used_done), dict(free))

        def restore(s):
            Q.count.update(s[0])
            for k in Q.seen:
                Q.seen[k] = dict(s[1][k])
            st.update(s[2])
            turn[0] = s[3]
            for now, then in zip((raw_ready, split_done, used_done, free), s[4:]):
                now.clear()
                now.update(then)

        before = state()
        with nc.If(largest < 65):
            with ExitStack() as late:
                sparse(late)
        restore(before)
        with nc.Else():
            with ExitStack() as late:
                dense(late)


def kernel(**inputs):
    import concourse.bacc as _bacc
    from concourse.bass_utils import run_bass_kernel_spmd as _run

    nc = _bacc.Bacc("TRN2", target_bir_lowering=False, num_devices=1)
    arrays, aps = {}, {}
    for name, a in {**inputs, "const": constants()}.items():
        a = np.ascontiguousarray(a)
        arrays[f"in_{name}"] = a
        aps[name] = nc.dram_tensor(f"in_{name}", a.shape, mybir.dt.from_np(a.dtype), kind="ExternalInput").ap()
    out = nc.dram_tensor("out_0", (1, S, D), F, kind="ExternalOutput").ap()
    build(nc, aps, out)
    r = _run(nc, [arrays], core_ids=[0])
    return r.results[0]["out_0"]
```
